# Optimizing a Trainium2 kernel written in Bass

```python
import math
import jax, jax.numpy as jnp
from jax import lax
import numpy as np

D_MODEL = 1024
BATCH = 1
SEQ = 256
DEPTH = 1

N_Q_HEADS = 8
N_KV_HEADS = 2
HEAD_DIM = 64
WINDOW = 128
ATTN_BLOCK = WINDOW
ROPE_THETA = 10000.0
MLSTM_HEADS = 4
MLSTM_HEAD_DIM = 128
MLSTM_CHUNK = 64
CONV_WIDTH = 4
D_FF = -(-8 * D_MODEL // (3 * 256)) * 256
NORM_EPS = 1e-6

ATTN_Q_WIDTH = N_Q_HEADS * HEAD_DIM
ATTN_KV_WIDTH = N_KV_HEADS * HEAD_DIM
MLSTM_WIDTH = MLSTM_HEADS * MLSTM_HEAD_DIM
IN_SPLIT_SIZES = (ATTN_Q_WIDTH, ATTN_KV_WIDTH, ATTN_KV_WIDTH,
                  MLSTM_WIDTH, MLSTM_WIDTH, MLSTM_WIDTH, MLSTM_WIDTH,
                  MLSTM_HEADS, MLSTM_HEADS, D_MODEL, D_MODEL)
IN_WIDTH = sum(IN_SPLIT_SIZES)


def rms_norm(x, g):
    xf = x.astype(jnp.float32)
    y = xf * lax.rsqrt(jnp.mean(xf * xf, axis=-1, keepdims=True) + NORM_EPS)
    return (y * g.astype(jnp.float32)).astype(x.dtype)

def modulate(h, shift, scale):
    return h * (1 + scale[:, None, :]) + shift[:, None, :]

def rope(t, positions):
    half = HEAD_DIM // 2
    inv_freq = ROPE_THETA ** (-2.0 * jnp.arange(half, dtype=jnp.float32) / HEAD_DIM)
    ang = positions.astype(jnp.float32)[..., None] * inv_freq
    cos = jnp.cos(ang)[:, :, None, :]
    sin = jnp.sin(ang)[:, :, None, :]
    tf = t.astype(jnp.float32)
    t1, t2 = tf[..., :half], tf[..., half:]
    return jnp.concatenate([t1 * cos - t2 * sin, t2 * cos + t1 * sin], axis=-1).astype(t.dtype)

def causal_depthwise_conv(u, w, b):
    S = u.shape[1]
    up = jnp.pad(u, ((0, 0), (CONV_WIDTH - 1, 0), (0, 0)))
    out = b
    for j in range(CONV_WIDTH):
        out = out + up[:, j:j + S] * w[j]
    return out

def sliding_window_attention(q, k, v, sinks):
    B, S = q.shape[0], q.shape[1]
    nb = S // ATTN_BLOCK
    g = N_Q_HEADS // N_KV_HEADS
    qb = q.astype(jnp.float32).reshape(B, nb, ATTN_BLOCK, N_KV_HEADS, g, HEAD_DIM) * (HEAD_DIM ** -0.5)

    def band(t):
        t = t.astype(jnp.float32).reshape(B, nb, ATTN_BLOCK, N_KV_HEADS, HEAD_DIM)
        prev = jnp.pad(t, ((0, 0), (1, 0), (0, 0), (0, 0), (0, 0)))[:, :-1]
        return jnp.concatenate([prev, t], axis=2)

    kb, vb = band(k), band(v)
    s = jnp.einsum('bnqhgd,bnkhd->bnhgqk', qb, kb)
    qi = jnp.arange(ATTN_BLOCK)[:, None]
    kj = jnp.arange(2 * ATTN_BLOCK)[None, :]
    rel = kj - ATTN_BLOCK
    in_band = (rel <= qi) & (qi - rel < WINDOW)
    blk = jnp.arange(nb)[:, None, None]
    mask = in_band[None] & ((blk > 0) | (kj[None] >= ATTN_BLOCK))
    s = jnp.where(mask[None, :, None, None], s, -jnp.inf)
    sink = sinks.astype(jnp.float32).reshape(N_KV_HEADS, g)[None, None, :, :, None, None]
    m = jnp.maximum(jnp.max(s, axis=-1, keepdims=True), sink)
    p = jnp.exp(s - m)
    p = p / (jnp.sum(p, axis=-1, keepdims=True) + jnp.exp(sink - m))
    o = jnp.einsum('bnhgqk,bnkhd->bnqhgd', p, vb)
    return o.reshape(B, S, N_Q_HEADS * HEAD_DIM)

def mlstm_chunkwise(q, k, v, i_pre, f_pre):
    B, S, H, D = q.shape
    L = MLSTM_CHUNK
    nc = S // L

    def chunks(t):
        return t.astype(jnp.float32).reshape(B, nc, L, H, D).transpose(0, 3, 1, 2, 4)

    qc = chunks(q)
    kc = chunks(k) * (D ** -0.5)
    vc = chunks(v)
    ig = i_pre.astype(jnp.float32).reshape(B, nc, L, H).transpose(0, 3, 1, 2)
    logf = jax.nn.log_sigmoid(f_pre.astype(jnp.float32)).reshape(B, nc, L, H).transpose(0, 3, 1, 2)
    b = jnp.cumsum(logf, axis=-1)
    b_last = b[..., -1]
    a = b_last[..., None] - b + ig

    def step(carry, inp):
        C, n, m = carry
        k_c, v_c, a_c, bl_c = inp
        m_new = jnp.maximum(bl_c + m, jnp.max(a_c, axis=-1))
        decay = jnp.exp(bl_c + m - m_new)
        kw = k_c * jnp.exp(a_c - m_new[..., None])[..., None]
        C_new = decay[..., None, None] * C + jnp.einsum('bhld,bhle->bhde', kw, v_c)
        n_new = decay[..., None] * n + jnp.sum(kw, axis=-2)
        return (C_new, n_new, m_new), (C, n, m)

    init = (jnp.zeros((B, H, D, D), jnp.float32), jnp.zeros((B, H, D), jnp.float32),
            jnp.zeros((B, H), jnp.float32))
    xs = (kc.transpose(2, 0, 1, 3, 4), vc.transpose(2, 0, 1, 3, 4),
          a.transpose(2, 0, 1, 3), b_last.transpose(2, 0, 1))
    _, (C_prev, n_prev, m_prev) = lax.scan(step, init, xs)
    C_prev = C_prev.transpose(1, 2, 0, 3, 4)
    n_prev = n_prev.transpose(1, 2, 0, 3)
    m_prev = m_prev.transpose(1, 2, 0)

    causal = jnp.tril(jnp.ones((L, L), dtype=bool))
    d_mat = jnp.where(causal, b[..., :, None] - b[..., None, :] + ig[..., None, :], -jnp.inf)
    inter = b + m_prev[..., None]
    m_t = jnp.maximum(inter, jnp.max(d_mat, axis=-1))
    w_intra = jnp.exp(d_mat - m_t[..., None])
    w_inter = jnp.exp(inter - m_t)
    scores = jnp.einsum('bhctd,bhcsd->bhcts', qc, kc) * w_intra
    num = jnp.einsum('bhcts,bhcsd->bhctd', scores, vc) + \
        w_inter[..., None] * jnp.einsum('bhctd,bhcde->bhcte', qc, C_prev)
    den = jnp.sum(scores, axis=-1) + w_inter * jnp.einsum('bhctd,bhcd->bhct', qc, n_prev)
    h = num / jnp.maximum(jnp.abs(den), jnp.exp(-m_t))[..., None]
    return h.transpose(0, 2, 3, 1, 4).reshape(B, S, H, D)

def head_layer_norm(h, w):
    mu = jnp.mean(h, axis=-1, keepdims=True)
    var = jnp.mean(jnp.square(h - mu), axis=-1, keepdims=True)
    y = (h - mu) * lax.rsqrt(var + NORM_EPS)
    return y.reshape(h.shape[0], h.shape[1], -1) * w.astype(jnp.float32)

def first_inputs(seed: int = 0) -> dict:
    key = jax.random.key(seed)
    ks = jax.random.split(key, 24)
    f32 = jnp.float32

    def dense(k, shape, fan_in, scale=1.0):
        return jax.random.normal(k, shape, f32) * (scale * fan_in ** -0.5)

    def gain(k, width):
        return 1.0 + 0.05 * jax.random.normal(k, (DEPTH, width), f32)

    x = jax.random.normal(ks[0], (BATCH, SEQ, D_MODEL), f32)
    c = jax.random.normal(ks[1], (BATCH, D_MODEL), f32)
    offsets = jax.random.randint(ks[2], (BATCH, 1), 0, 4096, dtype=jnp.int32)
    positions = (offsets + jnp.arange(SEQ, dtype=jnp.int32)[None, :]).astype(jnp.int32)
    w_ada = dense(ks[3], (DEPTH, D_MODEL, 6 * D_MODEL), D_MODEL, 0.5)
    b_ada = 0.02 * jax.random.normal(ks[4], (DEPTH, 6 * D_MODEL), f32)
    g_pre_mix = gain(ks[5], D_MODEL)
    g_post_mix = gain(ks[6], D_MODEL)
    w_in = dense(ks[7], (DEPTH, D_MODEL, IN_WIDTH), D_MODEL)
    b_i = 0.1 * jax.random.normal(ks[8], (DEPTH, MLSTM_HEADS), f32)
    b_f = jnp.linspace(3.0, 6.0, MLSTM_HEADS, dtype=f32)[None, :] + \
        0.1 * jax.random.normal(ks[9], (DEPTH, MLSTM_HEADS), f32)
    b_if = jnp.concatenate([b_i, b_f], axis=-1)
    conv_w = dense(ks[10], (DEPTH, CONV_WIDTH, 2 * MLSTM_WIDTH), CONV_WIDTH)
    conv_b = 0.02 * jax.random.normal(ks[11], (DEPTH, 2 * MLSTM_WIDTH), f32)
    attn_sinks = 0.5 * jax.random.normal(ks[12], (DEPTH, N_Q_HEADS), f32)
    mlstm_norm_w = gain(ks[13], MLSTM_WIDTH)
    w_branch_attn = dense(ks[14], (DEPTH, ATTN_Q_WIDTH, D_MODEL), ATTN_Q_WIDTH)
    w_branch_mlstm = dense(ks[15], (DEPTH, MLSTM_WIDTH, D_MODEL), MLSTM_WIDTH)
    w_out = dense(ks[16], (DEPTH, D_MODEL, D_MODEL), D_MODEL)
    g_pre_ffn = gain(ks[17], D_MODEL)
    g_post_ffn = gain(ks[18], D_MODEL)
    w_ffn_gate = dense(ks[19], (DEPTH, D_MODEL, D_FF), D_MODEL)
    w_ffn_up = dense(ks[20], (DEPTH, D_MODEL, D_FF), D_MODEL)
    w_ffn_down = dense(ks[21], (DEPTH, D_FF, D_MODEL), D_FF)
    return {'x': x, 'c': c, 'positions': positions, 'w_ada': w_ada, 'b_ada': b_ada,
            'g_pre_mix': g_pre_mix, 'g_post_mix': g_post_mix, 'w_in': w_in, 'b_if': b_if,
            'conv_w': conv_w, 'conv_b': conv_b, 'attn_sinks': attn_sinks,
            'mlstm_norm_w': mlstm_norm_w, 'w_branch_attn': w_branch_attn,
            'w_branch_mlstm': w_branch_mlstm, 'w_out': w_out, 'g_pre_ffn': g_pre_ffn,
            'g_post_ffn': g_post_ffn, 'w_ffn_gate': w_ffn_gate, 'w_ffn_up': w_ffn_up,
            'w_ffn_down': w_ffn_down}

def first_block(x, c, positions, w_ada, b_ada, g_pre_mix, g_post_mix, w_in, b_if, conv_w, conv_b,
              attn_sinks, mlstm_norm_w, w_branch_attn, w_branch_mlstm, w_out, g_pre_ffn,
              g_post_ffn, w_ffn_gate, w_ffn_up, w_ffn_down):
    B, S, _ = x.shape
    split_points = np.cumsum(IN_SPLIT_SIZES)[:-1].tolist()
    for l in range(DEPTH):
        mod = c @ w_ada[l] + b_ada[l]
        shift_m, scale_m, gate_m, shift_f, scale_f, gate_f = jnp.split(mod, 6, axis=-1)

        h = modulate(rms_norm(x, g_pre_mix[l]), shift_m, scale_m)
        proj = h @ w_in[l]
        q_a, k_a, v_a, q_m, k_m, v_m, o_m, i_m, f_m, g_a, g_m = jnp.split(proj, split_points, axis=-1)

        q_a = rope(q_a.reshape(B, S, N_Q_HEADS, HEAD_DIM), positions)
        k_a = rope(k_a.reshape(B, S, N_KV_HEADS, HEAD_DIM), positions)
        v_a = v_a.reshape(B, S, N_KV_HEADS, HEAD_DIM)
        y_a = sliding_window_attention(q_a, k_a, v_a, attn_sinks[l]).astype(x.dtype)

        qk_m = jax.nn.silu(causal_depthwise_conv(jnp.concatenate([q_m, k_m], axis=-1), conv_w[l], conv_b[l]))
        q_m, k_m = jnp.split(qk_m, 2, axis=-1)
        i_pre = i_m + b_if[l][:MLSTM_HEADS]
        f_pre = f_m + b_if[l][MLSTM_HEADS:]
        h_m = mlstm_chunkwise(q_m.reshape(B, S, MLSTM_HEADS, MLSTM_HEAD_DIM),
                              k_m.reshape(B, S, MLSTM_HEADS, MLSTM_HEAD_DIM),
                              v_m.reshape(B, S, MLSTM_HEADS, MLSTM_HEAD_DIM), i_pre, f_pre)
        y_m = (jax.nn.sigmoid(o_m.astype(jnp.float32)) * head_layer_norm(h_m, mlstm_norm_w[l])).astype(x.dtype)

        merged = jax.nn.sigmoid(g_a) * (y_a @ w_branch_attn[l]) + jax.nn.sigmoid(g_m) * (y_m @ w_branch_mlstm[l])
        mix = merged @ w_out[l]
        x = x + gate_m[:, None, :] * rms_norm(mix, g_post_mix[l])

        h2 = modulate(rms_norm(x, g_pre_ffn[l]), shift_f, scale_f)
        ff = (jax.nn.silu(h2 @ w_ffn_gate[l]) * (h2 @ w_ffn_up[l])) @ w_ffn_down[l]
        x = x + gate_f[:, None, :] * rms_norm(ff, g_post_ffn[l])
    return x


MIX_A = D_MODEL // 2
MIX_B = D_MODEL - MIX_A
CHUNK = 128
A_GROUPS = 4
A_GROUP_DIM = MIX_A // A_GROUPS
B_HEAD_DIM = 64
B_HEADS = MIX_B // B_HEAD_DIM
LORA_W = 64
LORA_A = 64
LORA_G = 160
RWKV_COLS = 3 * MIX_B + LORA_W + LORA_A + LORA_G
IN_COLS = 2 * MIX_A + RWKV_COLS
FFN_HIDDEN = ((8 * D_MODEL + 3 * 256 - 1) // (3 * 256)) * 256
ALPHA = (2 * DEPTH) ** 0.25
BETA = (8 * DEPTH) ** -0.25
LN_EPS = 1e-5
GN_EPS = 64e-5


def layer_norm(x, g, b, eps=LN_EPS):
    xf = x.astype(jnp.float32)
    mu = jnp.mean(xf, axis=-1, keepdims=True)
    var = jnp.mean(jnp.square(xf - mu), axis=-1, keepdims=True)
    y = (xf - mu) * lax.rsqrt(var + eps)
    return (y * g.astype(jnp.float32) + b.astype(jnp.float32)).astype(x.dtype)

def token_shift(p):
    return jnp.pad(p, ((0, 0), (1, 0), (0, 0)))[:, :-1]

def gmlp_spatial_gating(pu, pv, ln_g, ln_b, w_s, b_s):
    B, S, _ = pu.shape
    nc = S // CHUNK
    u = jax.nn.gelu(pu)
    v = layer_norm(jax.nn.gelu(pv), ln_g, ln_b)
    vc = v.reshape(B, nc, CHUNK, A_GROUPS, A_GROUP_DIM)
    mask = jnp.tril(jnp.ones((CHUNK, CHUNK), dtype=w_s.dtype))
    s = jnp.einsum('gts,bnsgd->bntgd', w_s * mask, vc) + b_s.T[None, None, :, :, None]
    return u * s.reshape(B, S, MIX_A)

def _rwkv7_step(S, inp):
    r, w, k, v, a, b = inp
    sa = jnp.einsum('bhij,bhj->bhi', S, a)
    S = S * w[:, :, None, :] + sa[..., None] * b[:, :, None, :] + v[..., None] * k[:, :, None, :]
    y = jnp.einsum('bhij,bhj->bhi', S, r)
    return S, y

def rwkv7_time_mix(p, mu, w0, w_up, a0, a_up, g_up, k_k, k_a, r_k, lnx_g, lnx_b):
    B, S, _ = p.shape
    p = p + (token_shift(p) - p) * mu
    r, k, v = p[..., :MIX_B], p[..., MIX_B:2 * MIX_B], p[..., 2 * MIX_B:3 * MIX_B]
    o = 3 * MIX_B
    wd = p[..., o:o + LORA_W]
    ad = p[..., o + LORA_W:o + LORA_W + LORA_A]
    gd = p[..., o + LORA_W + LORA_A:]
    f32 = jnp.float32
    wlog = -jax.nn.softplus(-(w0 + jnp.tanh(wd) @ w_up).astype(f32)) - 0.5
    decay = jnp.exp(-jnp.exp(wlog))
    a = jax.nn.sigmoid((a0 + ad @ a_up).astype(f32))
    g = jax.nn.sigmoid(gd) @ g_up
    rf, kf, vf = r.astype(f32), k.astype(f32), v.astype(f32)
    heads = lambda t: t.reshape(B, S, B_HEADS, B_HEAD_DIM)
    kk = heads(kf * k_k.astype(f32))
    kk = kk / jnp.maximum(jnp.sqrt(jnp.sum(kk * kk, axis=-1, keepdims=True)), 1e-12)
    kf = kf * (1.0 + (a - 1.0) * k_a.astype(f32))
    rh, kh, vh, wh, ah = heads(rf), heads(kf), heads(vf), heads(decay), heads(a)
    xs = tuple(jnp.swapaxes(t, 0, 1) for t in (rh, wh, kh, vh, -kk, kk * ah))
    S0 = jnp.zeros((B, B_HEADS, B_HEAD_DIM, B_HEAD_DIM), f32)
    _, y = lax.scan(_rwkv7_step, S0, xs)
    y = jnp.swapaxes(y, 0, 1)
    mu_y = jnp.mean(y, axis=-1, keepdims=True)
    var_y = jnp.mean(jnp.square(y - mu_y), axis=-1, keepdims=True)
    y = ((y - mu_y) * lax.rsqrt(var_y + GN_EPS)).reshape(B, S, MIX_B)
    y = y * lnx_g.astype(f32) + lnx_b.astype(f32)
    bonus = jnp.sum(rh * kh * r_k.astype(f32), axis=-1, keepdims=True) * vh
    y = y + bonus.reshape(B, S, MIX_B)
    return (y * g.astype(f32)).astype(p.dtype)

def second_inputs(seed: int = 0) -> dict:
    key = jax.random.key(seed)
    ks = jax.random.split(key, 32)
    L, D = DEPTH, D_MODEL
    f32 = jnp.float32
    nrm = lambda k, shape, s: jax.random.normal(k, shape, f32) * s
    return {
        "x": nrm(ks[0], (BATCH, SEQ, D), 1.0),
        "c": nrm(ks[1], (BATCH, D), 1.0),
        "emb_ln_g": 1.0 + nrm(ks[2], (D,), 0.05),
        "emb_ln_b": nrm(ks[3], (D,), 0.02),
        "w_ada": nrm(ks[4], (L, D, 6 * D), 0.5 * D ** -0.5),
        "b_ada": nrm(ks[5], (L, 6 * D), 0.02),
        "w_in": nrm(ks[6], (L, D, IN_COLS), D ** -0.5),
        "mu_shift": jax.random.uniform(ks[7], (L, RWKV_COLS), f32),
        "sg_ln_g": 1.0 + nrm(ks[8], (L, MIX_A), 0.05),
        "sg_ln_b": nrm(ks[9], (L, MIX_A), 0.02),
        "w_s": nrm(ks[10], (L, A_GROUPS, CHUNK, CHUNK), CHUNK ** -0.5),
        "b_s": 1.0 + nrm(ks[11], (L, A_GROUPS, CHUNK), 0.1),
        "w0": jax.random.uniform(ks[12], (L, MIX_B), f32, -6.0, 1.0),
        "w_up": nrm(ks[13], (L, LORA_W, MIX_B), LORA_W ** -0.5),
        "a0": nrm(ks[14], (L, MIX_B), 0.1),
        "a_up": nrm(ks[15], (L, LORA_A, MIX_B), LORA_A ** -0.5),
        "g_up": nrm(ks[16], (L, LORA_G, MIX_B), LORA_G ** -0.5),
        "k_k": 0.85 + nrm(ks[17], (L, MIX_B), 0.05),
        "k_a": 1.0 + nrm(ks[18], (L, MIX_B), 0.05),
        "r_k": nrm(ks[19], (L, B_HEADS, B_HEAD_DIM), 0.1),
        "lnx_g": 1.0 + nrm(ks[20], (L, MIX_B), 0.05),
        "lnx_b": nrm(ks[21], (L, MIX_B), 0.02),
        "w_out": nrm(ks[22], (L, D, D), BETA * D ** -0.5),
        "ln1_g": 1.0 + nrm(ks[23], (L, D), 0.05),
        "ln1_b": nrm(ks[24], (L, D), 0.02),
        "w_ffn_in": nrm(ks[25], (L, D, 2 * FFN_HIDDEN), D ** -0.5),
        "w_ffn_out": nrm(ks[26], (L, FFN_HIDDEN, D), BETA * FFN_HIDDEN ** -0.5),
        "ln2_g": 1.0 + nrm(ks[27], (L, D), 0.05),
        "ln2_b": nrm(ks[28], (L, D), 0.02),
    }

def second_block(x, c, emb_ln_g, emb_ln_b, w_ada, b_ada, w_in, mu_shift, sg_ln_g, sg_ln_b, w_s, b_s,
              w0, w_up, a0, a_up, g_up, k_k, k_a, r_k, lnx_g, lnx_b, w_out, ln1_g, ln1_b,
              w_ffn_in, w_ffn_out, ln2_g, ln2_b):
    x = layer_norm(x, emb_ln_g, emb_ln_b)
    cs = jax.nn.silu(c)
    for l in range(DEPTH):
        mod = cs @ w_ada[l] + b_ada[l]
        sh1, sc1, gt1, sh2, sc2, gt2 = [m[:, None, :] for m in jnp.split(mod, 6, axis=-1)]
        h = x * (1.0 + sc1) + sh1
        p = h @ w_in[l]
        y_a = gmlp_spatial_gating(p[..., :MIX_A], p[..., MIX_A:2 * MIX_A],
                                  sg_ln_g[l], sg_ln_b[l], w_s[l], b_s[l])
        y_b = rwkv7_time_mix(p[..., 2 * MIX_A:], mu_shift[l], w0[l], w_up[l], a0[l], a_up[l],
                             g_up[l], k_k[l], k_a[l], r_k[l], lnx_g[l], lnx_b[l])
        mix = jnp.concatenate([y_a, y_b], axis=-1) @ w_out[l]
        x = layer_norm(ALPHA * x + gt1 * mix, ln1_g[l], ln1_b[l])
        h = x * (1.0 + sc2) + sh2
        gu = h @ w_ffn_in[l]
        f = (jax.nn.silu(gu[..., :FFN_HIDDEN]) * gu[..., FFN_HIDDEN:]) @ w_ffn_out[l]
        x = layer_norm(ALPHA * x + gt2 * f, ln2_g[l], ln2_b[l])
    return x


def setup_inputs(seed=0):
    out = dict(first_inputs(seed))
    for name, value in second_inputs(seed + 1).items():
        if name != "x":
            out[name + "_2"] = value
    return out


def reference(
    x, c, positions, w_ada, b_ada, g_pre_mix, g_post_mix, w_in, b_if, conv_w, conv_b,
    attn_sinks, mlstm_norm_w, w_branch_attn, w_branch_mlstm, w_out, g_pre_ffn, g_post_ffn,
    w_ffn_gate, w_ffn_up, w_ffn_down, c_2, emb_ln_g_2, emb_ln_b_2, w_ada_2, b_ada_2, w_in_2,
    mu_shift_2, sg_ln_g_2, sg_ln_b_2, w_s_2, b_s_2, w0_2, w_up_2, a0_2, a_up_2, g_up_2, k_k_2,
    k_a_2, r_k_2, lnx_g_2, lnx_b_2, w_out_2, ln1_g_2, ln1_b_2, w_ffn_in_2, w_ffn_out_2, ln2_g_2,
    ln2_b_2,
):
    x = first_block(
        x, c, positions, w_ada, b_ada, g_pre_mix, g_post_mix, w_in, b_if, conv_w, conv_b,
        attn_sinks, mlstm_norm_w, w_branch_attn, w_branch_mlstm, w_out, g_pre_ffn, g_post_ffn,
        w_ffn_gate, w_ffn_up, w_ffn_down,
    )
    return second_block(
        x, c_2, emb_ln_g_2, emb_ln_b_2, w_ada_2, b_ada_2, w_in_2, mu_shift_2, sg_ln_g_2,
        sg_ln_b_2, w_s_2, b_s_2, w0_2, w_up_2, a0_2, a_up_2, g_up_2, k_k_2, k_a_2, r_k_2,
        lnx_g_2, lnx_b_2, w_out_2, ln1_g_2, ln1_b_2, w_ffn_in_2, w_ffn_out_2, ln2_g_2, ln2_b_2,
    )


_drawn_inputs = setup_inputs


def setup_inputs(seed=0):
    import zlib

    import numpy as np

    out = dict(_drawn_inputs(seed))
    spreads = {}
    factors = {'conv_b': 8.0,
     'attn_sinks': 8.0,
     'mlstm_norm_w': 3.187,
     'g_post_ffn': 2.826,
     'emb_ln_b_2': 2.793,
     'b_ada_2': 4.908,
     'sg_ln_g_2': 29.749,
     'sg_ln_b_2': 64.0,
     'b_s_2': 6.971,
     'w_up_2': 8.0,
     'a0_2': 8.0,
     'a_up_2': 2.899,
     'k_k_2': 23.105,
     'k_a_2': 7.474,
     'r_k_2': 2.978,
     'lnx_g_2': 27.967,
     'lnx_b_2': 64.0,
     'ln1_b_2': 2.819,
     'ln2_b_2': 2.906}
    for name, (base, spread) in spreads.items():
        noise = np.random.default_rng([zlib.crc32(name.encode()), seed]).standard_normal(out[name].shape)
        drawn = base * np.exp(spread * noise) if base else spread * noise
        out[name] = __import__('jax').numpy.asarray(drawn.astype(out[name].dtype))
    for name, factor in factors.items():
        out[name] = (out[name] * factor).astype(out[name].dtype)
    return out
```

```python
import math
import numpy as np
import concourse.bass as bass
from concourse import mybir
from contextlib import ExitStack

S = 256
D = 1024
P = 128
MT = S // P
KT = D // P
FF = 2816
FT = FF // P
HQ, HG, DH = 8, 2, 64
HM, DM = 4, 128
L = 64
NCH = S // L
SLOT_K = 8
SLOT_N = 520
RING = 3
NEG = -1e30
EPS = 1e-6
LN_EPS = 1e-5
GN_EPS = 64e-5
ALPHA = 2 ** 0.25
TWO_PI_1 = 6.28125
TWO_PI_2 = float(np.float32(np.frombuffer(np.uint32(
    np.float32(2 * math.pi - TWO_PI_1).view(np.uint32) & 0xFFFFF000).tobytes(), np.float32)[0]))
TWO_PI_3 = float(np.float32(2 * math.pi - TWO_PI_1 - TWO_PI_2))
ROUND = 12582912.0
SIN_MAX = 3.1415925

CONST = {}
_at = 0
for _name, _n in (("ident", 128), ("attn", 256), ("chunk_t", 128), ("ws", 128), ("ar", 128), ("low", 64),
                  ("b8", 64), ("o8", 64), ("o16", 64), ("o32", 64), ("eye2", 64), ("pairs", 128),
                  ("heads", 32), ("ones", 128), ("freq", 32)):
    CONST[_name] = (_at, _at + _n)
    _at += _n
CONST_N = _at


def constants():
    p = np.arange(P)[:, None]
    f = np.arange(P)[None, :]
    c = np.zeros((P, CONST_N), np.float32)

    def put(name, v):
        a, b = CONST[name]
        c[:, a:b] = v

    q, k = np.arange(P)[:, None], np.arange(2 * P)[None, :]
    rel = k - P
    h = p % L
    g = np.arange(L)[None, :]
    same = lambda n: (h // n == g // n)
    put("ident", np.eye(P))
    put("attn", np.where((rel <= q) & (q - rel < P), 0.0, NEG))
    put("chunk_t", np.where((p // L == f // L) & (p <= f), 0.0, NEG))
    put("ws", p <= f)
    put("ar", np.concatenate([h < g, h <= g], axis=1))
    put("low", g < h)
    put("b8", same(8))
    put("o8", same(16) & ~same(8))
    put("o16", same(32) & ~same(16))
    put("o32", ~same(32))
    put("eye2", h == g)
    put("pairs", p // L == f // L)
    heads = np.zeros((P, 4, 8))
    for j in range(4):
        heads[:L, j, 2 * j] = 1
        heads[L:, j, 2 * j + 1] = 1
    put("heads", heads.reshape(P, 32))
    put("ones", 1.0)
    put("freq", np.float32(10000.0) ** (np.float32(-2.0) * np.arange(32, dtype=np.float32) / np.float32(64)))
    s = np.zeros((8, 1024), np.float32)
    for r in range(4):
        s[r, r * 128:(r + 1) * 128] = 1
    for j in range(4):
        s[2 * j, 512 + j * 128:512 + j * 128 + 64] = 1
        s[2 * j + 1, 512 + j * 128 + 64:512 + (j + 1) * 128] = 1
    return c, s


ROWS1 = (("b_ada", 48), ("g_pre_mix", 8), ("g_pre_ffn", 8), ("conv_w", 32), ("conv_b", 8))
ROWS2 = (("b_ada_2", 48), ("mu_shift_2", 15), ("w0_2", 4), ("a0_2", 4), ("k_k_2", 4), ("k_a_2", 4),
         ("r_k_2", 4), ("lnx_g_2", 4), ("lnx_b_2", 4), ("b_s_2", 4))


def first_rows(rows):
    at, out = 0, {}
    for name, n in rows:
        out[name] = (at, at + n)
        at += n
    return out, at


def weight_items():
    items = [("ada1_0", 4), ("o_if", 1), ("qm", 1), ("km", 1), ("vm", 1), ("qa", 1), ("kva", 1),
             ("g0", 1), ("g1", 1), ("g2", 1), ("g3", 1), ("ada1_1", 4), ("ada1_2", 4),
             ("ada2_0", 4), ("ada2_1", 4), ("ada2_2", 4),
             ("ba0", 1), ("ba1", 1), ("bm0", 1), ("bm1", 1), ("gg1", 0), ("wo0", 1), ("wo1", 1)]
    items += [(f"ff{j}", 1) for j in range(FT // 2)]
    items += [("gg2", 0), ("dn1", 6), ("pu", 1), ("pv", 1), ("r", 1), ("k", 1), ("v", 1), ("lora", 1),
              ("gg3", 0), ("wo2", 1), ("wo3", 1)]
    items += [(f"gf{j}", 1) for j in range(FT // 2)]
    items += [("gg4", 0), ("dn2", 6)]
    return items


ITEMS = weight_items()


def build(nc, A, out):
    fp = mybir.dt.float32
    ALU = mybir.AluOpType
    ACT = mybir.ActivationFunctionType
    AX = mybir.AxisListType.X
    ctx = ExitStack()
    with ctx:
        sems = {}

        def sem(name):
            if name not in sems:
                sems[name] = ctx.enter_context(nc.semaphore(name))
            return sems[name]

        def sb(name, shape):
            return ctx.enter_context(nc.sbuf_tensor(name, shape, fp))

        place, blk, pairs = {}, 0, 0
        for name, n in ITEMS:
            pair = None
            if name[:2] != "dn":
                pair = pairs
                pairs += 1
            place[name] = (pair, blk, blk + n)
            blk += n

        ring = sb("ring", [P, RING, SLOT_K * SLOT_N])
        xt = sb("xt", [P, MT, D])
        xn = sb("xn", [P, MT * D])
        hT = sb("hT", [P, KT, S])
        bc = sb("bc", [P, 4, D])
        bcs = sb("bcs", [P, 3, 512])
        bsm = sb("bsm", [P, 16])
        gg = sb("gg", [P, D])
        cst = sb("cst", [P, CONST_N])
        csel = sb("csel", [8, 1024])
        vraw = sb("vraw", [P, 2, P])
        v1, n1 = first_rows(ROWS1)
        v2, n2 = first_rows(ROWS2)
        v1T = sb("v1T", [P, n1])
        v2T = sb("v2T", [P, n2])
        modT = sb("modT", [P, 2, 48])
        gain = sb("gain", [P, 4, 8])
        cc = sb("cc", [P, 2, 8])
        st = sb("st", [P, 256])
        posi = ctx.enter_context(nc.sbuf_tensor("posi", [P, MT], mybir.dt.int32))
        ARENA = 23300
        arena = sb("arena", [P, ARENA])

        def C(name):
            a, b = CONST[name]
            return cst[:, a:b]

        ident = C("ident")

        def region(at, n):
            assert at + n <= ARENA, (at, n)
            return arena[:, at:at + n]

        pos = [0]

        def take(n):
            pos[0] += n
            return region(pos[0] - n, n)

        conv_in = take(8 * 259).rearrange("p (t n) -> p t n", t=8)
        rope_a = take(640)
        rope_b = take(640)
        pT = region(0, 24 * 128).rearrange("p (t n) -> p t n", t=24)
        qk = take(8 * S).rearrange("p (t n) -> p t n", t=8)
        qr = take(MT * 512).rearrange("p (m n) -> p m n", m=MT)
        ya = qr
        kr = take(MT * 128).rearrange("p (m n) -> p m n", m=MT)
        va = take(MT * 128).rearrange("p (m n) -> p m n", m=MT)
        qT = take(4 * S).rearrange("p (i n) -> p i n", i=4)
        yaT = qT
        kT = take(S)
        sm0 = take(8 * 128).rearrange("p (h n) -> p h n", h=8)
        sm1 = xn[:, :].rearrange("p (h n) -> p h n", h=8)
        vaug = take(MT * HM * 129).rearrange("p (m h n) -> p m h n", m=MT, h=HM)
        osig = take(MT * 512).rearrange("p (m n) -> p m n", m=MT)
        ym = osig
        rows = take(10 * S).rearrange("p (r n) -> p r n", r=10)
        wT = bc[:, 2, :].rearrange("p (h m n) -> p h m n", h=HM, m=MT)
        sw = bc[:, 3, :].rearrange("p (h m n) -> p h m n", h=HM, m=MT)
        kw = take(MT * 512).rearrange("p (m h n) -> p m h n", m=MT, h=HM)
        ymT = kw.rearrange("p m h n -> p (m h n)").rearrange("p (i n) -> p i n", i=4)
        cst_at = pos[0]
        cstate = take(NCH * HM * 129).rearrange("p (c h n) -> p c h n", c=NCH, h=HM)
        merged = region(cst_at, 8 * S).rearrange("p (t n) -> p t n", t=8)
        intra = take(MT * HM * 129).rearrange("p (m h n) -> p m h n", m=MT, h=HM)
        gT = take(16 * S).rearrange("p (t n) -> p t n", t=16)
        rsc = take(MT * 2 * 32 * 2).rearrange("p (w m f c) -> p w m f c", w=2, m=MT, f=2)
        cossin = take(MT * 2 * 32).rearrange("p (m f c) -> p m f c", m=MT, f=2)
        ffT = region(0, FT * S).rearrange("p (t n) -> p t n", t=FT)
        sil = region(FT * S, 2 * 512).rearrange("p (b n) -> p b n", b=2)
        pos[0] = 0
        praw = take(15 * 257).rearrange("p (t n) -> p t n", t=15)
        aT_rT = region(0, 2048).rearrange("p (j c w n) -> p j c w n", j=4, c=NCH, w=2)
        bT = region(2048, 1024).rearrange("p (j n) -> p j n", j=4)
        pm = take(15 * S).rearrange("p (t n) -> p t n", t=15)
        t_at = pos[0]
        tmp = [take(1024).rearrange("p (j n) -> p j n", j=4) for _ in range(7)]
        kk, av, lw, cum, dec1, dec2, dtmp = tmp
        inv = [t.rearrange("p j n -> p (j n)").rearrange("p (q n) -> p q n", q=16) for t in tmp]
        kTt = take(1024).rearrange("p (j n) -> p j n", j=4)
        vtok = take(1024).rearrange("p (q n) -> p q n", q=16)
        gB = take(2048).rearrange("p (q w n) -> p q w n", q=16, w=2)
        gK = xn[:, :].rearrange("p (q w n) -> p q w n", q=16, w=2)
        nlow = take(1024).rearrange("p (q n) -> p q n", q=16)
        xs = take(256).rearrange("p (j n) -> p j n", j=4)
        us = take(256).rearrange("p (j n) -> p j n", j=4)
        ms = take(256).rearrange("p (j n) -> p j n", j=4)
        cat = take(8 * S).rearrange("p (t n) -> p t n", t=8)
        reset = gg[:, :]
        nrm = take(256)
        btok = hT[:, 0:4, :].rearrange("p t n -> p (t n)").rearrange("p (q n) -> p q n", q=16)
        ktok = hT[:, 4:8, :].rearrange("p t n -> p (t n)").rearrange("p (q n) -> p q n", q=16)
        bonus = pm[:, 4:8, :]
        yT = cat[:, 4:8, :]
        lup = bc[:, 0, 0:512]
        gu0 = bc[:, 0, 512:1024]
        gu1 = bc[:, 1, 0:512]
        wsr = bc[:, 1, 512:1024].rearrange("p (g n) -> p g n", g=4)
        wsT = bc[:, 2, 0:512].rearrange("p (g n) -> p g n", g=4)
        gmT = bc[:, 3, :].rearrange("p (j n) -> p j n", j=4)
        gv = xn[:, 0:1024].rearrange("p (m n) -> p m n", m=MT)
        gu = xn[:, 1024:2048].rearrange("p (m n) -> p m n", m=MT)

        bank = [ctx.enter_context(nc.psum_tensor(f"bank{i}", [P, 512], fp)) for i in range(8)]

        def wsrc(w, r0, nk, c0, n):
            return w[0, r0:r0 + nk * P, c0:c0 + n].rearrange("(k p) n -> p k n", p=P)

        def ada_src(w, c0):
            return w[0, :, c0:c0 + 512].rearrange("(p k) n -> p k n", k=8)

        def slot(b, nk, n):
            return ring[:, b % RING, 0:nk * n].rearrange("p (k n) -> p k n", k=nk)

        blocks = []
        for name, n in ITEMS:
            if name[:3] == "ada":
                w = A["w_ada"] if name[3] == "1" else A["w_ada_2"]
                u = int(name[5])
                blocks += [[(ada_src(w, 2048 * u + 512 * i), 8, 512, 0, 512)] for i in range(4)]
            elif name in ("o_if", "qm", "km", "vm", "qa", "kva", "g0", "g1", "g2", "g3"):
                c0, w = {"o_if": (2304, 520), "qm": (768, 512), "km": (1280, 512), "vm": (1792, 512),
                         "qa": (0, 512), "kva": (512, 256), "g0": (2824, 512), "g1": (3336, 512),
                         "g2": (3848, 512), "g3": (4360, 512)}[name]
                blocks.append([(wsrc(A["w_in"], 0, 8, c0, w), 8, w, 0, w)])
            elif name in ("pu", "pv", "r", "k", "v", "lora"):
                c0, w = {"pu": (0, 512), "pv": (512, 512), "r": (1024, 512), "k": (1536, 512),
                         "v": (2048, 512), "lora": (2560, 288)}[name]
                blocks.append([(wsrc(A["w_in_2"], 0, 8, c0, w), 8, w, 0, w)])
            elif name in ("ba0", "ba1", "bm0", "bm1"):
                w = A["w_branch_attn"] if name[1] == "a" else A["w_branch_mlstm"]
                blocks.append([(wsrc(w, 0, 4, 512 * int(name[2]), 512), 4, 512, 0, 512)])
            elif name[:2] == "wo":
                w, i = (A["w_out"], int(name[2])) if int(name[2]) < 2 else (A["w_out_2"], int(name[2]) - 2)
                blocks.append([(wsrc(w, 0, 8, 512 * i, 512), 8, 512, 0, 512)])
            elif name[:2] == "ff":
                c0 = 256 * int(name[2:])
                blocks.append([(wsrc(A["w_ffn_gate"], 0, 8, c0, 256), 8, 512, 0, 256),
                               (wsrc(A["w_ffn_up"], 0, 8, c0, 256), 8, 512, 256, 512)])
            elif name[:2] == "gf":
                c0 = 256 * int(name[2:])
                blocks.append([(wsrc(A["w_ffn_in_2"], 0, 8, c0, 256), 8, 512, 0, 256),
                               (wsrc(A["w_ffn_in_2"], 0, 8, FF + c0, 256), 8, 512, 256, 512)])
            elif name[:2] == "dn":
                w = A["w_ffn_down"] if name == "dn1" else A["w_ffn_out_2"]
                for i in range(6):
                    nk = min(4, FT - 4 * i)
                    blocks.append([(wsrc(w, 512 * i, nk, 0, 1024), nk, 1024, 0, 1024)])
        landed, total = [], [0] * RING
        for b, parts in enumerate(blocks):
            total[b % RING] += 16 * len(parts)
            landed.append(total[b % RING])

        block = ctx.enter_context(nc.Block())

        @block.sync
        def _(sp):
            sp.dma_start(xt[:, :, :], A["x"][0].rearrange("(m p) n -> p m n", p=P)).then_inc(sem("x_in"), 16)
            for b, parts in enumerate(blocks):
                if b >= RING:
                    sp.wait_ge(sem("blocks_done"), b - RING + 1)
                for src, nk, width, a, z in parts:
                    sp.dma_start(slot(b, nk, width)[:, :, a:z], src).then_inc(sem(f"slot{b % RING}_in"), 16)
            for m in range(MT):
                sp.wait_ge(sem("y_out"), m + 1)
                sp.dma_start(out[0, m * P:(m + 1) * P, :], xt[:, m, :]).then_inc(sem("out_stored"), 16)
            sp.wait_ge(sem("out_stored"), 16 * MT)

        @block.gpsimd
        def _(pool):
            pool.memset(vraw[:, :, :], 0.0).then_inc(sem("vraw_zero"), 1)
            pool.memset(conv_in[:, :, 0:3], 0.0).then_inc(sem("pads"), 1)
            pool.memset(vaug[:, :, :, 128:129], 1.0).then_inc(sem("pads"), 1)
            pool.memset(cstate[:, 0, :, :], 0.0).then_inc(sem("pads"), 1)
            pool.memset(rows[0:4, 0, :], 1.0).then_inc(sem("pads"), 1)
            pool.memset(rows[0:4, 1, :], 0.0).then_inc(sem("pads"), 1)
            pool.wait_ge(sem("pads"), 5)
            pool.memset(rows[0:4, 0, :].rearrange("p (c n) -> p c n", c=NCH)[:, :, 0:1], 0.0).then_inc(sem("pads"), 1)
            pool.memset(rows[0:4, 1, :].rearrange("p (c n) -> p c n", c=NCH)[:, :, 0:1], NEG).then_inc(sem("pads"), 1)

            def spread(dst, src, s):
                pool.dma_start(dst, src.partition_broadcast(P)).then_inc(s, 16)

            spread(bsm[:, 0:8], A["b_if"][0], sem("spread1"))
            spread(bsm[:, 8:16], A["attn_sinks"][0], sem("spread1"))
            spread(bcs[:, 0, :], A["mlstm_norm_w"][0], sem("spread1"))
            spread(bcs[:, 1, :], A["sg_ln_g_2"][0], sem("spread1"))
            spread(bcs[:, 2, :], A["sg_ln_b_2"][0], sem("spread1"))
            spread(bc[:, 0, :], A["g_post_mix"][0], sem("spread1"))
            spread(bc[:, 1, :], A["g_post_ffn"][0], sem("spread1"))
            pool.wait_ge(sem("hT_ready"), 16)
            spread(bc[:, 2, :], A["emb_ln_g_2"], sem("spread2"))
            spread(bc[:, 3, :], A["emb_ln_b_2"], sem("spread2"))
            pool.wait_ge(sem("emb_done"), 2)
            pool.dma_start(lup[0:64, :], A["w_up_2"][0]).then_inc(sem("lora_in"), 16)
            pool.dma_start(lup[64:128, :], A["a_up_2"][0]).then_inc(sem("lora_in"), 16)
            pool.dma_start(gu0, A["g_up_2"][0, 0:128, :]).then_inc(sem("lora_in"), 16)
            pool.dma_start(gu1[0:32, :], A["g_up_2"][0, 128:160, :]).then_inc(sem("lora_in"), 16)
            pool.dma_start(wsr, A["w_s_2"][0].rearrange("g t s -> t g s")).then_inc(sem("ws_in"), 16)
            pool.memset(praw[:, :, 0:1], 0.0).then_inc(sem("pads2"), 1)
            pool.memset(ms, 0.0).then_inc(sem("pads2"), 1)
            pool.memset(reset, 1.0).then_inc(sem("pads2"), 1)
            pool.wait_ge(sem("pads2"), 3)
            pool.memset(reset.rearrange("p (q n) -> p q n", q=16)[:, :, 0:1], 0.0).then_inc(sem("pads2"), 1)
            pool.wait_ge(sem("yb_ready"), 1)
            spread(bc[:, 0, :], A["ln1_g_2"][0], sem("spread3"))
            spread(bc[:, 1, :], A["ln1_b_2"][0], sem("spread3"))
            spread(bc[:, 2, :], A["ln2_g_2"][0], sem("spread3"))
            spread(bc[:, 3, :], A["ln2_b_2"][0], sem("spread3"))

        def flat(name):
            a = A[name]
            if name == "conv_w":
                return a[0].rearrange("j (t p) -> (j t) p", p=P)
            if name == "b_s_2":
                return a[0]
            if name == "r_k_2":
                return a[0].rearrange("(t h) n -> t (h n)", h=2)
            return a[0].rearrange("(t p) -> t p", p=P)

        @block.scalar
        def _(act):
            chain = [0]

            def step(ins):
                chain[0] += 1
                ins.then_inc(sem("act_chain"), 1)
                act.wait_ge(sem("act_chain"), chain[0])

            def item(name):
                pair, _, z = place[name]
                act.wait_ge(sem("blocks_done"), z)
                return bank[2 * (pair % 2)], bank[2 * (pair % 2) + 1]

            def freed(name, ins):
                ins.then_inc(sem(f"pair{place[name][0] % 2}_free"), 1)

            act.dma_start(cst[:, :], A["const"]).then_inc(sem("const_in"), 16)
            act.dma_start(csel[:, :], A["selector"]).then_inc(sem("const_in"), 16)
            act.dma_start(cc[:, 0, :], A["c"][0].rearrange("(p k) -> p k", k=8)).then_inc(sem("c_in"), 16)
            act.dma_start(cc[:, 1, :], A["c_2"][0].rearrange("(p k) -> p k", k=8)).then_inc(sem("c_in"), 16)
            act.dma_start(posi[:, :], A["positions"][0].rearrange("(m p) -> p m", p=P),
                          allow_slow_non_contiguous=True).then_inc(sem("pos_in"), 16)
            act.wait_ge(sem("vraw_zero"), 1)
            for i, (tab, where) in enumerate(((ROWS1, v1), (ROWS2, v2))):
                for name, n in tab:
                    a, b = where[name]
                    if name == "mu_shift_2":
                        act.dma_start(vraw[a:b - 1, i, :], A[name][0, 0:14 * P].rearrange("(t p) -> t p", p=P))\
                           .then_inc(sem(f"vec{i}_in"), 16)
                        act.dma_start(vraw[b - 1:b, i, 0:32], A[name][:, 14 * P:1824]).then_inc(sem(f"vec{i}_in"), 16)
                    else:
                        act.dma_start(vraw[a:b, i, :], flat(name)).then_inc(sem(f"vec{i}_in"), 16)

            def rms_squares(src, col, s):
                return act.activation(s, src, ACT.Square, accum_out=st[:, col:col + 1])

            def evac_h(u):
                g = gain[:, u, :]
                sh = modT[:, u // 2, (24 if u % 2 else 0):(32 if u % 2 else 8)]
                act.wait_ge(sem("gain_ready"), 2 * u + 2)
                for k in range(4):
                    act.wait_ge(sem("hx_turned"), 4 * u + k // 2 + 1)
                    act.activation(hT[:, k, :], bank[4 + k // 2][:, 256 * (k % 2):256 * (k % 2) + 256], ACT.Identity,
                                   bias=sh[:, k:k + 1], scale=g[:, k:k + 1]).then_inc(sem("hT_ready"), 1)

            def branch_gates(n):
                for h, b in enumerate(item(f"g{n}")):
                    ins = act.activation(gT[:, 4 * n + 2 * h:4 * n + 2 * h + 2, :],
                                         b[:, :].rearrange("p (t n) -> p t n", t=2), ACT.Sigmoid)
                    ins.then_inc(sem("gT_ready"), 1) if h == 0 else freed(f"g{n}", ins)

            act.wait_ge(sem("x_in"), 16)
            for m in range(MT):
                act.activation(xn[:, m * D:(m + 1) * D], xt[:, m, :], ACT.Square,
                               accum_out=st[:, m:m + 1]).then_inc(sem("squares"), 1)
            act.wait_ge(sem("var_ready"), 1)
            act.activation(st[:, 4:6], st[:, 2:4], ACT.Sqrt).then_inc(sem("std_ready"), 1)
            act.wait_ge(sem("c_in"), 32)
            act.activation(cc[:, 1, :], cc[:, 1, :], ACT.Silu).then_inc(sem("cs_ready"), 1)
            act.wait_ge(sem("angles"), 1)
            act.activation(cossin, rsc[:, 1], ACT.Sin).then_inc(sem("cossin_ready"), 1)
            evac_h(0)
            b0, b1 = item("o_if")
            act.activation(osig[:, 0, :], b0[:, :], ACT.Sigmoid).then_inc(sem("osig_ready"), 1)
            freed("o_if", act.activation(osig[:, 1, :], b1[:, :], ACT.Sigmoid))
            for t0, name in ((0, "qm"), (4, "km")):
                for h, b in enumerate(item(name)):
                    act.wait_ge(sem("pads"), 1)
                    ins = act.activation(conv_in[:, t0 + 2 * h:t0 + 2 * h + 2, 3:259],
                                         b[:, :].rearrange("p (t n) -> p t n", t=2), ACT.Copy)
                    if h == 0:
                        ins.then_inc(sem("conv_raw"), 1)
                    else:
                        freed(name, ins)
            act.wait_ge(sem("if_turned"), 1)
            r_i, r_f, r_l = rows[0:4, 2, :], rows[0:4, 3, :], rows[0:4, 4, :]
            act.activation(r_i, bank[7][0:4, 0:256], ACT.Copy).then_inc(sem("act_chain"), 1)
            chain[0] += 1
            step(act.activation(r_f, bank[7][0:4, 256:512], ACT.Copy))
            step(act.activation(r_l, r_f, ACT.Abs))
            step(act.activation(r_l, r_l, ACT.Exp, scale=-1.0))
            act.activation(r_l, r_l, ACT.Ln, bias=1.0).then_inc(sem("log_ready"), 1)
            for m, b in enumerate(item("vm")):
                ins = act.activation(vaug[:, m, :, 0:128], b[:, :].rearrange("p (h n) -> p h n", h=HM), ACT.Copy)
                ins.then_inc(sem("v_ready"), 1) if m == 0 else freed("vm", ins)
            act.wait_ge(sem("rows_ready"), 1)
            act.activation(rows[0:4, 6, :], rows[0:4, 6, :], ACT.Exp).then_inc(sem("rows_exp"), 1)
            act.activation(rows[0:4, 7, :], rows[0:4, 7, :], ACT.Exp).then_inc(sem("rows_exp"), 1)
            act.activation(rows[0:4, 8, :], rows[0:4, 8, :], ACT.Exp, scale=-1.0).then_inc(sem("rows_exp"), 1)
            act.activation(rows[0:4, 4, 16:20], rows[0:4, 4, 16:20], ACT.Exp).then_inc(sem("rows_exp"), 1)
            act.wait_ge(sem("conv_done"), 1)
            for t in range(2):
                act.activation(qk[:, 4 * t:4 * t + 4, :], qk[:, 4 * t:4 * t + 4, :], ACT.Silu)\
                   .then_inc(sem("silu_done"), 1)
            act.wait_ge(sem("arg_ready"), 1)
            for h in range(HM):
                for m in range(MT):
                    act.activation(wT[:, h, m, :], wT[:, h, m, :], ACT.Exp,
                                   bias=st[:, 64 + 16 * m + h:64 + 16 * m + h + 1]).then_inc(sem("wT_ready"), 1)
            for n in range(3):
                branch_gates(n)
            for m in range(MT):
                act.wait_ge(sem("qr_turned"), m + 1)
                act.activation(qT[:, :, m * P:(m + 1) * P], bank[4 + m][:, :].rearrange("p (i n) -> p i n", i=4),
                               ACT.Copy, scale=DH ** -0.5).then_inc(sem("qT_ready"), 1)
            act.wait_ge(sem("qr_turned"), 3)
            act.activation(kT, bank[6][:, 0:256], ACT.Copy).then_inc(sem("qT_ready"), 1)
            for m, sm in ((0, sm0), (1, sm1)):
                act.wait_ge(sem("smax_ready"), m + 1)
                for h in range(HQ):
                    act.activation(sm[:, h, :], sm[:, h, :], ACT.Exp, bias=st[:, 16 + 8 * m + h:17 + 8 * m + h],
                                   accum_out=st[:, 32 + 8 * m + h:33 + 8 * m + h]).then_inc(sem("exp_ready"), 1)
                act.activation(st[:, 48 + 8 * m:56 + 8 * m], st[:, 48 + 8 * m:56 + 8 * m], ACT.Exp)\
                   .then_inc(sem("exp_ready"), 1)
            branch_gates(3)
            for n in range(6):
                act.wait_ge(sem("p_turned"), n + 1)
                act.activation(pT[:, 4 * n:4 * n + 4, :], bank[4 + n % 4][:, :].rearrange("p (h n) -> p h n", h=4),
                               ACT.Copy).then_inc(sem("pT_ready"), 1)
            for m in range(MT):
                for h2 in range(2):
                    act.wait_ge(sem("intra_done"), 2 * m + h2 + 1)
                    act.activation(intra[:, m, 2 * h2:2 * h2 + 2, :],
                                   bank[4 + 2 * 0 + h2][:, 0:258].rearrange("p (h n) -> p h n", h=2),
                                   ACT.Copy).then_inc(sem("intra_ready"), 1)
            act.wait_ge(sem("hvar_ready"), 1)
            act.activation(st[:, 112:120], st[:, 112:120], ACT.Sqrt).then_inc(sem("hstd_ready"), 1)
            for m in range(MT):
                act.wait_ge(sem("ya_turned"), m + 1)
                act.activation(yaT[:, :, m * P:(m + 1) * P], bank[4 + m][:, :].rearrange("p (i n) -> p i n", i=4),
                               ACT.Copy).then_inc(sem("yaT_ready"), 1)
            for m in range(MT):
                act.wait_ge(sem("ym_turned"), m + 1)
                act.activation(ymT[:, :, m * P:(m + 1) * P], bank[6 + m][:, :].rearrange("p (i n) -> p i n", i=4),
                               ACT.Copy).then_inc(sem("ymT_ready"), 1)

            def post_rms(names, base, u):
                for i, b in enumerate(names):
                    m, half = i // 2, i % 2
                    act.activation(sil_out[:, :], b, ACT.Square,
                                   accum_out=st[:, base + i:base + i + 1]).then_inc(sem("post_squares"), 1)

            def std(n, a, z):
                act.wait_ge(sem("var_ready"), n)
                act.activation(st[:, a:z], st[:, a:z], ACT.Sqrt).then_inc(sem("std_ready"), 1)

            sil_out = xn[:, 0:512]
            wo = [item("wo0"), item("wo1")]
            act.wait_ge(sem("gg_free"), 1)
            for m in range(MT):
                for half in range(2):
                    step(act.activation(sil_out, wo[half][m][:, :], ACT.Square,
                                        accum_out=st[:, 120 + 2 * m + half:121 + 2 * m + half]))
            act.nop().then_inc(sem("post_squares"), 1)
            std(2, 124, 126)
            for m in range(MT):
                act.wait_ge(sem("x_added"), m + 1)
                act.activation(xn[:, m * D:(m + 1) * D], xt[:, m, :], ACT.Square,
                               accum_out=st[:, m:m + 1]).then_inc(sem("squares"), 1)
            act.wait_ge(sem("var_ready"), 3)
            act.activation(st[:, 4:6], st[:, 2:4], ACT.Sqrt).then_inc(sem("std_ready"), 1)
            evac_h(1)

            def feed_forward(letter, n):
                for j in range(FT // 2):
                    g, _ = item(f"{letter}{j}")
                    q = n * (FT // 2) + j
                    if j >= 2:
                        act.wait_ge(sem("ff_ready"), q - 1)
                    act.activation(sil[:, j % 2, :], g[:, :], ACT.Silu).then_inc(sem("sil_ready"), 1)

            feed_forward("ff", 0)
            act.wait_ge(sem("blocks_done"), place["dn1"][2])
            act.wait_ge(sem("gg_free"), 2)
            for m in range(MT):
                for half in range(2):
                    step(act.activation(sil_out, bank[4 + 2 * m + half][:, :], ACT.Square,
                                        accum_out=st[:, 120 + 2 * m + half:121 + 2 * m + half]))
            act.nop().then_inc(sem("post_squares"), 1)
            std(4, 124, 126)
            std(5, 126, 128)
            evac_h(2)

            for name, dst in (("pu", gu), ("pv", gv)):
                act.wait_ge(sem("hx_turned"), 12)
                for m, b in enumerate(item(name)):
                    ins = act.activation(dst[:, m, :], b[:, :], ACT.Gelu_apprx_tanh)
                    ins.then_inc(sem("gelu_done"), 1) if m == 0 else freed(name, ins)
            act.wait_ge(sem("gvar_ready"), 1)
            act.activation(st[:, 132:134], st[:, 132:134], ACT.Sqrt).then_inc(sem("gstd_ready"), 1)
            act.wait_ge(sem("pads2"), 1)
            for t0, name in ((0, "r"), (4, "k"), (8, "v")):
                for h, b in enumerate(item(name)):
                    ins = act.activation(praw[:, t0 + 2 * h:t0 + 2 * h + 2, 1:257],
                                         b[:, :].rearrange("p (t n) -> p t n", t=2), ACT.Copy)
                    ins.then_inc(sem("praw_ready"), 1) if h == 0 else freed(name, ins)
            b0, b1 = item("lora")
            act.activation(praw[:, 12:14, 1:257], b0[:, :].rearrange("p (t n) -> p t n", t=2), ACT.Copy)\
               .then_inc(sem("praw_ready"), 1)
            freed("lora", act.activation(praw[0:32, 14, 1:257], b1[0:32, 0:256], ACT.Copy))
            act.wait_ge(sem("lora_mixed"), 1)
            act.activation(pm[0:64, 12, :], pm[0:64, 12, :], ACT.Tanh).then_inc(sem("lora_act"), 1)
            act.activation(pm[:, 13, :], pm[:, 13, :], ACT.Sigmoid).then_inc(sem("lora_act"), 1)
            act.activation(pm[0:32, 14, :], pm[0:32, 14, :], ACT.Sigmoid).then_inc(sem("lora_act"), 1)
            for n, (dst, off) in enumerate(((lw, "w0_2"), (av, "a0_2"))):
                for j in range(4):
                    act.wait_ge(sem("lora_done"), 2 * n + j // 2 + 1)
                    act.activation(dst[:, j, :], bank[4 + 2 * n + j // 2][:, 256 * (j % 2):256 * (j % 2) + 256],
                                   ACT.Sigmoid, bias=v2T[:, v2[off][0] + j:v2[off][0] + j + 1])\
                       .then_inc(sem("lwa_ready"), 1)
            for j in range(2):
                act.wait_ge(sem("lora_done"), 5 + j)
                act.activation(gmT[:, 2 * j:2 * j + 2, :], bank[4 + j][:, :].rearrange("p (t n) -> p t n", t=2),
                               ACT.Copy).then_inc(sem("gm_ready"), 1)
            act.wait_ge(sem("kk_summed"), 1)
            act.activation(nrm[0:8, :], bank[6][0:8, 0:256], ACT.Sqrt).then_inc(sem("kk_len"), 1)
            act.wait_ge(sem("cum_ready"), 1)
            act.activation(dec1, cum, ACT.Exp).then_inc(sem("dec_ready"), 1)
            act.wait_ge(sem("cum_ready"), 2)
            act.activation(dec2, lw, ACT.Exp).then_inc(sem("dec_ready"), 1)
            act.wait_ge(sem("dec_ready"), 2)
            act.activation(lw, cum, ACT.Exp, scale=-1.0).then_inc(sem("dec_ready"), 1)
            for n, dst in enumerate((btok, ktok, vtok)):
                for h in range(2):
                    act.wait_ge(sem("tok_turned"), 2 * n + h + 1)
                    act.activation(dst[:, 8 * h:8 * h + 8, :],
                                   bank[(2 * n + h) % 4 + 4][:, :].rearrange("p (q n) -> p q n", q=8), ACT.Copy)\
                       .then_inc(sem("tok_ready"), 1)
            for c in range(NCH):
                act.wait_ge(sem("x_done"), c + 1)
                act.activation(xs, bank[4][:, 0:256].rearrange("p (j n) -> p j n", j=4), ACT.Copy)\
                   .then_inc(sem("x_ready"), 1)
                act.wait_ge(sem("u_done"), c + 1)
                act.activation(us, bank[5][:, 0:256].rearrange("p (j n) -> p j n", j=4), ACT.Copy)\
                   .then_inc(sem("u_ready"), 1)
                act.wait_ge(sem("yc_done"), c + 1)
                act.activation(yT[:, :, c * L:(c + 1) * L], bank[7][:, 0:256].rearrange("p (j n) -> p j n", j=4),
                               ACT.Copy).then_inc(sem("yc_ready"), 1)
            act.wait_ge(sem("yvar_ready"), 1)
            act.activation(nrm[0:8, :], nrm[0:8, :], ACT.Sqrt).then_inc(sem("ystd_ready"), 1)
            std(6, 126, 128)
            evac_h(3)
            feed_forward("gf", 1)
            std(7, 126, 128)

        @block.vector
        def _(dve):
            chain = [0]

            def step(ins):
                chain[0] += 1
                ins.then_inc(sem("dve_chain"), 1)
                dve.wait_ge(sem("dve_chain"), chain[0])

            def item(name):
                pair, _, z = place[name]
                dve.wait_ge(sem("blocks_done"), z)
                return bank[2 * (pair % 2)], bank[2 * (pair % 2) + 1]

            def freed(name, ins):
                ins.then_inc(sem(f"pair{place[name][0] % 2}_free"), 1)

            def bcast(ap, n):
                return ap.unsqueeze(len(ap.shape)).to_broadcast(list(ap.shape) + [n])

            TT = dve.tensor_tensor
            TS = dve.tensor_scalar
            STT = dve.scalar_tensor_tensor
            for i, (dst, n) in enumerate(((v1T, n1), (v2T, n2))):
                dve.wait_ge(sem("vec_turned"), i + 1)
                step(dve.tensor_copy(dst[:, :], bank[4 + i][:, 0:n]))

            def rms_rows(n):
                dve.wait_ge(sem("squares"), 2 * n + 2)
                step(TS(st[:, 2:4], st[:, 0:2], 1.0 / D, EPS, ALU.mult, ALU.add))
                step(dve.reciprocal(st[:, 2:4], st[:, 2:4]))
                dve.nop().then_inc(sem("var_ready"), 1)

            rms_rows(0)
            dve.wait_ge(sem("std_ready"), 1)
            for m in range(MT):
                TS(xn[:, m * D:(m + 1) * D], xt[:, m, :], st[:, 4 + m:5 + m], None, ALU.mult)\
                    .then_inc(sem("xn_ready"), 1)
            dve.wait_ge(sem("pos_in"), 16)
            dve.wait_ge(sem("const_in"), 32)
            step(dve.tensor_copy(st[:, 10:12], posi[:, :]))
            ang, red = rsc[:, 0], rsc[:, 1]
            for m in range(MT):
                for f in range(2):
                    TS(ang[:, m, f, :], C("freq"), st[:, 10 + m:11 + m], None, ALU.mult).then_inc(sem("dve_chain"), 1)
                    chain[0] += 1
            dve.wait_ge(sem("dve_chain"), chain[0])
            step(TS(red[:, :, 0, :], ang[:, :, 0, :], 1 / (2 * math.pi), 0.0, ALU.mult, ALU.add))
            step(TS(red[:, :, 1, :], ang[:, :, 1, :], 1 / (2 * math.pi), 0.25, ALU.mult, ALU.add))
            step(TS(red, red, ROUND, None, ALU.add))
            step(TS(red, red, ROUND, None, ALU.subtract))
            for piece in (TWO_PI_1, TWO_PI_2, TWO_PI_3):
                a2, r2 = (v.rearrange("p m f c -> p (m f c)") for v in (ang, red))
                step(STT(a2, r2, -piece, a2, ALU.mult, ALU.add))
            step(TS(ang[:, :, 1, :], ang[:, :, 1, :], math.pi / 2, None, ALU.add))
            TS(red, ang, SIN_MAX, -SIN_MAX, ALU.min, ALU.max).then_inc(sem("angles"), 1)

            def modulation(i, u):
                b0, _ = item(f"ada{i + 1}_{u}")
                src = v1T if i == 0 else v2T
                freed(f"ada{i + 1}_{u}", TT(modT[:, i, 16 * u:16 * u + 16], b0[:, 0:16], src[:, 16 * u:16 * u + 16],
                                            ALU.add))

            def gains(u, g):
                i, c0 = u // 2, (32 if u % 2 else 8)
                sc = modT[:, i, c0:c0 + 8]
                step(TS(gain[:, u, :], sc, 1.0, None, ALU.add))
                if g is not None:
                    step(TT(gain[:, u, :], gain[:, u, :], g, ALU.mult))
                dve.nop().then_inc(sem("gain_ready"), 2)

            def pair_wait(name):
                dve.wait_ge(sem(f"pair{place[name][0] % 2}_free"), place[name][0] // 2 + 1)

            def evac_h(u):
                sh = modT[:, u // 2, (24 if u % 2 else 0):(32 if u % 2 else 8)]
                for k in range(4, 8):
                    dve.wait_ge(sem("hx_turned"), 4 * u + k // 2 + 1)
                    TS(hT[:, k, :], bank[4 + k // 2][:, 256 * (k % 2):256 * (k % 2) + 256], gain[:, u, k:k + 1],
                       sh[:, k:k + 1], ALU.mult, ALU.add).then_inc(sem("hT_ready"), 1)

            modulation(0, 0)
            pair_wait("ada1_0")
            gains(0, v1T[:, v1["g_pre_mix"][0]:v1["g_pre_mix"][1]])
            evac_h(0)
            item("o_if")
            dve.wait_ge(sem("spread1"), 7 * 16)
            for m in range(MT):
                TT(st[:, 240 + 8 * m:248 + 8 * m], bank[4][:, 8 * m:8 * m + 8], bsm[:, 0:8], ALU.add)\
                    .then_inc(sem("if_ready"), 1)
            dve.wait_ge(sem("osig_ready"), 1)
            dve.wait_ge(sem(f"pair{place['o_if'][0] % 2}_free"), place["o_if"][0] // 2 + 1)
            for m in range(MT):
                step(TT(osig[:, m, :], osig[:, m, :], bcs[:, 0, :], ALU.mult))
            for t in range(8):
                name = "qm" if t < 4 else "km"
                if t % 4 < 2:
                    dve.wait_ge(sem("conv_raw"), t // 4 + 1)
                else:
                    dve.wait_ge(sem(f"pair{place[name][0] % 2}_free"), place[name][0] // 2 + 1)
                w = lambda j: v1T[:, v1["conv_w"][0] + 8 * j + t:v1["conv_w"][0] + 8 * j + t + 1]
                cb = v1T[:, v1["conv_b"][0] + t:v1["conv_b"][0] + t + 1]
                step(TS(qk[:, t, :], conv_in[:, t, 0:256], w(0), cb, ALU.mult, ALU.add))
                for j in range(1, 4):
                    step(STT(qk[:, t, :], conv_in[:, t, j:j + 256], w(j), qk[:, t, :], ALU.mult, ALU.add))
            dve.nop().then_inc(sem("conv_done"), 1)

            def row(i):
                return rows[0:4, i, :]

            def chunked(i):
                return rows[0:4, i, :].rearrange("p (c n) -> p c n", c=NCH)

            dve.wait_ge(sem("log_ready"), 1)
            dve.wait_ge(sem("pads"), 7)
            step(STT(row(3), row(3), 0.0, row(4), ALU.min, ALU.subtract))
            step(dve.tensor_tensor_scan(row(5), row(0), row(3), 0.0, ALU.mult, ALU.add))
            step(TT(row(2), row(2), row(5), ALU.subtract))
            step(dve.tensor_tensor_scan(row(8), row(1), row(2), 0.0, ALU.add, ALU.max))
            bl = rows[0:4, 4, 0:4]
            amax, mnew, mprev, dcy = (rows[0:4, 4, 4 * i:4 * i + 4] for i in range(1, 5))
            step(dve.tensor_copy(bl, chunked(5)[:, :, L - 1]))
            step(TT(chunked(6), chunked(2), bcast(bl, L), ALU.add))
            step(dve.tensor_reduce(amax, chunked(6), AX, ALU.max))
            step(dve.tensor_tensor_scan(mnew, bl, amax, 0.0, ALU.add, ALU.max))
            step(dve.memset(mprev[:, 0:1], 0.0))
            step(dve.tensor_copy(mprev[:, 1:4], mnew[:, 0:3]))
            step(TT(dcy, bl, mprev, ALU.add))
            step(TT(dcy, dcy, mnew, ALU.subtract))
            step(TT(chunked(6), chunked(6), bcast(mnew, L), ALU.subtract))
            step(TT(chunked(7), chunked(5), bcast(mprev, L), ALU.add))
            step(TT(row(8), row(8), row(5), ALU.add))
            step(TT(row(8), row(8), row(7), ALU.max))
            step(TT(row(7), row(7), row(8), ALU.subtract))
            step(TT(row(9), row(5), row(8), ALU.subtract))
            dve.nop().then_inc(sem("rows_ready"), 1)
            def rotate(src, nh, m, dst):
                w = nh * 64
                v = src.rearrange("p (h f c) -> p h f c", h=nh, f=2)
                fa = rope_a[:, 0:w].rearrange("p (h f c) -> p h f c", h=nh, f=2)
                fb = rope_b[:, 0:w].rearrange("p (h f c) -> p h f c", h=nh, f=2)
                cos = cossin[:, m, 1, :].unsqueeze(1).to_broadcast([P, nh, 32])
                sin = cossin[:, m, 0, :].unsqueeze(1).to_broadcast([P, nh, 32])
                for f in range(2):
                    step(TT(fa[:, :, f, :], v[:, :, f, :], cos, ALU.mult))
                    step(TT(fb[:, :, f, :], v[:, :, f, :], sin, ALU.mult))
                step(TT(dst(0), fa[:, :, 0, :], fb[:, :, 1, :], ALU.subtract))
                return TT(dst(1), fa[:, :, 1, :], fb[:, :, 0, :], ALU.add)

            dve.wait_ge(sem("cossin_ready"), 1)
            for m, b in enumerate(item("qa")):
                q4 = qr[:, m, :].rearrange("p (i g f c) -> p g i f c", i=4, g=HG, f=2)
                v = b[:, :].rearrange("p (g i f c) -> p g i f c", g=HG, i=4, f=2)
                fa = rope_a[:, 0:512].rearrange("p (g i f c) -> p g i f c", g=HG, i=4, f=2)
                fb = rope_b[:, 0:512].rearrange("p (g i f c) -> p g i f c", g=HG, i=4, f=2)
                cos = cossin[:, m, 1, :].unsqueeze(1).to_broadcast([P, 8, 32])
                sin = cossin[:, m, 0, :].unsqueeze(1).to_broadcast([P, 8, 32])
                v8 = b[:, :].rearrange("p (h f c) -> p h f c", h=8, f=2)
                fa8 = rope_a[:, 0:512].rearrange("p (h f c) -> p h f c", h=8, f=2)
                fb8 = rope_b[:, 0:512].rearrange("p (h f c) -> p h f c", h=8, f=2)
                for f in range(2):
                    step(TT(fa8[:, :, f, :], v8[:, :, f, :], cos, ALU.mult))
                    step(TT(fb8[:, :, f, :], v8[:, :, f, :], sin, ALU.mult))
                for g in range(HG):
                    step(TT(q4[:, g, :, 0, :], fa[:, g, :, 0, :], fb[:, g, :, 1, :], ALU.subtract))
                    step(TT(q4[:, g, :, 1, :], fa[:, g, :, 1, :], fb[:, g, :, 0, :], ALU.add))
                dve.nop().then_inc(sem("qr_ready"), 1)
            dve.nop().then_inc(sem(f"pair{place['qa'][0] % 2}_free"), 1)
            for m, b in enumerate(item("kva")):
                k4 = kr[:, m, :].rearrange("p (g f c) -> p g f c", g=HG, f=2)
                step(rotate(b[:, 0:128], HG, m, lambda f: k4[:, :, f, :]))
                dve.nop().then_inc(sem("qr_ready"), 1)
                step(dve.tensor_copy(va[:, m, :], b[:, 128:256]))
                dve.nop().then_inc(sem("va_ready"), 1)
            dve.nop().then_inc(sem(f"pair{place['kva'][0] % 2}_free"), 1)

            dve.wait_ge(sem("silu_done"), 2)
            TS(qk[:, 4:8, :], qk[:, 4:8, :], DM ** -0.5, None, ALU.mult).then_inc(sem("k_scaled"), 1)
            dve.wait_ge(sem("cols_turned"), 1)
            step(dve.tensor_copy(st[:, 64:96], bank[7][:, 0:32]))
            step(dve.tensor_copy(st[:, 96:112], bank[7][:, 32:48]))
            for h2 in range(2):
                dve.wait_ge(sem("bm_spread"), h2 + 1)
                for h in range(2):
                    step(TT(wT[:, 2 * h2 + h, :, :],
                            bank[4 + h2][:, 256 * h:256 * h + 256].rearrange("p (m n) -> p m n", m=MT),
                            C("chunk_t").unsqueeze(1).to_broadcast([P, MT, P]), ALU.add))
            dve.nop().then_inc(sem("arg_ready"), 1)
            for m in range(MT):
                dve.wait_ge(sem("kc_turned"), m + 1)
                wk = st[:, 64 + 16 * m + 4:64 + 16 * m + 8]
                TT(kw[:, m, :, :], bank[4 + m][:, :].rearrange("p (h n) -> p h n", h=HM), bcast(wk, 128), ALU.mult)\
                    .then_inc(sem("kw_ready"), 1)
            dve.wait_ge(sem("wT_ready"), 8)
            for h2 in range(2):
                dve.wait_ge(sem("ms_done"), h2 + 1)
                TT(sw[:, 2 * h2:2 * h2 + 2, :, :],
                   bank[6 + h2][:, :].rearrange("p (h m n) -> p h m n", h=2, m=MT),
                   wT[:, 2 * h2:2 * h2 + 2, :, :], ALU.mult).then_inc(sem("sw_ready"), 1)
            for c in range(NCH - 1):
                for h2 in range(2):
                    dve.wait_ge(sem("kv_done"), 2 * c + h2 + 1)
                    for h in range(2 * h2, 2 * h2 + 2):
                        src = bank[4 + 2 * (c % 2) + h2][:, 129 * (h % 2):129 * (h % 2) + 129]
                        if c == 0:
                            ins = dve.tensor_copy(cstate[:, 1, h, :], src)
                        else:
                            ins = STT(cstate[:, c + 1, h, :], cstate[:, c, h, :],
                                      st[:, 96 + 4 * h + c:97 + 4 * h + c], src, ALU.mult, ALU.add)
                        step(ins)
                    dve.nop().then_inc(sem("state_ready"), 1)

            sink = bsm[:, 8:16]
            for m, sm in ((0, sm0), (1, sm1)):
                n = 128 if m == 0 else 256
                mask = C("attn")[:, 256 - n:256]
                hb = 4 if m == 0 else 2
                for b in range(HQ // hb):
                    dve.wait_ge(sem("s_done"), (0 if m == 0 else 2) + b + 1)
                    bk = bank[(4, 5)[b] if m == 0 else (6, 7, 4, 5)[b]]
                    TT(sm[:, hb * b:hb * b + hb, :], bk[:, :].rearrange("p (h n) -> p h n", h=hb),
                       mask.unsqueeze(1).to_broadcast([P, hb, n]), ALU.add).then_inc(sem("s_masked"), 1)
                dve.wait_ge(sem("s_masked"), 2 if m == 0 else 6)
                mx = st[:, 16 + 8 * m:24 + 8 * m]
                step(dve.tensor_reduce(mx, sm, AX, ALU.max))
                step(TT(mx, mx, sink, ALU.max))
                step(TT(st[:, 48 + 8 * m:56 + 8 * m], sink, mx, ALU.subtract))
                step(TS(mx, mx, -1.0, None, ALU.mult))
                dve.nop().then_inc(sem("smax_ready"), 1)
            modulation(0, 1)
            for m in range(MT):
                dve.wait_ge(sem("exp_ready"), 9 * m + 9)
                step(TT(st[:, 32 + 8 * m:40 + 8 * m], st[:, 32 + 8 * m:40 + 8 * m], st[:, 48 + 8 * m:56 + 8 * m],
                        ALU.add))
                step(dve.reciprocal(st[:, 32 + 8 * m:40 + 8 * m], st[:, 32 + 8 * m:40 + 8 * m]))
            modulation(0, 2)
            for m in range(MT):
                dve.wait_ge(sem("o_done"), m + 1)
                TT(ya[:, m, :].rearrange("p (h c) -> p h c", h=HQ), bank[6 + m][:, :].rearrange("p (h c) -> p h c", h=HQ),
                   bcast(st[:, 32 + 8 * m:40 + 8 * m], 64), ALU.mult)\
                    .then_inc(sem("ya_ready"), 1)
            for m in range(MT):
                for h2 in range(2):
                    dve.wait_ge(sem("inter_done"), 2 * m + h2 + 1)
                    dve.wait_ge(sem("intra_ready"), 2 * m + h2 + 1)
                    for h in range(2 * h2, 2 * h2 + 2):
                        ins = STT(intra[:, m, h, :], bank[6 + h2][:, 129 * (h % 2):129 * (h % 2) + 129],
                                  st[:, 64 + 16 * m + 8 + h:64 + 16 * m + 9 + h], intra[:, m, h, :],
                                  ALU.mult, ALU.add)
                        if h % 2:
                            ins.then_inc(sem("inter_used"), 1)
                        else:
                            step(ins)
                dve.wait_ge(sem("inter_used"), 2 * m + 2)
                den = st[:, 136 + 4 * m:140 + 4 * m]
                step(TS(den, intra[:, m, :, 128], -1.0, None, ALU.mult))
                step(TT(den, den, intra[:, m, :, 128], ALU.max))
                step(TT(den, den, st[:, 64 + 16 * m + 12:64 + 16 * m + 16], ALU.max))
                step(dve.reciprocal(den, den))
                step(TT(intra[:, m, :, 0:128], intra[:, m, :, 0:128], bcast(den, 128), ALU.mult))
                for h in range(HM):
                    step(dve.bn_stats(st[:, 144 + 6 * h:150 + 6 * h], intra[:, m, h, 0:128]))
                    step(dve.bn_aggr(st[:, 176 + 8 * m + 2 * h:178 + 8 * m + 2 * h], st[:, 144 + 6 * h:150 + 6 * h]))
            mv = st[:, 176:192].rearrange("p (q w) -> p q w", w=2)
            step(TS(st[:, 112:120], mv[:, :, 1], EPS, None, ALU.add))
            step(dve.reciprocal(st[:, 112:120], st[:, 112:120]))
            dve.nop().then_inc(sem("hvar_ready"), 1)
            dve.wait_ge(sem("hstd_ready"), 1)
            for m in range(MT):
                for h in range(HM):
                    step(TS(intra[:, m, h, 0:128], intra[:, m, h, 0:128], mv[:, 4 * m + h, 0:1],
                            st[:, 112 + 4 * m + h:113 + 4 * m + h], ALU.subtract, ALU.mult))
                TT(ym[:, m, :].rearrange("p (h n) -> p h n", h=HM), intra[:, m, :, 0:128],
                   osig[:, m, :].rearrange("p (h n) -> p h n", h=HM), ALU.mult).then_inc(sem("ym_ready"), 1)
            pair_wait("ada1_2")
            pair_wait("ada1_1")
            gains(1, v1T[:, v1["g_pre_ffn"][0]:v1["g_pre_ffn"][1]])
            for u in range(3):
                modulation(1, u)
            for u in range(3):
                pair_wait(f"ada2_{u}")
            gains(2, None)
            gains(3, None)
            dve.wait_ge(sem("gT_ready"), 4)
            for n in range(4):
                dve.wait_ge(sem(f"pair{place[f'g{n}'][0] % 2}_free"), place[f"g{n}"][0] // 2 + 1)
            for n in range(2):
                for h, b in enumerate(item(f"ba{n}")):
                    t = 4 * n + 2 * h
                    step(TT(merged[:, t:t + 2, :], b[:, :].rearrange("p (t n) -> p t n", t=2), gT[:, t:t + 2, :],
                            ALU.mult))
                dve.nop().then_inc(sem(f"pair{place[f'ba{n}'][0] % 2}_free"), 1)
            for n in range(2):
                for h, b in enumerate(item(f"bm{n}")):
                    t = 4 * n + 2 * h
                    step(TT(gT[:, 8 + t:10 + t, :], b[:, :].rearrange("p (t n) -> p t n", t=2),
                            gT[:, 8 + t:10 + t, :], ALU.mult))
                dve.nop().then_inc(sem(f"pair{place[f'bm{n}'][0] % 2}_free"), 1)
                TT(merged[:, 4 * n:4 * n + 4, :], merged[:, 4 * n:4 * n + 4, :], gT[:, 8 + 4 * n:12 + 4 * n, :],
                   ALU.add).then_inc(sem("merged_ready"), 1)

            def gate_row(n, name, i, c0, gpost):
                diag = xn[:, 0:1024].rearrange("p (j n) -> p j n", j=8)
                step(TT(diag, ident.unsqueeze(1).to_broadcast([P, 8, P]), bcast(modT[:, i, c0:c0 + 8], P), ALU.mult))
                dve.nop().then_inc(sem("diag_ready"), 1)
                dve.wait_ge(sem("gg_done"), n + 1)
                pair = place[name][0] % 2
                for h in range(2):
                    dst = gg[:, 512 * h:512 * h + 512]
                    src = bank[2 * pair + h][:, :]
                    step(TT(dst, src, gpost[:, 512 * h:512 * h + 512], ALU.mult) if gpost is not None
                         else dve.tensor_copy(dst, src))
                dve.nop().then_inc(sem(f"pair{pair}_free"), 1)
                dve.nop().then_inc(sem("gg_free"), 1)

            def post_rms(n, banks, free, squares):
                dve.wait_ge(sem("post_squares"), n + 1)
                sq = st[:, 120:124].rearrange("p (m h) -> p m h", m=MT)
                step(TT(st[:, 124:126], sq[:, :, 0], sq[:, :, 1], ALU.add))
                step(TS(st[:, 124:126], st[:, 124:126], 1.0 / D, EPS, ALU.mult, ALU.add))
                step(dve.reciprocal(st[:, 124:126], st[:, 124:126]))
                dve.nop().then_inc(sem("var_ready"), 1)
                dve.wait_ge(sem("std_ready"), squares)
                for m in range(MT):
                    for h in range(2):
                        step(STT(xn[:, 1024 + 512 * h:1536 + 512 * h], banks[m][h][:, :], st[:, 124 + m:125 + m],
                                 gg[:, 512 * h:512 * h + 512], ALU.mult, ALU.mult))
                    step(TT(xt[:, m, :], xt[:, m, :], xn[:, 1024:2048], ALU.add))
                    dve.nop().then_inc(sem("x_added"), 1)
                for name in free:
                    dve.nop().then_inc(sem(f"pair{place[name][0] % 2}_free"), 1)

            gate_row(0, "gg1", 0, 16, bc[:, 0, :])
            w0, w1 = item("wo0"), item("wo1")
            post_rms(0, [(w0[0], w1[0]), (w0[1], w1[1])], ("wo0", "wo1"), 2)
            rms_rows(1)
            dve.wait_ge(sem("std_ready"), 3)
            for m in range(MT):
                TS(xn[:, m * D:(m + 1) * D], xt[:, m, :], st[:, 4 + m:5 + m], None, ALU.mult)\
                    .then_inc(sem("xn_ready"), 1)
            evac_h(1)

            def feed_forward(letter, n):
                for j in range(FT // 2):
                    _, up = item(f"{letter}{j}")
                    dve.wait_ge(sem("sil_ready"), n * (FT // 2) + j + 1)
                    ins = TT(ffT[:, 2 * j:2 * j + 2, :], up[:, :].rearrange("p (t n) -> p t n", t=2),
                             sil[:, j % 2, :].rearrange("p (t n) -> p t n", t=2), ALU.mult)
                    ins.then_inc(sem("ff_ready"), 1)
                    dve.wait_ge(sem("ff_ready"), n * (FT // 2) + j + 1)
                    dve.nop().then_inc(sem(f"pair{place[f'{letter}{j}'][0] % 2}_free"), 1)

            feed_forward("ff", 0)
            gate_row(1, "gg2", 0, 40, bc[:, 1, :])
            dve.wait_ge(sem("blocks_done"), place["dn1"][2])
            post_rms(1, [(bank[4], bank[5]), (bank[6], bank[7])], (), 4)

            def layer_norm(n, g, b):
                for m in range(MT):
                    for h in range(2):
                        step(dve.bn_stats(st[:, 192 + 6 * h:198 + 6 * h], xt[:, m, 512 * h:512 * h + 512]))
                    step(dve.bn_aggr(st[:, 204 + 2 * m:206 + 2 * m], st[:, 192:204]))
                mv = st[:, 204:208].rearrange("p (m w) -> p m w", w=2)
                step(TS(st[:, 126:128], mv[:, :, 1], LN_EPS, None, ALU.add))
                step(dve.reciprocal(st[:, 126:128], st[:, 126:128]))
                dve.nop().then_inc(sem("var_ready"), 1)
                dve.wait_ge(sem("std_ready"), n)
                for m in range(MT):
                    step(TS(xt[:, m, :], xt[:, m, :], mv[:, m, 0:1], st[:, 126 + m:127 + m], ALU.subtract, ALU.mult))
                    step(TT(xt[:, m, :], xt[:, m, :], g, ALU.mult))
                    step(TT(xt[:, m, :], xt[:, m, :], b, ALU.add))
                    yield m

            dve.wait_ge(sem("spread2"), 32)
            for m in layer_norm(5, bc[:, 2, :], bc[:, 3, :]):
                dve.nop().then_inc(sem("emb_done"), 1)
            evac_h(2)

            dve.wait_ge(sem("ws_turned"), 1)
            step(TT(wsT, bank[4][:, :].rearrange("p (g n) -> p g n", g=4),
                    C("ws").unsqueeze(1).to_broadcast([P, 4, P]), ALU.mult))
            dve.nop().then_inc(sem("wsT_ready"), 1)
            item("pv")
            pair_wait("pv")
            dve.wait_ge(sem("gelu_done"), 2)
            for m in range(MT):
                step(dve.bn_stats(st[:, 192:198], gv[:, m, :]))
                step(dve.bn_aggr(st[:, 208 + 2 * m:210 + 2 * m], st[:, 192:198]))
            mv = st[:, 208:212].rearrange("p (m w) -> p m w", w=2)
            step(TS(st[:, 132:134], mv[:, :, 1], LN_EPS, None, ALU.add))
            step(dve.reciprocal(st[:, 132:134], st[:, 132:134]))
            dve.nop().then_inc(sem("gvar_ready"), 1)
            dve.wait_ge(sem("gstd_ready"), 1)
            for m in range(MT):
                step(TS(gv[:, m, :], gv[:, m, :], mv[:, m, 0:1], st[:, 132 + m:133 + m], ALU.subtract, ALU.mult))
                step(TT(gv[:, m, :], gv[:, m, :], bcs[:, 1, :], ALU.mult))
                step(TT(gv[:, m, :], gv[:, m, :], bcs[:, 2, :], ALU.add))
                dve.nop().then_inc(sem("gv_ready"), 1)
            pair_wait("pu")
            for m in range(MT):
                dve.wait_ge(sem("sg_done"), m + 1)
                for g in range(4):
                    c0 = v2["b_s_2"][0] + g
                    step(STT(gu[:, m, 128 * g:128 * g + 128], bank[4 + m][:, 128 * g:128 * g + 128],
                             v2T[:, c0:c0 + 1], gu[:, m, 128 * g:128 * g + 128], ALU.add, ALU.mult))
                dve.nop().then_inc(sem("ga_ready"), 1)
            for m in range(MT):
                dve.wait_ge(sem("ga_turned"), m + 1)
                step(dve.tensor_copy(cat[:, 0:4, m * P:(m + 1) * P],
                                     bank[6 + m][:, :].rearrange("p (i n) -> p i n", i=4)))
            dve.nop().then_inc(sem("cat_a_ready"), 1)
            def shift(t0, t1, rows_):
                for t in range(t0, t1):
                    now = praw[0:rows_, t, 1:257]
                    d = dtmp[0:rows_, t % 4, :]
                    mu = v2T[0:rows_, v2["mu_shift_2"][0] + t:v2["mu_shift_2"][0] + t + 1]
                    step(TT(d, praw[0:rows_, t, 0:256], now, ALU.subtract))
                    step(STT(pm[0:rows_, t, :], d, mu, now, ALU.mult, ALU.add))

            def raw_in(name):
                pair_wait(name)

            dve.wait_ge(sem("praw_ready"), 4)
            for name in ("r", "k", "v", "lora"):
                raw_in(name)
            shift(12, 14, P)
            shift(14, 15, 32)
            dve.nop().then_inc(sem("lora_mixed"), 1)
            shift(0, 12, P)

            def col(name, j):
                c0 = v2[name][0] + j
                return v2T[:, c0:c0 + 1]

            rT, kT2, vT = pm[:, 0:4, :], pm[:, 4:8, :], pm[:, 8:12, :]
            for j in range(4):
                step(TS(kk[:, j, :], kT2[:, j, :], col("k_k_2", j), None, ALU.mult))
            step(TT(dtmp, kk, kk, ALU.mult))
            dve.nop().then_inc(sem("kk_squared"), 1)
            dve.wait_ge(sem("lwa_ready"), 8)
            step(TS(lw, lw, -math.exp(-0.5), None, ALU.mult))
            dve.wait_ge(sem("pads2"), 4)
            f = lambda t: t.rearrange("p j n -> p (j n)")
            step(dve.tensor_tensor_scan(f(cum), reset, f(lw), 0.0, ALU.mult, ALU.add))
            dve.nop().then_inc(sem("cum_ready"), 1)
            step(TT(lw, cum, lw, ALU.subtract))
            dve.nop().then_inc(sem("cum_ready"), 1)
            dve.wait_ge(sem("kk_len"), 1)
            step(TS(nrm[0:8, :], nrm[0:8, :], 1e-12, None, ALU.max))
            step(dve.reciprocal(nrm[0:8, :], nrm[0:8, :]))
            dve.nop().then_inc(sem("kk_inv"), 1)
            for j in range(4):
                step(TS(dtmp[:, j, :], av[:, j, :], 1.0, col("k_a_2", j), ALU.subtract, ALU.mult))
                step(STT(kT2[:, j, :], dtmp[:, j, :], 1.0, kT2[:, j, :], ALU.add, ALU.mult))
            for h in range(2):
                dve.wait_ge(sem("kk_spread"), h + 1)
                step(TT(kk[:, 2 * h:2 * h + 2, :], kk[:, 2 * h:2 * h + 2, :],
                        bank[4 + h][:, :].rearrange("p (t n) -> p t n", t=2), ALU.mult))
            dve.wait_ge(sem("dec_ready"), 3)
            ch = lambda t: t.rearrange("p j (c n) -> p j c n", c=NCH)
            for j in range(4):
                step(TT(aT_rT[:, j, :, 1, :], ch(rT)[:, j], ch(dec1)[:, j], ALU.mult))
                step(STT(aT_rT[:, j, :, 0, :], ch(kk)[:, j], -1.0, ch(dec2)[:, j], ALU.mult, ALU.mult))
            step(TT(bT, kk, av, ALU.mult))
            step(TT(bT, bT, lw, ALU.mult))
            step(TT(kTt, kT2, lw, ALU.mult))
            step(dve.tensor_copy(st[:, 212:228].rearrange("p (j c) -> p j c", j=4), ch(dec1)[:, :, :, L - 1]))
            for j in range(4):
                step(STT(dtmp[:, j, :], rT[:, j, :], col("r_k_2", j), kT2[:, j, :], ALU.mult, ALU.mult))
            dve.nop().then_inc(sem("tilde_ready"), 1)
            for h in range(2):
                dve.wait_ge(sem("bonus_summed"), h + 1)
                step(TT(bonus[:, 2 * h:2 * h + 2, :], vT[:, 2 * h:2 * h + 2, :],
                        bank[6 + h][:, :].rearrange("p (t n) -> p t n", t=2), ALU.mult))
            dve.nop().then_inc(sem("bonus_ready"), 1)
            dve.wait_ge(sem("tok_ready"), 6)

            def quad(b, w):
                return b[:, :].rearrange("p (q w n) -> p q w n", w=w, n=L) if w > 1 else \
                    b[:, :].rearrange("p (q n) -> p q n", n=L)

            ar = C("ar").rearrange("p (w n) -> p w n", w=2)

            def masked(dst, src, mask_name, n):
                return TT(dst, src, C(mask_name).unsqueeze(1).to_broadcast([P, n, L]), ALU.mult)

            for n, dst in enumerate((gB, gK)):
                for b in range(4):
                    dve.wait_ge(sem("gram_done"), 4 * n + b + 1)
                    for w in range(2):
                        step(TT(dst[:, 4 * b:4 * b + 4, w, :], quad(bank[4 + b], 2)[:, :, w, :],
                                ar[:, w, :].unsqueeze(1).to_broadcast([P, 4, L]), ALU.mult))
                    dve.nop().then_inc(sem("gram_ready"), 1)
            for h in range(2):
                dve.wait_ge(sem("gram_done"), 9 + h)
                step(masked(nlow[:, 8 * h:8 * h + 8, :], quad(bank[4 + h], 1), "low", 8))
            eye = C("eye2").unsqueeze(1).to_broadcast([P, 16, L])
            S1, S1t, P2, P2t, P4, T2, T2t = inv
            step(masked(T2, nlow, "b8", 16))
            step(masked(T2t, gB[:, :, 0, :], "b8", 16))
            step(TT(S1, T2, eye, ALU.add))
            step(TT(S1t, T2t, eye, ALU.add))
            dve.nop().then_inc(sem("inv_ready"), 2)

            def collect(n, dst, add, mask=None):
                for h in range(2):
                    dve.wait_ge(sem("inv_done"), 2 * n + h + 1)
                    src = quad(bank[4 + 2 * (n % 2) + h], 1)
                    s = slice(8 * h, 8 * h + 8)
                    step(TT(dst[:, s, :], src, add[:, s, :], ALU.add) if add is not None
                         else dve.tensor_copy(dst[:, s, :], src))
                    dve.nop().then_inc(sem("inv_ready"), 1)

            collect(0, P2, None)
            collect(1, P2t, None)
            collect(2, T2, S1)
            collect(3, T2t, S1t)
            collect(4, P4, None)
            collect(5, S1, T2)
            collect(6, S1t, T2t)
            n = 7
            cur, curt, nxt, nxtt = S1, S1t, T2, T2t
            for lvl, name in enumerate(("o8", "o16", "o32")):
                step(masked(P4, gB[:, :, 0, :], name, 16))
                step(masked(P2t, nlow, name, 16))
                dve.nop().then_inc(sem("off_ready"), 1)
                collect(n, P2, None)
                collect(n + 1, nxtt, curt)
                n += 2
                if lvl < 2:
                    collect(n, P2, None)
                    collect(n + 1, nxt, cur)
                    n += 2
                cur, curt, nxt, nxtt = nxt, nxtt, cur, curt

            dl = st[:, 212:228].rearrange("p (j c) -> p j c", j=4)
            for c in range(NCH - 1):
                dve.wait_ge(sem("m_done"), c + 1)
                dve.wait_ge(sem("yc_done"), c + 1)
                step(TT(ms, bank[6][:, 0:256].rearrange("p (j n) -> p j n", j=4), ms, ALU.add))
                step(TT(ms, ms, bcast(dl[:, :, c], L), ALU.mult))
                dve.nop().then_inc(sem("m_ready"), 1)
            dve.wait_ge(sem("yc_ready"), NCH)
            for h in range(2):
                dve.wait_ge(sem("ymean_done"), h + 1)
                step(STT(f(yT)[:, 512 * h:512 * h + 512], bank[4 + h][:, :], -1.0 / L, f(yT)[:, 512 * h:512 * h + 512],
                         ALU.mult, ALU.add))
            step(TT(dtmp, yT, yT, ALU.mult))
            dve.nop().then_inc(sem("ysq_ready"), 1)
            dve.wait_ge(sem("yvar_done"), 1)
            step(TS(nrm[0:8, :], bank[6][0:8, 0:256], 1.0 / L, GN_EPS, ALU.mult, ALU.add))
            step(dve.reciprocal(nrm[0:8, :], nrm[0:8, :]))
            dve.nop().then_inc(sem("yvar_ready"), 1)
            for h in range(2):
                dve.wait_ge(sem("ystd_spread"), h + 1)
                step(TT(yT[:, 2 * h:2 * h + 2, :], yT[:, 2 * h:2 * h + 2, :],
                        bank[4 + h][:, :].rearrange("p (t n) -> p t n", t=2), ALU.mult))
            for j in range(4):
                step(TS(yT[:, j, :], yT[:, j, :], col("lnx_g_2", j), col("lnx_b_2", j), ALU.mult, ALU.add))
            step(TT(yT, yT, bonus, ALU.add))
            dve.wait_ge(sem("gm_ready"), 2)
            step(TT(yT, yT, gmT, ALU.mult))
            dve.nop().then_inc(sem("yb_ready"), 1)

            def post_ln(banks):
                for m in range(MT):
                    for h in range(2):
                        step(TT(xn[:, 1024 + 512 * h:1536 + 512 * h], banks[m][h][:, :],
                                gg[:, 512 * h:512 * h + 512], ALU.mult))
                    step(STT(xt[:, m, :], xt[:, m, :], ALPHA, xn[:, 1024:2048], ALU.mult, ALU.add))

            gate_row(2, "gg3", 1, 16, None)
            w0, w1 = item("wo2"), item("wo3")
            post_ln([(w0[0], w1[0]), (w0[1], w1[1])])
            for name in ("wo2", "wo3"):
                dve.nop().then_inc(sem(f"pair{place[name][0] % 2}_free"), 1)
            dve.wait_ge(sem("spread3"), 64)
            for m in layer_norm(6, bc[:, 0, :], bc[:, 1, :]):
                dve.nop().then_inc(sem("ln1_done"), 1)
            evac_h(3)
            feed_forward("gf", 1)
            gate_row(3, "gg4", 1, 40, None)
            dve.wait_ge(sem("blocks_done"), place["dn2"][2])
            post_ln([(bank[4], bank[5]), (bank[6], bank[7])])
            for m in layer_norm(7, bc[:, 2, :], bc[:, 3, :]):
                dve.nop().then_inc(sem("y_out"), 1)

        @block.tensor
        def _(pe):
            mm = nc.tensor.matmul
            tr = nc.tensor.transpose

            def start_item(name):
                pair, _, _ = place[name]
                if pair >= 2:
                    pe.wait_ge(sem(f"pair{pair % 2}_free"), pair // 2)
                return bank[2 * (pair % 2)], bank[2 * (pair % 2) + 1]

            def weights(b, nk, n):
                pe.wait_ge(sem(f"slot{b % RING}_in"), landed[b])
                return slot(b, nk, n)

            def ada(name):
                b0, _ = start_item(name)
                i = int(name[3]) - 1
                if i:
                    pe.wait_ge(sem("cs_ready"), 1)
                for n, b in enumerate(range(*place[name][1:])):
                    w = weights(b, 8, 512)
                    for t in range(4):
                        for k in range(8):
                            last = mm(b0[:, 4 * n + t:4 * n + t + 1], w[:, k, t * P:(t + 1) * P], cc[:, i, k:k + 1],
                                      start=(k == 0), stop=(k == 7))
                    last.then_inc(sem("blocks_done"), 1)

            def tokens_out(name, n, src=hT, extra=None, width=None):
                banks = start_item(name)
                w = weights(place[name][1], 8, width or n)
                if extra is not None:
                    for m in range(MT):
                        for k in range(8):
                            mm(bank[4][:, 8 * m:8 * m + 8], src[:, k, m * P:(m + 1) * P], w[:, k, extra:extra + 8],
                               start=(k == 0), stop=(k == 7))
                for m in range(MT):
                    for k in range(8):
                        last = mm(banks[m][:, 0:n], src[:, k, m * P:(m + 1) * P], w[:, k, 0:n],
                                  start=(k == 0), stop=(k == 7))
                last.then_inc(sem("blocks_done"), 1)

            def features_out(name, tiles, src=hT, nk=8, width=512):
                banks = start_item(name)
                w = weights(place[name][1], nk, width)
                for t, n in enumerate(tiles):
                    for k in range(nk):
                        last = mm(banks[t // 2][0:n, 256 * (t % 2):256 * (t % 2) + 256], w[:, k, t * P:t * P + n],
                                  src[:, k, :], start=(k == 0), stop=(k == nk - 1))
                last.then_inc(sem("blocks_done"), 1)

            def turn_h(src):
                for k in range(8):
                    for m in range(MT):
                        last = tr(bank[4 + k // 2][:, 256 * (k % 2) + P * m:256 * (k % 2) + P * m + P],
                                  src(m)[:, k * P:(k + 1) * P], ident)
                    if k % 2:
                        last.then_inc(sem("hx_turned"), 1)

            four = [P] * 4
            pe.wait_ge(sem("const_in"), 32)
            pe.wait_ge(sem("vec0_in"), 16 * len(ROWS1))
            tr(bank[4][:, 0:n1], vraw[0:n1, 0, :], ident[0:n1, 0:n1]).then_inc(sem("vec_turned"), 1)
            pe.wait_ge(sem("vec1_in"), 16 * (len(ROWS2) + 1))
            tr(bank[5][:, 0:n2], vraw[0:n2, 1, :], ident[0:n2, 0:n2]).then_inc(sem("vec_turned"), 1)
            pe.wait_ge(sem("xn_ready"), 2)
            turn_h(lambda m: xn[:, m * D:(m + 1) * D])
            pe.wait_ge(sem("c_in"), 32)
            ada("ada1_0")
            pe.wait_ge(sem("hT_ready"), 8)
            tokens_out("o_if", 512, extra=512, width=520)
            features_out("qm", four)
            features_out("km", four)
            pe.wait_ge(sem("if_ready"), 2)
            for w in range(2):
                for m in range(MT):
                    last = tr(bank[7][0:4, 256 * w + P * m:256 * w + P * m + P],
                              st[:, 240 + 8 * m + 4 * w:244 + 8 * m + 4 * w], ident)
            last.then_inc(sem("if_turned"), 1)
            tokens_out("vm", 512)
            tokens_out("qa", 512)
            tokens_out("kva", 256)
            pe.wait_ge(sem("rows_exp"), 4)
            for m in range(MT):
                for q, r in enumerate((2, 6, 7, 8)):
                    tr(bank[7][:, 16 * m + 4 * q:16 * m + 4 * q + 4], rows[0:4, r, m * P:(m + 1) * P], ident[0:4, 0:4])
            for h in range(HM):
                last = mm(bank[7][:, 32 + 4 * h:36 + 4 * h], csel[0:4, h * P:(h + 1) * P], rows[0:4, 4, 16:20],
                          start=True, stop=True)
            last.then_inc(sem("cols_turned"), 1)
            for h2 in range(2):
                for h in range(2):
                    last = mm(bank[4 + h2][:, 256 * h:256 * h + 256], csel[0:4, (2 * h2 + h) * P:(2 * h2 + h + 1) * P],
                              rows[0:4, 9, :], start=True, stop=True)
                last.then_inc(sem("bm_spread"), 1)
            features_out("g0", four)
            pe.wait_ge(sem("k_scaled"), 1)
            pe.wait_ge(sem("arg_ready"), 1)
            for m in range(MT):
                for h in range(HM):
                    last = tr(bank[4 + m][:, h * P:(h + 1) * P], qk[:, 4 + h, m * P:(m + 1) * P], ident)
                last.then_inc(sem("kc_turned"), 1)
            for h2 in range(2):
                for h in range(2):
                    for m in range(MT):
                        t = slice(m * P, (m + 1) * P)
                        last = mm(bank[6 + h2][:, 256 * h + P * m:256 * h + P * m + P], qk[:, 4 + 2 * h2 + h, t],
                                  qk[:, 2 * h2 + h, t], start=True, stop=True)
                last.then_inc(sem("ms_done"), 1)
            features_out("g1", four)
            pe.wait_ge(sem("kw_ready"), 2)
            pe.wait_ge(sem(f"pair{place['vm'][0] % 2}_free"), place["vm"][0] // 2 + 1)
            pe.wait_ge(sem("v_ready"), 1)
            pe.wait_ge(sem("pads"), 3)
            pe.wait_ge(sem("sw_ready"), 2)
            for c in range(NCH - 1):
                rows_ = slice(L * (c % 2), L * (c % 2) + L)
                for h2 in range(2):
                    if c == 2:
                        pe.wait_ge(sem("state_ready"), h2 + 1)
                    for h in range(2 * h2, 2 * h2 + 2):
                        last = mm(bank[4 + 2 * (c % 2) + h2][:, 129 * (h % 2):129 * (h % 2) + 129],
                                  kw[rows_, c // 2, h, :], vaug[rows_, c // 2, h, :], start=True, stop=True)
                    last.then_inc(sem("kv_done"), 1)
            features_out("g2", four)
            pe.wait_ge(sem("state_ready"), 6)
            for m in range(MT):
                pe.wait_ge(sem("qr_ready"), m + 1)
                for i in range(4):
                    last = tr(bank[4 + m][:, i * P:(i + 1) * P], qr[:, m, i * P:(i + 1) * P], ident)
                last.then_inc(sem("qr_turned"), 1)
            pe.wait_ge(sem("qr_ready"), 4)
            for m in range(MT):
                last = tr(bank[6][:, m * P:(m + 1) * P], kr[:, m, :], ident)
            last.then_inc(sem("qr_turned"), 1)
            pe.wait_ge(sem("qT_ready"), 3)

            def scores(m, h, b, at, n):
                g, i = h // 4, h % 4
                half = slice(64 * g, 64 * g + 64)
                return mm(b[:, at:at + n], qT[half, i, m * P:(m + 1) * P], kT[half, S - n if m else 0:S if m else n],
                          start=True, stop=True)

            for b in range(2):
                for h in range(4):
                    last = scores(0, 4 * b + h, bank[4 + b], 128 * h, 128)
                last.then_inc(sem("s_done"), 1)
            for b in range(4):
                if b >= 2:
                    pe.wait_ge(sem("s_masked"), b - 1)
                for h in range(2):
                    last = scores(1, 2 * b + h, bank[(6, 7, 4, 5)[b]], 256 * h, 256)
                last.then_inc(sem("s_done"), 1)
            features_out("g3", four)
            ada("ada1_1")
            for n in range(6):
                m = 0 if n < 2 else 1
                pe.wait_ge(sem("s_masked"), 6)
                pe.wait_ge(sem("exp_ready"), 9 * m + 9)
                if n >= 4:
                    pe.wait_ge(sem("pT_ready"), n - 3)
                for q in range(4):
                    if m == 0:
                        src = sm0[:, 4 * n + q, :]
                    else:
                        idx = 4 * (n - 2) + q
                        src = sm1[:, idx // 2, P * (idx % 2):P * (idx % 2) + P]
                    last = tr(bank[4 + n % 4][:, q * P:(q + 1) * P], src, ident)
                last.then_inc(sem("p_turned"), 1)
            ada("ada1_2")
            pe.wait_ge(sem("pT_ready"), 6)
            pe.wait_ge(sem("va_ready"), 2)
            for h in range(HQ):
                g = h // 4
                last = mm(bank[6][:, 64 * h:64 * h + 64], pT[:, h, :], va[:, 0, 64 * g:64 * g + 64],
                          start=True, stop=True)
            last.then_inc(sem("o_done"), 1)
            for h in range(HQ):
                g = h // 4
                for kb in range(2):
                    last = mm(bank[7][:, 64 * h:64 * h + 64], pT[:, 8 + 2 * h + kb, :], va[:, kb, 64 * g:64 * g + 64],
                              start=(kb == 0), stop=(kb == 1))
            last.then_inc(sem("o_done"), 1)
            for m in range(MT):
                for h2 in range(2):
                    if m:
                        pe.wait_ge(sem("intra_ready"), h2 + 1)
                    for h in range(2 * h2, 2 * h2 + 2):
                        last = mm(bank[4 + h2][:, 129 * (h % 2):129 * (h % 2) + 129], sw[:, h, m, :],
                                  vaug[:, m, h, :], start=True, stop=True)
                    last.then_inc(sem("intra_done"), 1)
                if m == 0:
                    pe.wait_ge(sem("ya_ready"), 2)
                for h2 in range(2):
                    if m:
                        pe.wait_ge(sem("inter_used"), h2 + 1)
                    for h in range(2 * h2, 2 * h2 + 2):
                        for half in range(2):
                            c = 2 * m + half
                            last = mm(bank[6 + h2][L * half:L * half + L, 129 * (h % 2):129 * (h % 2) + 129],
                                      qk[:, h, c * L:(c + 1) * L], cstate[:, c, h, :], start=True, stop=True)
                    last.then_inc(sem("inter_done"), 1)
            ada("ada2_0")
            pe.wait_ge(sem("intra_ready"), 4)
            for m in range(MT):
                for i in range(4):
                    last = tr(bank[4 + m][:, i * P:(i + 1) * P], ya[:, m, i * P:(i + 1) * P], ident)
                last.then_inc(sem("ya_turned"), 1)
            ada("ada2_1")
            pe.wait_ge(sem("inter_used"), 4)
            for m in range(MT):
                pe.wait_ge(sem("ym_ready"), m + 1)
                for i in range(4):
                    last = tr(bank[6 + m][:, i * P:(i + 1) * P], ym[:, m, i * P:(i + 1) * P], ident)
                last.then_inc(sem("ym_turned"), 1)
            ada("ada2_2")
            pe.wait_ge(sem("yaT_ready"), 2)
            features_out("ba0", four, yaT, 4)
            features_out("ba1", four, yaT, 4)
            pe.wait_ge(sem("ymT_ready"), 2)
            features_out("bm0", four, ymT, 4)
            features_out("bm1", four, ymT, 4)

            def gate_row(n, name):
                banks = start_item(name)
                pe.wait_ge(sem("diag_ready"), n + 1)
                for h in range(2):
                    last = mm(banks[h][:, :], C("ones"), xn[:, 512 * h:512 * h + 512], start=True, stop=True)
                last.then_inc(sem("gg_done"), 1)

            gate_row(0, "gg1")
            pe.wait_ge(sem("merged_ready"), 2)
            tokens_out("wo0", 512, merged)
            tokens_out("wo1", 512, merged)
            pe.wait_ge(sem("xn_ready"), 4)
            turn_h(lambda m: xn[:, m * D:(m + 1) * D])

            def feed_forward(letter, down, n):
                pe.wait_ge(sem("hT_ready"), 16 + 16 * n)
                for j in range(FT // 2):
                    features_out(f"{letter}{j}", four)
                gate_row(2 * n + 1, f"gg{2 * n + 2}")
                for i, b in enumerate(range(*place[down][1:])):
                    nk = min(4, FT - 4 * i)
                    w = weights(b, nk, 1024)
                    for k in range(nk):
                        t = 4 * i + k
                        pe.wait_ge(sem("ff_ready"), n * (FT // 2) + t // 2 + 1)
                        for m in range(MT):
                            for h in range(2):
                                last = mm(bank[4 + 2 * m + h][:, :], ffT[:, t, m * P:(m + 1) * P],
                                          w[:, k, 512 * h:512 * h + 512], start=(t == 0), stop=(t == FT - 1))
                    last.then_inc(sem("blocks_done"), 1)

            feed_forward("ff", "dn1", 0)
            pe.wait_ge(sem("emb_done"), 2)
            turn_h(lambda m: xt[:, m, :])
            pe.wait_ge(sem("hT_ready"), 24)
            tokens_out("pu", 512)
            tokens_out("pv", 512)
            pe.wait_ge(sem("ws_in"), 16)
            for g in range(4):
                last = tr(bank[4][:, g * P:(g + 1) * P], wsr[:, g, :], ident)
            last.then_inc(sem("ws_turned"), 1)
            features_out("r", four)
            features_out("k", four)
            features_out("v", four)
            features_out("lora", [P, P, 32], width=288)
            pe.wait_ge(sem("wsT_ready"), 1)
            for m in range(MT):
                pe.wait_ge(sem("gv_ready"), m + 1)
                for g in range(4):
                    last = mm(bank[4 + m][:, g * P:(g + 1) * P], wsT[:, g, :], gv[:, m, g * P:(g + 1) * P],
                              start=True, stop=True)
                last.then_inc(sem("sg_done"), 1)
            for m in range(MT):
                pe.wait_ge(sem("ga_ready"), m + 1)
                for i in range(4):
                    last = tr(bank[6 + m][:, i * P:(i + 1) * P], gu[:, m, i * P:(i + 1) * P], ident)
                last.then_inc(sem("ga_turned"), 1)
            pe.wait_ge(sem("cat_a_ready"), 1)
            pe.wait_ge(sem("lora_in"), 64)
            pe.wait_ge(sem("lora_act"), 3)
            for n, half in enumerate((slice(0, 64), slice(64, 128))):
                for j in range(4):
                    last = mm(bank[4 + 2 * n + j // 2][:, 256 * (j % 2):256 * (j % 2) + 256],
                              lup[half, j * P:(j + 1) * P], pm[half, 12, :], start=True, stop=True)
                    if j % 2:
                        last.then_inc(sem("lora_done"), 1)
            for j in range(4):
                if j % 2 == 0:
                    pe.wait_ge(sem("lwa_ready"), j + 2)
                o = bank[4 + j // 2][:, 256 * (j % 2):256 * (j % 2) + 256]
                mm(o, gu0[:, j * P:(j + 1) * P], pm[:, 13, :], start=True, stop=False)
                last = mm(o, gu1[0:32, j * P:(j + 1) * P], pm[0:32, 14, :], start=False, stop=True)
                if j % 2:
                    last.then_inc(sem("lora_done"), 1)
            heads = C("heads").rearrange("p (j n) -> p j n", j=4)

            def head_sums(src, dst, s):
                for j in range(4):
                    last = mm(dst, heads[:, j, :], src[:, j, :], start=(j == 0), stop=(j == 3))
                last.then_inc(s, 1)

            def head_spread(s):
                for j in range(4):
                    last = mm(bank[4 + j // 2][:, 256 * (j % 2):256 * (j % 2) + 256],
                              csel[0:8, 512 + j * P:512 + (j + 1) * P], nrm[0:8, :], start=True, stop=True)
                    if j % 2:
                        last.then_inc(s, 1)

            pe.wait_ge(sem("kk_squared"), 1)
            pe.wait_ge(sem("lwa_ready"), 8)
            head_sums(dtmp, bank[6][0:8, 0:256], sem("kk_summed"))
            pe.wait_ge(sem("kk_inv"), 1)
            pe.wait_ge(sem("gm_ready"), 2)
            head_spread(sem("kk_spread"))
            pe.wait_ge(sem("tilde_ready"), 1)
            for j in range(4):
                last = mm(bank[6 + j // 2][:, 256 * (j % 2):256 * (j % 2) + 256], C("pairs"), dtmp[:, j, :],
                          start=True, stop=True)
                if j % 2:
                    last.then_inc(sem("bonus_summed"), 1)
            eye2 = C("eye2")
            half = (slice(0, 64), slice(64, 128))

            def each(q0, q1):
                for q in range(q0, q1):
                    for g in range(2):
                        yield q, q // 4, q % 4, half[g]

            pe.wait_ge(sem("bonus_ready"), 1)
            for n, src in enumerate((bT, kTt, pm[:, 8:12, :])):
                for h in range(2):
                    i = 2 * n + h
                    if i >= 4:
                        pe.wait_ge(sem("tok_ready"), i - 3)
                    for q, c, j, r in each(8 * h, 8 * h + 8):
                        last = mm(bank[4 + i % 4][r, L * (q % 8):L * (q % 8) + L], src[r, j, c * L:(c + 1) * L],
                                  eye2[r, :], start=True, stop=True)
                    last.then_inc(sem("tok_turned"), 1)
            pe.wait_ge(sem("tok_ready"), 6)
            for n, src in enumerate((bT, kTt)):
                for b in range(4):
                    if n:
                        pe.wait_ge(sem("gram_ready"), b + 1)
                    for q, c, j, r in each(4 * b, 4 * b + 4):
                        last = mm(bank[4 + b][r, 2 * L * (q % 4):2 * L * (q % 4) + 2 * L],
                                  src[r, j, c * L:(c + 1) * L],
                                  aT_rT[r, j, c, :, :].rearrange("p w n -> p (w n)"), start=True, stop=True)
                    last.then_inc(sem("gram_done"), 1)
            for h in range(2):
                pe.wait_ge(sem("gram_ready"), 5 + h)
                for q, c, j, r in each(8 * h, 8 * h + 8):
                    last = mm(bank[4 + h][r, L * (q % 8):L * (q % 8) + L], aT_rT[r, j, c, 0, :],
                              bT[r, j, c * L:(c + 1) * L], start=True, stop=True)
                last.then_inc(sem("gram_done"), 1)
            S1, S1t, P2, P2t, P4, T2, T2t = inv

            def product(n, lhsT, rhs, ready):
                for h in range(2):
                    pe.wait_ge(sem("inv_ready"), ready + h)
                    for q, c, j, r in each(8 * h, 8 * h + 8):
                        last = mm(bank[4 + 2 * (n % 2) + h][r, L * (q % 8):L * (q % 8) + L], lhsT[r, q, :],
                                  rhs[r, q, :], start=True, stop=True)
                    last.then_inc(sem("inv_done"), 1)

            done = lambda n: 2 + 2 * n + 1
            pe.wait_ge(sem("gram_ready"), 8)
            product(0, T2t, T2, 1)
            product(1, T2, T2t, 1)
            product(2, S1t, P2, done(0))
            product(3, P2, S1t, done(1))
            product(4, P2t, P2, done(2))
            product(5, T2t, P4, done(4))
            product(6, P4, T2t, done(4))
            n = 7
            cur, curt, nxt, nxtt = S1, S1t, T2, T2t
            for lvl in range(3):
                pe.wait_ge(sem("off_ready"), lvl + 1)
                product(n, P2t, curt, done(n - 1))
                product(n + 1, cur, P2, done(n))
                n += 2
                if lvl < 2:
                    product(n, P4, cur, done(n - 1))
                    product(n + 1, curt, P2, done(n))
                    n += 2
                cur, curt, nxt, nxtt = nxt, nxtt, cur, curt
            solve = curt
            pe.wait_ge(sem("inv_ready"), done(n - 1) + 1)
            pe.wait_ge(sem("pads2"), 4)
            for c in range(NCH):
                if c:
                    pe.wait_ge(sem("m_ready"), c)
                for q, _, j, r in each(4 * c, 4 * c + 4):
                    mm(bank[4][r, L * j:L * j + L], aT_rT[r, j, c, 0, :], ms[r, j, :], start=True, stop=False)
                    last = mm(bank[4][r, L * j:L * j + L], gK[r, q, 0, :], vtok[r, q, :], start=False, stop=True)
                last.then_inc(sem("x_done"), 1)
                pe.wait_ge(sem("x_ready"), c + 1)
                for q, _, j, r in each(4 * c, 4 * c + 4):
                    last = mm(bank[5][r, L * j:L * j + L], solve[r, q, :], xs[r, j, :], start=True, stop=True)
                last.then_inc(sem("u_done"), 1)
                pe.wait_ge(sem("u_ready"), c + 1)
                if c < NCH - 1:
                    for q, _, j, r in each(4 * c, 4 * c + 4):
                        mm(bank[6][r, L * j:L * j + L], btok[r, q, :], us[r, j, :], start=True, stop=False)
                        last = mm(bank[6][r, L * j:L * j + L], ktok[r, q, :], vtok[r, q, :], start=False, stop=True)
                    last.then_inc(sem("m_done"), 1)
                if c:
                    pe.wait_ge(sem("yc_ready"), c)
                for q, _, j, r in each(4 * c, 4 * c + 4):
                    o = bank[7][r, L * j:L * j + L]
                    mm(o, ms[r, j, :], aT_rT[r, j, c, 1, :], start=True, stop=False)
                    mm(o, us[r, j, :], gB[r, q, 1, :], start=False, stop=False)
                    last = mm(o, vtok[r, q, :], gK[r, q, 1, :], start=False, stop=True)
                last.then_inc(sem("yc_done"), 1)
            pe.wait_ge(sem("yc_ready"), NCH)
            for j in range(4):
                last = mm(bank[4 + j // 2][:, 256 * (j % 2):256 * (j % 2) + 256], C("pairs"), yT[:, j, :],
                          start=True, stop=True)
                if j % 2:
                    last.then_inc(sem("ymean_done"), 1)
            pe.wait_ge(sem("ysq_ready"), 1)
            head_sums(dtmp, bank[6][0:8, 0:256], sem("yvar_done"))
            pe.wait_ge(sem("ystd_ready"), 1)
            head_spread(sem("ystd_spread"))
            gate_row(2, "gg3")
            pe.wait_ge(sem("yb_ready"), 1)
            tokens_out("wo2", 512, cat)
            tokens_out("wo3", 512, cat)
            pe.wait_ge(sem("ln1_done"), 2)
            turn_h(lambda m: xt[:, m, :])
            feed_forward("gf", "dn2", 1)


_INS = ["x", "c", "positions", "w_ada", "b_ada", "g_pre_mix", "g_post_mix", "w_in", "b_if", "conv_w", "conv_b",
        "attn_sinks", "mlstm_norm_w", "w_branch_attn", "w_branch_mlstm", "w_out", "g_pre_ffn", "g_post_ffn",
        "w_ffn_gate", "w_ffn_up", "w_ffn_down", "c_2", "emb_ln_g_2", "emb_ln_b_2", "w_ada_2", "b_ada_2", "w_in_2",
        "mu_shift_2", "sg_ln_g_2", "sg_ln_b_2", "w_s_2", "b_s_2", "w0_2", "w_up_2", "a0_2", "a_up_2", "g_up_2",
        "k_k_2", "k_a_2", "r_k_2", "lnx_g_2", "lnx_b_2", "w_out_2", "ln1_g_2", "ln1_b_2", "w_ffn_in_2",
        "w_ffn_out_2", "ln2_g_2", "ln2_b_2"]


def kernel(**inputs):
    import numpy as _np
    import concourse.bacc as _bacc
    from concourse import mybir as _mybir
    from concourse.bass_utils import run_bass_kernel_spmd as _run

    nc = _bacc.Bacc("TRN2", target_bir_lowering=False, num_devices=1)
    arrays, args = {}, {}
    const, selector = constants()
    for name in _INS + ["const", "selector"]:
        a = {"const": const, "selector": selector}[name] if name in ("const", "selector") else \
            _np.ascontiguousarray(inputs[name])
        arrays[f"in_{name}"] = a
        args[name] = nc.dram_tensor(f"in_{name}", a.shape, _mybir.dt.from_np(a.dtype), kind="ExternalInput").ap()
    out = nc.dram_tensor("out_dram", (1, S, D), _mybir.dt.float32, kind="ExternalOutput").ap()
    build(nc, args, out)
    r = _run(nc, [arrays], core_ids=[0])
    return r.results[0]["out_dram"]
```

```python
import math
import numpy as np
import concourse.bass as bass
from concourse import mybir
from contextlib import ExitStack

S = 256
D = 1024
P = 128
MT = S // P
KT = D // P
FF = 2816
FT = FF // P
HQ, HG, DH = 8, 2, 64
HM, DM = 4, 128
L = 64
NCH = S // L
SLOT = 4 * 520
RAW = 3
HL = 2
NEG = -1e30
EPS = 1e-6
LN_EPS = 1e-5
GN_EPS = 64e-5
ALPHA = 2 ** 0.25
TWO_PI_1 = 6.28125
TWO_PI_2 = float(np.float32(np.frombuffer(np.uint32(
    np.float32(2 * math.pi - TWO_PI_1).view(np.uint32) & 0xFFFFF000).tobytes(), np.float32)[0]))
TWO_PI_3 = float(np.float32(2 * math.pi - TWO_PI_1 - TWO_PI_2))
ROUND = 12582912.0
SIN_MAX = 3.1415925

CONST = {}
_at = 0
for _name, _n in (("ident", 128), ("attn", 256), ("chunk_t", 128), ("ws", 128), ("ar", 128), ("low", 64),
                  ("b8", 64), ("o8", 64), ("o16", 64), ("o32", 64), ("eye2", 64), ("pairs", 128),
                  ("heads", 32), ("ones", 128), ("freq", 32), ("b8low", 64)):
    CONST[_name] = (_at, _at + _n)
    _at += _n
CONST_N = _at


def constants():
    p = np.arange(P)[:, None]
    f = np.arange(P)[None, :]
    c = np.zeros((P, CONST_N), np.float32)

    def put(name, v):
        a, b = CONST[name]
        c[:, a:b] = v

    q, k = np.arange(P)[:, None], np.arange(2 * P)[None, :]
    rel = k - P
    h = p % L
    g = np.arange(L)[None, :]
    same = lambda n: (h // n == g // n)
    put("ident", np.eye(P))
    put("attn", np.where((rel <= q) & (q - rel < P), 0.0, NEG))
    put("chunk_t", np.where((p // L == f // L) & (p <= f), 0.0, NEG))
    put("ws", p <= f)
    put("ar", np.concatenate([h < g, h <= g], axis=1))
    put("low", g < h)
    put("b8", same(8))
    put("b8low", same(8) & (g < h))
    put("o8", same(16) & ~same(8))
    put("o16", same(32) & ~same(16))
    put("o32", ~same(32))
    put("eye2", h == g)
    put("pairs", p // L == f // L)
    heads = np.zeros((P, 4, 8))
    for j in range(4):
        heads[:L, j, 2 * j] = 1
        heads[L:, j, 2 * j + 1] = 1
    put("heads", heads.reshape(P, 32))
    put("ones", 1.0)
    put("freq", np.float32(10000.0) ** (np.float32(-2.0) * np.arange(32, dtype=np.float32) / np.float32(64)))
    return c


ROWS1 = (("g_pre_mix", 8), ("g_pre_ffn", 8), ("conv_w", 32), ("conv_b", 8))
ROWS2 = (("mu_shift_2", 15), ("w0_2", 4), ("a0_2", 4), ("k_k_2", 4), ("k_a_2", 4),
         ("r_k_2", 4), ("lnx_g_2", 4), ("lnx_b_2", 4), ("b_s_2", 4))


def first_rows(rows):
    at, out = 0, {}
    for name, n in rows:
        out[name] = (at, at + n)
        at += n
    return out, at


def stream():
    head = ["c0", "c1", "c2", "c3", "o_if", "qm", "km", "c4", "vm", "c5", "qa", "c6", "kva", "c7", "g0", "c8", "g1",
            "c9", "g2", "g3", "ba0", "ba1", "bm0", "bm1", "wo0", "wo1"]
    first = [x for j in range(FT // 2) for x in ([f"ff{j}"] + ([f"c{9 + j}"] if 1 <= j <= 10 else []))]
    middle = ["dn1", "pu", "pv", "r", "k", "v", "lora", "c20", "c21", "wo2", "wo3"]
    second = [x for j in range(FT // 2) for x in ([f"gf{j}"] + ([f"c{18 + j}"] if j in (4, 5) else []))]
    count = lambda n: {"b": 1, "d": 11}.get(n[0], 1 if n == "kva" else 2)
    return [(n, count(n)) for n in head + first + middle + second + ["dn2"]]


PIECES = [(0, 512 * i) for i in (0, 1, 2, 3, 6, 7, 8, 9, 4, 5, 10, 11)] + \
         [(1, 512 * i) for i in (0, 1, 2, 3, 6, 7, 8, 9, 4, 5, 10, 11)]
GATES = (8, 9, 10, 11, 20, 21, 22, 23)


ITEMS = stream()


def build(nc, A, out):
    fp = mybir.dt.float32
    ALU = mybir.AluOpType
    ACT = mybir.ActivationFunctionType
    AX = mybir.AxisListType.X
    ctx = ExitStack()
    with ctx:
        sems = {}

        def sem(name):
            if name not in sems:
                sems[name] = ctx.enter_context(nc.semaphore(name))
            return sems[name]

        def sb(name, shape):
            return ctx.enter_context(nc.sbuf_tensor(name, shape, fp))

        fr = mybir.dt.float32r

        ARENA = 20496
        arena_at = -(-nc.sbuf_base // 32) * 32
        arena = sb("arena", [P, ARENA])
        hreg = sb("hreg", [P, 4096])

        def rounded(name, at, shape):
            return nc.alloc_sbuf_tensor_at(name, [P] + shape, fr, offset=arena_at + 4 * at)

        hh = rounded("hh", ARENA, [KT, S])
        hl = rounded("hl", ARENA + 2048, [KT, S])
        raw = sb("raw", [P, RAW, SLOT])
        whi = ctx.enter_context(nc.sbuf_tensor("whi", [P, HL, SLOT], fr))
        wlo = ctx.enter_context(nc.sbuf_tensor("wlo", [P, HL, SLOT], fr))
        acc = sb("acc", [P, 2, 512])
        xt = sb("xt", [P, MT, D])
        xn = sb("xn", [P, MT * D])
        bc = sb("bc", [P, 4, D])
        bcs = sb("bcs", [P, 3, 512])
        bsm = sb("bsm", [P, 16])
        gg = sb("gg", [P, D])
        cst = sb("cst", [P, CONST_N])
        vraw = hreg[:, 0:256].rearrange("p (i n) -> p i n", i=2)
        v1, n1 = first_rows(ROWS1)
        v2, n2 = first_rows(ROWS2)
        v1T = sb("v1T", [P, n1])
        v2T = sb("v2T", [P, n2])
        modT = sb("modT", [P, 2, 48])
        gain = sb("gain", [P, 4, 8])
        cc = sb("cc", [P, 2, 8])
        st = sb("st", [P, 256])
        posi = ctx.enter_context(nc.sbuf_tensor("posi", [P, MT], mybir.dt.int32))

        def C(name):
            a, b = CONST[name]
            return cst[:, a:b]

        ident = C("ident")

        def region(at, n):
            assert at + n <= ARENA, (at, n)
            return arena[:, at:at + n]

        pos = [0]

        def take(n):
            pos[0] += n
            return region(pos[0] - n, n)

        conv_in = take(8 * 259).rearrange("p (t n) -> p t n", t=8)
        rope_a = take(640)
        rope_b = take(640)
        pT = region(0, 24 * 128).rearrange("p (t n) -> p t n", t=24)
        qk = take(8 * S).rearrange("p (t n) -> p t n", t=8)
        qr = take(MT * 512).rearrange("p (m n) -> p m n", m=MT)
        ya = qr
        kr = take(MT * 128).rearrange("p (m n) -> p m n", m=MT)
        va = take(MT * 128).rearrange("p (m n) -> p m n", m=MT)
        qT = take(4 * S).rearrange("p (i n) -> p i n", i=4)
        yah, yal = rounded("yah", ARENA, [4, S]), rounded("yal", ARENA + 1024, [4, S])
        ymh, yml = rounded("ymh", ARENA + 2048, [4, S]), rounded("yml", ARENA + 3072, [4, S])
        kT = take(S)
        sm0 = take(8 * 128).rearrange("p (h n) -> p h n", h=8)
        sm1 = xn[:, :].rearrange("p (h n) -> p h n", h=8)
        vaug = take(MT * HM * 129).rearrange("p (m h n) -> p m h n", m=MT, h=HM)
        osig = take(MT * 512).rearrange("p (m n) -> p m n", m=MT)
        ym = osig
        resets = gg[:, 0:512].rearrange("p (r n) -> p r n", r=2)
        rows = xn[:, :].rearrange("p (r n) -> p r n", r=8)
        wT = bc[:, 2, :].rearrange("p (h m n) -> p h m n", h=HM, m=MT)
        sw = bc[:, 3, :].rearrange("p (h m n) -> p h m n", h=HM, m=MT)
        kw = take(MT * 512).rearrange("p (m h n) -> p m h n", m=MT, h=HM)
        cstate = take(NCH * HM * 129).rearrange("p (c h n) -> p c h n", c=NCH, h=HM)
        merged = (rounded("mgh", 0, [KT, S]), rounded("mgl", 2048, [KT, S]))
        intra = take(MT * HM * 129).rearrange("p (m h n) -> p m h n", m=MT, h=HM)
        gT = take(16 * S).rearrange("p (t n) -> p t n", t=16)
        rsc = gg[:, 512:768].rearrange("p (w m f c) -> p w m f c", w=2, m=MT, f=2)
        cossin = gg[:, 768:896].rearrange("p (m f c) -> p m f c", m=MT, f=2)
        ffh, ffl = rounded("ffh", 0, [FT, S]), rounded("ffl", FT * S, [FT, S])
        sil = region(2 * FT * S, 2 * 512).rearrange("p (b n) -> p b n", b=2)
        ffp = region(2 * FT * S + 1024, 2 * 512).rearrange("p (b n) -> p b n", b=2)
        hx = region(ARENA - 2048, 2048).rearrange("p (t n) -> p t n", t=KT)
        pos[0] = 0
        praw = take(15 * 257).rearrange("p (t n) -> p t n", t=15)
        aT_rT = region(0, 2048).rearrange("p (j c w n) -> p j c w n", j=4, c=NCH, w=2)
        bT = region(2048, 1024).rearrange("p (j n) -> p j n", j=4)
        pm = take(15 * S).rearrange("p (t n) -> p t n", t=15)
        t_at = pos[0]
        tmp = [take(1024).rearrange("p (j n) -> p j n", j=4) for _ in range(7)]
        kk, av, lw, cum, dec1, dec2, dtmp = tmp
        inv = [t.rearrange("p j n -> p (j n)").rearrange("p (q n) -> p q n", q=16) for t in tmp]
        kTt = take(1024).rearrange("p (j n) -> p j n", j=4)
        vtok = take(1024).rearrange("p (q n) -> p q n", q=16)
        gB = take(2048).rearrange("p (q w n) -> p q w n", q=16, w=2)
        gK = xn[:, :].rearrange("p (q w n) -> p q w n", q=16, w=2)
        xs = bc[:, 2, 512:768].rearrange("p (j n) -> p j n", j=4)
        us = bc[:, 2, 768:1024].rearrange("p (j n) -> p j n", j=4)
        ms = take(256).rearrange("p (j n) -> p j n", j=4)
        cat = (hh, hl)
        yT = take(1024).rearrange("p (j n) -> p j n", j=4)
        reset = gg[:, :]
        nrm = take(256)
        btok = hreg[:, 1024:2048].rearrange("p (q n) -> p q n", q=16)
        ktok = hreg[:, 3072:4096].rearrange("p (q n) -> p q n", q=16)
        bonus = pm[:, 4:8, :]
        lup = bc[:, 0, 0:512]
        gu0 = bc[:, 0, 512:1024]
        gu1 = bc[:, 1, 0:512]
        wsr = bc[:, 1, 512:1024].rearrange("p (g n) -> p g n", g=4)
        wsT = bc[:, 2, 0:512].rearrange("p (g n) -> p g n", g=4)
        gmT = bc[:, 3, :].rearrange("p (j n) -> p j n", j=4)
        gv = xn[:, 0:1024].rearrange("p (m n) -> p m n", m=MT)
        gu = xn[:, 1024:2048].rearrange("p (m n) -> p m n", m=MT)

        bank = [ctx.enter_context(nc.psum_tensor(f"bank{i}", [P, 512], fp)) for i in range(8)]

        def wsrc(w, r0, nk, c0, n):
            return w[0, r0:r0 + nk * P, c0:c0 + n].rearrange("(k p) n -> p k n", p=P)

        def cut(buf, i, nk, n):
            return buf[:, i, 0:nk * n].rearrange("p (k n) -> p k n", k=nk)

        IN1 = {"o_if": (2304, 520), "qm": (768, 512), "km": (1280, 512), "vm": (1792, 512), "qa": (0, 512),
               "kva": (512, 256), "g0": (2824, 512), "g1": (3336, 512), "g2": (3848, 512), "g3": (4360, 512)}
        IN2 = {"pu": (0, 512), "pv": (512, 512), "r": (1024, 512), "k": (1536, 512), "v": (2048, 512),
               "lora": (2560, 288)}

        def sources(name):
            if name in IN1 or name in IN2:
                w, (c0, n) = (A["w_in"], IN1[name]) if name in IN1 else (A["w_in_2"], IN2[name])
                nk = 8 if name == "kva" else 4
                return [(nk, n, [(wsrc(w, P * k, nk, c0, n), 0, n)]) for k in range(0, 8, nk)]
            if name[0] == "c":
                i, c0 = PIECES[int(name[1:])]
                w = (A["w_ada"], A["w_ada_2"])[i][0, :, c0:c0 + 512].rearrange("(p k) n -> p k n", k=8)
                return [(4, 512, [(w[:, k:k + 4, :], 0, 512)]) for k in (0, 4)]
            if name[0] == "b":
                w = A["w_branch_attn"] if name[1] == "a" else A["w_branch_mlstm"]
                return [(4, 512, [(wsrc(w, 0, 4, 512 * int(name[2]), 512), 0, 512)])]
            if name[:2] == "wo":
                n = int(name[2])
                w = (A["w_out"], A["w_out_2"])[n // 2]
                return [(4, 512, [(wsrc(w, P * k, 4, 512 * (n % 2), 512), 0, 512)]) for k in (0, 4)]
            if name[:2] == "ff":
                c0 = 256 * int(name[2:])
                return [(4, 512, [(wsrc(A["w_ffn_gate"], P * k, 4, c0, 256), 0, 256),
                                  (wsrc(A["w_ffn_up"], P * k, 4, c0, 256), 256, 512)]) for k in (0, 4)]
            if name[:2] == "gf":
                c0 = 256 * int(name[2:])
                return [(4, 512, [(wsrc(A["w_ffn_in_2"], P * k, 4, c0, 256), 0, 256),
                                  (wsrc(A["w_ffn_in_2"], P * k, 4, FF + c0, 256), 256, 512)]) for k in (0, 4)]
            w = A["w_ffn_down"] if name == "dn1" else A["w_ffn_out_2"]
            return [(2, 1024, [(wsrc(w, P * k, 2, 0, 1024), 0, 1024)]) for k in range(0, FT, 2)]

        place, order, split_n, pairs = {}, [], 0, 0
        total = [0] * RAW
        for name, n in ITEMS:
            pair = None
            if name[0] != "d":
                pair = pairs
                pairs += 1
            blocks = sources(name)
            assert len(blocks) == n, name
            first = split_n
            for i, (nk, width, parts) in enumerate(blocks):
                b = len(order)
                total[b % RAW] += 16 * len(parts)
                split = None
                if name[0] != "c":
                    split = split_n
                    split_n += 1
                order.append((name, i, nk, width, parts, total[b % RAW], split))
            place[name] = (pair, first, split_n)
        at_block = {}
        for b, o in enumerate(order):
            at_block.setdefault(o[0], []).append(b)

        block = ctx.enter_context(nc.Block())

        @block.sync
        def _(sp):
            sp.dma_start(xt[:, :, :], A["x"][0].rearrange("(m p) n -> p m n", p=P)).then_inc(sem("x_in"), 16)
            for b, (_, _, nk, width, parts, _, _) in enumerate(order):
                if b >= RAW:
                    sp.wait_ge(sem("block_ready"), b - RAW + 1)
                for src, a, z in parts:
                    sp.dma_start(cut(raw, b % RAW, nk, width)[:, :, a:z], src).then_inc(sem(f"raw{b % RAW}_in"), 16)
            for m in range(MT):
                sp.wait_ge(sem("y_out"), m + 1)
                sp.dma_start(out[0, m * P:(m + 1) * P, :], xt[:, m, :]).then_inc(sem("out_stored"), 16)
            sp.wait_ge(sem("out_stored"), 16 * MT)

        @block.gpsimd
        def _(pool):
            pool.memset(conv_in[:, :, 0:3], 0.0).then_inc(sem("pads"), 1)
            pool.memset(vaug[:, :, :, 128:129], 1.0).then_inc(sem("pads"), 1)
            pool.memset(cstate[:, 0, :, :], 0.0).then_inc(sem("pads"), 1)
            pool.memset(resets[0:4, 0, :], 1.0).then_inc(sem("pads"), 1)
            pool.memset(resets[0:4, 1, :], 0.0).then_inc(sem("pads"), 1)
            pool.wait_ge(sem("pads"), 5)
            pool.memset(resets[0:4, 0, :].rearrange("p (c n) -> p c n", c=NCH)[:, :, 0:1], 0.0).then_inc(sem("pads"), 1)
            pool.memset(resets[0:4, 1, :].rearrange("p (c n) -> p c n", c=NCH)[:, :, 0:1], NEG).then_inc(sem("pads"), 1)

            def start_piece(a):
                i, c0 = PIECES[a]
                if a >= 2:
                    pool.wait_ge(sem("piece_done"), a - 1)
                pool.memset(acc[:, a % 2, :], 0.0).then_inc(sem("acc_zero"), 1)
                pool.wait_ge(sem("acc_zero"), a + 1)
                pool.dma_start(acc[0:1, a % 2, :], (A["b_ada"], A["b_ada_2"])[i][0:1, c0:c0 + 512])\
                    .then_inc(sem(f"acc{a % 2}_started"), 16)

            def spread(dst, src, s):
                pool.dma_start(dst, src.partition_broadcast(P)).then_inc(s, 16)

            for a in range(2):
                start_piece(a)
            spread(bsm[:, 0:8], A["b_if"][0], sem("spread1"))
            spread(bsm[:, 8:16], A["attn_sinks"][0], sem("spread1"))
            spread(bcs[:, 0, :], A["mlstm_norm_w"][0], sem("spread1"))
            spread(bcs[:, 1, :], A["sg_ln_g_2"][0], sem("spread1"))
            spread(bcs[:, 2, :], A["sg_ln_b_2"][0], sem("spread1"))
            spread(bc[:, 0, :], A["g_post_mix"][0], sem("spread1"))
            spread(bc[:, 1, :], A["g_post_ffn"][0], sem("spread1"))
            for a in range(2, 10):
                start_piece(a)
            pool.wait_ge(sem("h_ready"), 4)
            spread(bc[:, 2, :], A["emb_ln_g_2"], sem("spread2"))
            spread(bc[:, 3, :], A["emb_ln_b_2"], sem("spread2"))
            for a in range(10, 22):
                start_piece(a)
            pool.wait_ge(sem("emb_done"), 2)
            pool.dma_start(lup[0:64, :], A["w_up_2"][0]).then_inc(sem("lora_in"), 16)
            pool.dma_start(lup[64:128, :], A["a_up_2"][0]).then_inc(sem("lora_in"), 16)
            pool.dma_start(gu0, A["g_up_2"][0, 0:128, :]).then_inc(sem("lora_in"), 16)
            pool.dma_start(gu1[96:128, :], A["g_up_2"][0, 128:160, :]).then_inc(sem("lora_in"), 16)
            pool.dma_start(wsr, A["w_s_2"][0].rearrange("g t s -> t g s")).then_inc(sem("ws_in"), 16)
            pool.memset(praw[:, :, 0:1], 0.0).then_inc(sem("pads2"), 1)
            pool.wait_ge(sem("h_ready"), 6)
            pool.memset(ms, 0.0).then_inc(sem("pads2"), 1)
            pool.memset(reset, 1.0).then_inc(sem("pads2"), 1)
            pool.wait_ge(sem("pads2"), 3)
            pool.memset(reset.rearrange("p (q n) -> p q n", q=16)[:, :, 0:1], 0.0).then_inc(sem("pads2"), 1)
            for a in range(22, 24):
                start_piece(a)
            pool.wait_ge(sem("yb_ready"), 1)
            spread(bc[:, 0, :], A["ln1_g_2"][0], sem("spread3"))
            spread(bc[:, 1, :], A["ln1_b_2"][0], sem("spread3"))
            spread(bc[:, 2, :], A["ln2_g_2"][0], sem("spread3"))
            spread(bc[:, 3, :], A["ln2_b_2"][0], sem("spread3"))

        def flat(name):
            a = A[name]
            if name == "conv_w":
                return a[0].rearrange("j (t p) -> (j t) p", p=P)
            if name == "b_s_2":
                return a[0]
            if name == "r_k_2":
                return a[0].rearrange("(t h) n -> t (h n)", h=2)
            return a[0].rearrange("(t p) -> t p", p=P)

        @block.scalar
        def _(act):
            chain = [0]

            def step(ins):
                chain[0] += 1
                ins.then_inc(sem("act_chain"), 1)
                act.wait_ge(sem("act_chain"), chain[0])

            def item(name):
                pair, _, z = place[name]
                act.wait_ge(sem("blocks_done"), z)
                return bank[2 * (pair % 2)], bank[2 * (pair % 2) + 1]

            def freed(name, ins):
                ins.then_inc(sem(f"pair{place[name][0] % 2}_free"), 1)

            act.dma_start(cst[:, :], A["const"]).then_inc(sem("const_in"), 16)
            act.dma_start(cc[:, 0, :], A["c"][0].rearrange("(p k) -> p k", k=8)).then_inc(sem("c_in"), 16)
            act.dma_start(cc[:, 1, :], A["c_2"][0].rearrange("(p k) -> p k", k=8)).then_inc(sem("c_in"), 16)
            act.dma_start(posi[:, :], A["positions"][0].rearrange("(m p) -> p m", p=P),
                          allow_slow_non_contiguous=True).then_inc(sem("pos_in"), 16)
            for i, (tab, where) in enumerate(((ROWS1, v1), (ROWS2, v2))):
                for name, n in tab:
                    a, b = where[name]
                    if name == "mu_shift_2":
                        act.dma_start(vraw[a:b - 1, i, :], A[name][0, 0:14 * P].rearrange("(t p) -> t p", p=P))\
                           .then_inc(sem(f"vec{i}_in"), 16)
                        act.dma_start(vraw[b - 1:b, i, :], A[name][:, 1824 - P:1824]).then_inc(sem(f"vec{i}_in"), 16)
                    else:
                        act.dma_start(vraw[a:b, i, :], flat(name)).then_inc(sem(f"vec{i}_in"), 16)

            def split(name):
                for b in at_block[name]:
                    _, _, nk, width, _, count, g = order[b]
                    act.wait_ge(sem(f"raw{b % RAW}_in"), count)
                    if g >= HL:
                        act.wait_ge(sem("blocks_done"), g - HL + 1)
                    act.activation(whi[:, g % HL, 0:nk * width], raw[:, b % RAW, 0:nk * width], ACT.Copy)\
                       .then_inc(sem("hi_ready"), 1)

            def scale_h(u):
                g = gain[:, u, :]
                sh = modT[:, u // 2, (24 if u % 2 else 0):(32 if u % 2 else 8)]
                act.wait_ge(sem("gain_ready"), u + 1)
                for k in range(4):
                    act.wait_ge(sem("hx_turned"), 4 * u + k // 2 + 1)
                    act.activation(hx[:, k, :], bank[4 + k // 2][:, 256 * (k % 2):256 * (k % 2) + 256], ACT.Identity,
                                   bias=sh[:, k:k + 1], scale=g[:, k:k + 1]).then_inc(sem("hx_scaled"), 1)

            def branch_gates(n):
                for h, b in enumerate(item(f"g{n}")):
                    ins = act.activation(gT[:, 4 * n + 2 * h:4 * n + 2 * h + 2, :],
                                         b[:, :].rearrange("p (t n) -> p t n", t=2), ACT.Sigmoid)
                    ins.then_inc(sem("gT_ready"), 1) if h == 0 else freed(f"g{n}", ins)

            act.wait_ge(sem("x_in"), 16)
            for m in range(MT):
                act.activation(xn[:, m * D:(m + 1) * D], xt[:, m, :], ACT.Square,
                               accum_out=st[:, m:m + 1]).then_inc(sem("squares"), 1)
            act.wait_ge(sem("var_ready"), 1)
            act.activation(st[:, 4:6], st[:, 2:4], ACT.Sqrt).then_inc(sem("std_ready"), 1)
            act.wait_ge(sem("c_in"), 32)
            act.activation(cc[:, 1, :], cc[:, 1, :], ACT.Silu).then_inc(sem("cs_ready"), 1)
            act.wait_ge(sem("angles"), 1)
            act.activation(cossin, rsc[:, 1], ACT.Sin).then_inc(sem("cossin_ready"), 1)
            scale_h(0)
            split("o_if")
            split("qm")
            b0, b1 = item("o_if")
            act.activation(osig[:, 0, :], b0[:, :], ACT.Sigmoid).then_inc(sem("osig_ready"), 1)
            freed("o_if", act.activation(osig[:, 1, :], b1[:, :], ACT.Sigmoid))
            split("km")
            for t0, name, nxt in ((0, "qm", "vm"), (4, "km", None)):
                for h, b in enumerate(item(name)):
                    act.wait_ge(sem("pads"), 1)
                    ins = act.activation(conv_in[:, t0 + 2 * h:t0 + 2 * h + 2, 3:259],
                                         b[:, :].rearrange("p (t n) -> p t n", t=2), ACT.Copy)
                    if h == 0:
                        ins.then_inc(sem("conv_raw"), 1)
                    else:
                        freed(name, ins)
                if nxt:
                    split(nxt)
            act.wait_ge(sem("if_turned"), 1)
            r_i, r_f, r_l = rows[0:4, 0, :], rows[0:4, 1, :], rows[0:4, 2, :]
            act.activation(r_i, bank[7][0:4, 0:256], ACT.Copy).then_inc(sem("act_chain"), 1)
            chain[0] += 1
            step(act.activation(r_f, bank[7][0:4, 256:512], ACT.Copy))
            step(act.activation(r_l, r_f, ACT.Abs))
            step(act.activation(r_l, r_l, ACT.Exp, scale=-1.0))
            act.activation(r_l, r_l, ACT.Ln, bias=1.0).then_inc(sem("log_ready"), 1)
            for m, b in enumerate(item("vm")):
                ins = act.activation(vaug[:, m, :, 0:128], b[:, :].rearrange("p (h n) -> p h n", h=HM), ACT.Copy)
                ins.then_inc(sem("v_ready"), 1) if m == 0 else freed("vm", ins)
            split("qa")
            split("kva")
            act.wait_ge(sem("rows_ready"), 1)
            act.activation(rows[0:4, 4, :], rows[0:4, 4, :], ACT.Exp).then_inc(sem("rows_exp"), 1)
            act.activation(rows[0:4, 5, :], rows[0:4, 5, :], ACT.Exp).then_inc(sem("rows_exp"), 1)
            act.activation(rows[0:4, 6, :], rows[0:4, 6, :], ACT.Exp, scale=-1.0).then_inc(sem("rows_exp"), 1)
            act.activation(rows[0:4, 2, 16:20], rows[0:4, 2, 16:20], ACT.Exp).then_inc(sem("rows_exp"), 1)
            act.wait_ge(sem("conv_done"), 1)
            for t in range(2):
                act.activation(qk[:, 4 * t:4 * t + 4, :], qk[:, 4 * t:4 * t + 4, :], ACT.Silu)\
                   .then_inc(sem("silu_done"), 1)
            split("g0")
            act.wait_ge(sem("arg_ready"), 1)
            for h in range(HM):
                for m in range(MT):
                    act.activation(wT[:, h, m, :], wT[:, h, m, :], ACT.Exp,
                                   bias=st[:, 64 + 16 * m + h:64 + 16 * m + h + 1]).then_inc(sem("wT_ready"), 1)
            split("g1")
            branch_gates(0)
            split("g2")
            branch_gates(1)
            split("g3")
            branch_gates(2)
            for m in range(MT):
                act.wait_ge(sem("qr_turned"), m + 1)
                act.activation(qT[:, :, m * P:(m + 1) * P], bank[4 + m][:, :].rearrange("p (i n) -> p i n", i=4),
                               ACT.Copy, scale=DH ** -0.5).then_inc(sem("qT_ready"), 1)
            act.wait_ge(sem("qr_turned"), 3)
            act.activation(kT, bank[6][:, 0:256], ACT.Copy).then_inc(sem("qT_ready"), 1)
            for m, sm in ((0, sm0), (1, sm1)):
                act.wait_ge(sem("smax_ready"), m + 1)
                for h in range(HQ):
                    act.activation(sm[:, h, :], sm[:, h, :], ACT.Exp, bias=st[:, 16 + 8 * m + h:17 + 8 * m + h],
                                   accum_out=st[:, 32 + 8 * m + h:33 + 8 * m + h]).then_inc(sem("exp_ready"), 1)
                act.activation(st[:, 48 + 8 * m:56 + 8 * m], st[:, 48 + 8 * m:56 + 8 * m], ACT.Exp)\
                   .then_inc(sem("exp_ready"), 1)
            branch_gates(3)
            split("ba0")
            split("ba1")
            for n in range(6):
                act.wait_ge(sem("p_turned"), n + 1)
                act.activation(pT[:, 4 * n:4 * n + 4, :], bank[4 + n % 4][:, :].rearrange("p (h n) -> p h n", h=4),
                               ACT.Copy).then_inc(sem("pT_ready"), 1)
            for m in range(MT):
                for h2 in range(2):
                    act.wait_ge(sem("intra_done"), 2 * m + h2 + 1)
                    act.activation(intra[:, m, 2 * h2:2 * h2 + 2, :],
                                   bank[4 + 2 * 0 + h2][:, 0:258].rearrange("p (h n) -> p h n", h=2),
                                   ACT.Copy).then_inc(sem("intra_ready"), 1)
            act.wait_ge(sem("hvar_ready"), 1)
            act.activation(st[:, 112:120], st[:, 112:120], ACT.Sqrt).then_inc(sem("hstd_ready"), 1)
            for m in range(MT):
                act.wait_ge(sem("ya_turned"), m + 1)
                act.activation(yah[:, :, m * P:(m + 1) * P], bank[4 + m][:, :].rearrange("p (i n) -> p i n", i=4),
                               ACT.Copy).then_inc(sem("yah_ready"), 1)
            for m in range(MT):
                act.wait_ge(sem("ym_turned"), m + 1)
                act.activation(ymh[:, :, m * P:(m + 1) * P], bank[6 + m][:, :].rearrange("p (i n) -> p i n", i=4),
                               ACT.Copy).then_inc(sem("ymh_ready"), 1)
            split("bm0")
            split("bm1")
            for n in range(2):
                act.wait_ge(sem("sum_ready"), n + 1)
                act.activation(merged[0][:, 4 * n:4 * n + 4, :], gT[:, 4 * n:4 * n + 4, :], ACT.Copy)\
                   .then_inc(sem("mgh_ready"), 1)
            split("wo0")
            split("wo1")

            def std(n, a, z):
                act.wait_ge(sem("var_ready"), n)
                act.activation(st[:, a:z], st[:, a:z], ACT.Sqrt).then_inc(sem("std_ready"), 1)

            sil_out = xn[:, 0:512]
            wo = [item("wo0"), item("wo1")]
            for m in range(MT):
                for half in range(2):
                    step(act.activation(sil_out, wo[half][m][:, :], ACT.Square,
                                        accum_out=st[:, 120 + 2 * m + half:121 + 2 * m + half]))
            act.nop().then_inc(sem("post_squares"), 1)
            std(2, 124, 126)
            split("ff0")
            for m in range(MT):
                act.wait_ge(sem("x_added"), m + 1)
                act.activation(xn[:, m * D:(m + 1) * D], xt[:, m, :], ACT.Square,
                               accum_out=st[:, m:m + 1]).then_inc(sem("squares"), 1)
            act.wait_ge(sem("var_ready"), 3)
            act.activation(st[:, 4:6], st[:, 2:4], ACT.Sqrt).then_inc(sem("std_ready"), 1)
            scale_h(1)

            def feed_forward(letter, down, n):
                for j in range(FT // 2):
                    if j + 1 < FT // 2:
                        split(f"{letter}{j + 1}")
                    g, _ = item(f"{letter}{j}")
                    q = n * (FT // 2) + j
                    if j >= 2:
                        act.wait_ge(sem("ffp_ready"), q - 1)
                    act.activation(sil[:, j % 2, :], g[:, :], ACT.Silu).then_inc(sem("sil_ready"), 1)
                    act.wait_ge(sem("ffp_ready"), q + 1)
                    act.activation(ffh[:, 2 * j:2 * j + 2, :], ffp[:, j % 2, :].rearrange("p (t n) -> p t n", t=2),
                                   ACT.Copy).then_inc(sem("ffh_ready"), 1)
                split(down)

            feed_forward("ff", "dn1", 0)
            act.wait_ge(sem("blocks_done"), place["dn1"][2])
            for m in range(MT):
                for half in range(2):
                    step(act.activation(sil_out, bank[4 + 2 * m + half][:, :], ACT.Square,
                                        accum_out=st[:, 120 + 2 * m + half:121 + 2 * m + half]))
            act.nop().then_inc(sem("post_squares"), 1)
            std(4, 124, 126)
            std(5, 126, 128)
            split("pu")
            scale_h(2)

            for name, dst, nxt in (("pu", gu, "pv"), ("pv", gv, "r")):
                split(nxt)
                act.wait_ge(sem("h_ready"), 6)
                for m, b in enumerate(item(name)):
                    ins = act.activation(dst[:, m, :], b[:, :], ACT.Gelu_apprx_tanh)
                    ins.then_inc(sem("gelu_done"), 1) if m == 0 else freed(name, ins)
            act.wait_ge(sem("gvar_ready"), 1)
            act.activation(st[:, 132:134], st[:, 132:134], ACT.Sqrt).then_inc(sem("gstd_ready"), 1)
            act.wait_ge(sem("pads2"), 1)
            for t0, name, nxt in ((0, "r", "k"), (4, "k", "v"), (8, "v", "lora")):
                split(nxt)
                for h, b in enumerate(item(name)):
                    ins = act.activation(praw[:, t0 + 2 * h:t0 + 2 * h + 2, 1:257],
                                         b[:, :].rearrange("p (t n) -> p t n", t=2), ACT.Copy)
                    ins.then_inc(sem("praw_ready"), 1) if h == 0 else freed(name, ins)
            b0, b1 = item("lora")
            act.activation(praw[:, 12:14, 1:257], b0[:, :].rearrange("p (t n) -> p t n", t=2), ACT.Copy)\
               .then_inc(sem("praw_ready"), 1)
            freed("lora", act.activation(praw[:, 14, 1:257], b1[:, 0:256], ACT.Copy))
            for m in range(MT):
                act.wait_ge(sem("ga_turned"), m + 1)
                act.activation(hh[:, 0:4, m * P:(m + 1) * P], bank[6 + m][:, :].rearrange("p (i n) -> p i n", i=4),
                               ACT.Copy).then_inc(sem("gah_ready"), 1)
            act.wait_ge(sem("lora_mixed"), 1)
            act.activation(pm[0:64, 12, :], pm[0:64, 12, :], ACT.Tanh).then_inc(sem("lora_act"), 1)
            act.activation(pm[:, 13, :], pm[:, 13, :], ACT.Sigmoid).then_inc(sem("lora_act"), 1)
            act.activation(pm[96:128, 14, :], pm[96:128, 14, :], ACT.Sigmoid).then_inc(sem("lora_act"), 1)
            for n, (dst, off) in enumerate(((lw, "w0_2"), (av, "a0_2"))):
                for j in range(4):
                    act.wait_ge(sem("lora_done"), 2 * n + j // 2 + 1)
                    act.activation(dst[:, j, :], bank[4 + 2 * n + j // 2][:, 256 * (j % 2):256 * (j % 2) + 256],
                                   ACT.Sigmoid, bias=v2T[:, v2[off][0] + j:v2[off][0] + j + 1])\
                       .then_inc(sem("lwa_ready"), 1)
            for j in range(2):
                act.wait_ge(sem("lora_done"), 5 + j)
                act.activation(gmT[:, 2 * j:2 * j + 2, :], bank[4 + j][:, :].rearrange("p (t n) -> p t n", t=2),
                               ACT.Copy).then_inc(sem("gm_ready"), 1)
            act.wait_ge(sem("kk_summed"), 1)
            act.activation(nrm[0:8, :], bank[6][0:8, 0:256], ACT.Sqrt).then_inc(sem("kk_len"), 1)
            act.wait_ge(sem("cum_ready"), 1)
            act.activation(dec1, cum, ACT.Exp).then_inc(sem("dec_ready"), 1)
            act.wait_ge(sem("cum_ready"), 2)
            act.activation(dec2, lw, ACT.Exp).then_inc(sem("dec_ready"), 1)
            act.wait_ge(sem("dec_ready"), 2)
            act.activation(lw, cum, ACT.Exp, scale=-1.0).then_inc(sem("dec_ready"), 1)
            for n, dst in enumerate((btok, ktok, vtok)):
                for h in range(2):
                    act.wait_ge(sem("tok_turned"), 2 * n + h + 1)
                    act.activation(dst[:, 8 * h:8 * h + 8, :],
                                   bank[(2 * n + h) % 4 + 4][:, :].rearrange("p (q n) -> p q n", q=8), ACT.Copy)\
                       .then_inc(sem("tok_ready"), 1)
            for c in range(NCH):
                act.wait_ge(sem("x_done"), c + 1)
                act.activation(xs, bank[4][:, 0:256].rearrange("p (j n) -> p j n", j=4), ACT.Copy)\
                   .then_inc(sem("x_ready"), 1)
                act.wait_ge(sem("u_done"), c + 1)
                act.activation(us, bank[5][:, 0:256].rearrange("p (j n) -> p j n", j=4), ACT.Copy)\
                   .then_inc(sem("u_ready"), 1)
                act.wait_ge(sem("yc_done"), c + 1)
                act.activation(yT[:, :, c * L:(c + 1) * L], bank[7][:, 0:256].rearrange("p (j n) -> p j n", j=4),
                               ACT.Copy).then_inc(sem("yc_ready"), 1)
            split("wo2")
            act.wait_ge(sem("yvar_ready"), 1)
            act.activation(nrm[0:8, :], nrm[0:8, :], ACT.Sqrt).then_inc(sem("ystd_ready"), 1)
            act.wait_ge(sem("yb_ready"), 1)
            act.activation(hh[:, 4:8, :], yT, ACT.Copy).then_inc(sem("ybh_ready"), 1)
            split("wo3")
            split("gf0")
            std(6, 126, 128)
            scale_h(3)
            feed_forward("gf", "dn2", 1)
            std(7, 126, 128)

        @block.vector
        def _(dve):
            chain = [0]

            def step(ins):
                chain[0] += 1
                ins.then_inc(sem("dve_chain"), 1)
                dve.wait_ge(sem("dve_chain"), chain[0])

            def item(name):
                pair, _, z = place[name]
                dve.wait_ge(sem("blocks_done"), z)
                return bank[2 * (pair % 2)], bank[2 * (pair % 2) + 1]

            def freed(name, ins):
                ins.then_inc(sem(f"pair{place[name][0] % 2}_free"), 1)

            def bcast(ap, n):
                return ap.unsqueeze(len(ap.shape)).to_broadcast(list(ap.shape) + [n])

            TT = dve.tensor_tensor
            TS = dve.tensor_scalar
            STT = dve.scalar_tensor_tensor
            for i, (dst, n) in enumerate(((v1T, n1), (v2T, n2))):
                dve.wait_ge(sem("vec_turned"), i + 1)
                step(dve.tensor_copy(dst[:, :], bank[4 + i][:, 0:n]))

            def rms_rows(n):
                dve.wait_ge(sem("squares"), 2 * n + 2)
                step(TS(st[:, 2:4], st[:, 0:2], 1.0 / D, EPS, ALU.mult, ALU.add))
                step(dve.reciprocal(st[:, 2:4], st[:, 2:4]))
                dve.nop().then_inc(sem("var_ready"), 1)

            rms_rows(0)
            dve.wait_ge(sem("std_ready"), 1)
            for m in range(MT):
                TS(xn[:, m * D:(m + 1) * D], xt[:, m, :], st[:, 4 + m:5 + m], None, ALU.mult)\
                    .then_inc(sem("xn_ready"), 1)
            dve.wait_ge(sem("pos_in"), 16)
            dve.wait_ge(sem("const_in"), 16)
            step(dve.tensor_copy(st[:, 10:12], posi[:, :]))
            ang, red = rsc[:, 0], rsc[:, 1]
            for m in range(MT):
                for f in range(2):
                    TS(ang[:, m, f, :], C("freq"), st[:, 10 + m:11 + m], None, ALU.mult).then_inc(sem("dve_chain"), 1)
                    chain[0] += 1
            dve.wait_ge(sem("dve_chain"), chain[0])
            step(TS(red[:, :, 0, :], ang[:, :, 0, :], 1 / (2 * math.pi), 0.0, ALU.mult, ALU.add))
            step(TS(red[:, :, 1, :], ang[:, :, 1, :], 1 / (2 * math.pi), 0.25, ALU.mult, ALU.add))
            step(TS(red, red, ROUND, None, ALU.add))
            step(TS(red, red, ROUND, None, ALU.subtract))
            for piece in (TWO_PI_1, TWO_PI_2, TWO_PI_3):
                a2, r2 = (v.rearrange("p m f c -> p (m f c)") for v in (ang, red))
                step(STT(a2, r2, -piece, a2, ALU.mult, ALU.add))
            step(TS(ang[:, :, 1, :], ang[:, :, 1, :], math.pi / 2, None, ALU.add))
            TS(red, ang, SIN_MAX, -SIN_MAX, ALU.min, ALU.max).then_inc(sem("angles"), 1)

            def pair_wait(name):
                dve.wait_ge(sem(f"pair{place[name][0] % 2}_free"), place[name][0] // 2 + 1)

            def prepare(name):
                for b in at_block[name]:
                    _, i, nk, width, _, count, g = order[b]
                    if g is not None:
                        dve.wait_ge(sem("hi_ready"), g + 1)
                        TT(wlo[:, g % HL, 0:nk * width], raw[:, b % RAW, 0:nk * width],
                           whi[:, g % HL, 0:nk * width].bitcast(fp), ALU.subtract).then_inc(sem("block_ready"), 1)
                        continue
                    a = int(name[1:])
                    which = PIECES[a][0]
                    dve.wait_ge(sem(f"raw{b % RAW}_in"), count)
                    if i == 0:
                        dve.wait_ge(sem(f"acc{a % 2}_started"), 16 * (a // 2 + 1))
                        if a == 0:
                            dve.wait_ge(sem("c_in"), 32)
                        if a == 12:
                            dve.wait_ge(sem("cs_ready"), 1)
                    w = cut(raw, b % RAW, nk, width)
                    for k in range(4):
                        step(STT(acc[:, a % 2, :], w[:, k, :], cc[:, which, 4 * i + k:4 * i + k + 1],
                                 acc[:, a % 2, :], ALU.mult, ALU.add))
                    dve.nop().then_inc(sem("block_ready"), 1)
                    if i == 1:
                        dve.nop().then_inc(sem("acc_ready"), 1)

            def collect_piece(a, gpost=None):
                i, c0 = PIECES[a]
                dve.wait_ge(sem("piece_done"), a + 1)
                b0 = bank[2 * (place[f"c{a}"][0] % 2)]
                if a in GATES:
                    dst = gg[:, c0 % 1024:c0 % 1024 + 512]
                    ins = dve.tensor_copy(dst, b0[:, :]) if gpost is None else \
                        TT(dst, b0[:, :], gpost[:, c0 % 1024:c0 % 1024 + 512], ALU.mult)
                else:
                    ins = dve.tensor_copy(modT[:, i, c0 // P:c0 // P + 4], b0[:, 0:4])
                step(ins)
                dve.nop().then_inc(sem(f"pair{place[f'c{a}'][0] % 2}_free"), 1)

            def gains(u, g):
                i, c0 = u // 2, (32 if u % 2 else 8)
                sc = modT[:, i, c0:c0 + 8]
                step(TS(gain[:, u, :], sc, 1.0, None, ALU.add))
                if g is not None:
                    step(TT(gain[:, u, :], gain[:, u, :], g, ALU.mult))
                dve.nop().then_inc(sem("gain_ready"), 1)

            def scale_h(u):
                sh = modT[:, u // 2, (24 if u % 2 else 0):(32 if u % 2 else 8)]
                for k in range(4, 8):
                    dve.wait_ge(sem("hx_turned"), 4 * u + k // 2 + 1)
                    TS(hx[:, k, :], bank[4 + k // 2][:, 256 * (k % 2):256 * (k % 2) + 256], gain[:, u, k:k + 1],
                       sh[:, k:k + 1], ALU.mult, ALU.add).then_inc(sem("dve_chain"), 1)
                chain[0] += 4
                for n in range(2):
                    if n == 0:
                        dve.wait_ge(sem("hx_scaled"), 4 * u + 4)
                    else:
                        dve.wait_ge(sem("dve_chain"), chain[0])
                    t = slice(4 * n, 4 * n + 4)
                    step(dve.tensor_copy(hh[:, t, :], hx[:, t, :]))
                    TT(hl[:, t, :], hx[:, t, :], hh[:, t, :].bitcast(fp), ALU.subtract).then_inc(sem("h_ready"), 1)

            for a in range(4):
                prepare(f"c{a}")
                if a:
                    collect_piece(a - 1)
            collect_piece(3)
            gains(0, v1T[:, v1["g_pre_mix"][0]:v1["g_pre_mix"][1]])
            scale_h(0)
            prepare("o_if")
            prepare("qm")
            item("o_if")
            dve.wait_ge(sem("spread1"), 7 * 16)
            for m in range(MT):
                TT(st[:, 240 + 8 * m:248 + 8 * m], bank[4 + m][:, 0:8], bsm[:, 0:8], ALU.add)\
                    .then_inc(sem("if_ready"), 1)
            dve.wait_ge(sem("osig_ready"), 1)
            dve.wait_ge(sem(f"pair{place['o_if'][0] % 2}_free"), place["o_if"][0] // 2 + 1)
            for m in range(MT):
                step(TT(osig[:, m, :], osig[:, m, :], bcs[:, 0, :], ALU.mult))
            prepare("km")
            prepare("c4")
            for t in range(8):
                if t == 4:
                    prepare("vm")
                    collect_piece(4)
                    prepare("c5")
                name = "qm" if t < 4 else "km"
                if t % 4 < 2:
                    dve.wait_ge(sem("conv_raw"), t // 4 + 1)
                else:
                    dve.wait_ge(sem(f"pair{place[name][0] % 2}_free"), place[name][0] // 2 + 1)
                w = lambda j: v1T[:, v1["conv_w"][0] + 8 * j + t:v1["conv_w"][0] + 8 * j + t + 1]
                cb = v1T[:, v1["conv_b"][0] + t:v1["conv_b"][0] + t + 1]
                step(TS(qk[:, t, :], conv_in[:, t, 0:256], w(0), cb, ALU.mult, ALU.add))
                for j in range(1, 4):
                    step(STT(qk[:, t, :], conv_in[:, t, j:j + 256], w(j), qk[:, t, :], ALU.mult, ALU.add))
            dve.nop().then_inc(sem("conv_done"), 1)
            prepare("qa")
            collect_piece(5)
            prepare("c6")

            def row(i):
                return rows[0:4, i, :]

            def chunked(i):
                return rows[0:4, i, :].rearrange("p (c n) -> p c n", c=NCH)

            dve.wait_ge(sem("log_ready"), 1)
            dve.wait_ge(sem("pads"), 7)
            step(STT(row(1), row(1), 0.0, row(2), ALU.min, ALU.subtract))
            step(dve.tensor_tensor_scan(row(3), resets[0:4, 0, :], row(1), 0.0, ALU.mult, ALU.add))
            step(TT(row(0), row(0), row(3), ALU.subtract))
            step(dve.tensor_tensor_scan(row(6), resets[0:4, 1, :], row(0), 0.0, ALU.add, ALU.max))
            bl = rows[0:4, 2, 0:4]
            amax, mnew, mprev, dcy = (rows[0:4, 2, 4 * i:4 * i + 4] for i in range(1, 5))
            step(dve.tensor_copy(bl, chunked(3)[:, :, L - 1]))
            step(TT(chunked(4), chunked(0), bcast(bl, L), ALU.add))
            step(dve.tensor_reduce(amax, chunked(4), AX, ALU.max))
            step(dve.tensor_tensor_scan(mnew, bl, amax, 0.0, ALU.add, ALU.max))
            step(dve.memset(mprev[:, 0:1], 0.0))
            step(dve.tensor_copy(mprev[:, 1:4], mnew[:, 0:3]))
            step(TT(dcy, bl, mprev, ALU.add))
            step(TT(dcy, dcy, mnew, ALU.subtract))
            step(TT(chunked(4), chunked(4), bcast(mnew, L), ALU.subtract))
            step(TT(chunked(5), chunked(3), bcast(mprev, L), ALU.add))
            step(TT(row(6), row(6), row(3), ALU.add))
            step(TT(row(6), row(6), row(5), ALU.max))
            step(TT(row(5), row(5), row(6), ALU.subtract))
            step(TT(row(7), row(3), row(6), ALU.subtract))
            dve.nop().then_inc(sem("rows_ready"), 1)
            prepare("kva")
            def rotate(src, nh, m, dst):
                w = nh * 64
                v = src.rearrange("p (h f c) -> p h f c", h=nh, f=2)
                fa = rope_a[:, 0:w].rearrange("p (h f c) -> p h f c", h=nh, f=2)
                fb = rope_b[:, 0:w].rearrange("p (h f c) -> p h f c", h=nh, f=2)
                cos = cossin[:, m, 1, :].unsqueeze(1).to_broadcast([P, nh, 32])
                sin = cossin[:, m, 0, :].unsqueeze(1).to_broadcast([P, nh, 32])
                for f in range(2):
                    step(TT(fa[:, :, f, :], v[:, :, f, :], cos, ALU.mult))
                    step(TT(fb[:, :, f, :], v[:, :, f, :], sin, ALU.mult))
                step(TT(dst(0), fa[:, :, 0, :], fb[:, :, 1, :], ALU.subtract))
                return TT(dst(1), fa[:, :, 1, :], fb[:, :, 0, :], ALU.add)

            dve.wait_ge(sem("cossin_ready"), 1)
            for m, b in enumerate(item("qa")):
                q4 = qr[:, m, :].rearrange("p (i g f c) -> p g i f c", i=4, g=HG, f=2)
                v = b[:, :].rearrange("p (g i f c) -> p g i f c", g=HG, i=4, f=2)
                fa = rope_a[:, 0:512].rearrange("p (g i f c) -> p g i f c", g=HG, i=4, f=2)
                fb = rope_b[:, 0:512].rearrange("p (g i f c) -> p g i f c", g=HG, i=4, f=2)
                cos = cossin[:, m, 1, :].unsqueeze(1).to_broadcast([P, 8, 32])
                sin = cossin[:, m, 0, :].unsqueeze(1).to_broadcast([P, 8, 32])
                v8 = b[:, :].rearrange("p (h f c) -> p h f c", h=8, f=2)
                fa8 = rope_a[:, 0:512].rearrange("p (h f c) -> p h f c", h=8, f=2)
                fb8 = rope_b[:, 0:512].rearrange("p (h f c) -> p h f c", h=8, f=2)
                for f in range(2):
                    step(TT(fa8[:, :, f, :], v8[:, :, f, :], cos, ALU.mult))
                    step(TT(fb8[:, :, f, :], v8[:, :, f, :], sin, ALU.mult))
                for g in range(HG):
                    step(TT(q4[:, g, :, 0, :], fa[:, g, :, 0, :], fb[:, g, :, 1, :], ALU.subtract))
                    step(TT(q4[:, g, :, 1, :], fa[:, g, :, 1, :], fb[:, g, :, 0, :], ALU.add))
                dve.nop().then_inc(sem("qr_ready"), 1)
            dve.nop().then_inc(sem(f"pair{place['qa'][0] % 2}_free"), 1)
            collect_piece(6)
            prepare("c7")
            for m, b in enumerate(item("kva")):
                k4 = kr[:, m, :].rearrange("p (g f c) -> p g f c", g=HG, f=2)
                step(rotate(b[:, 0:128], HG, m, lambda f: k4[:, :, f, :]))
                dve.nop().then_inc(sem("qr_ready"), 1)
                step(dve.tensor_copy(va[:, m, :], b[:, 128:256]))
                dve.nop().then_inc(sem("va_ready"), 1)
            dve.nop().then_inc(sem(f"pair{place['kva'][0] % 2}_free"), 1)

            prepare("g0")
            collect_piece(7)
            gains(1, v1T[:, v1["g_pre_ffn"][0]:v1["g_pre_ffn"][1]])
            prepare("c8")
            dve.wait_ge(sem("silu_done"), 2)
            TS(qk[:, 4:8, :], qk[:, 4:8, :], DM ** -0.5, None, ALU.mult).then_inc(sem("k_scaled"), 1)
            dve.wait_ge(sem("cols_turned"), 1)
            step(dve.tensor_copy(st[:, 64:96], bank[7][:, 0:32]))
            step(dve.tensor_copy(st[:, 96:112], bank[7][:, 32:48]))
            for h2 in range(2):
                dve.wait_ge(sem("bm_spread"), h2 + 1)
                for h in range(2):
                    step(TT(wT[:, 2 * h2 + h, :, :],
                            bank[4 + h2][:, 256 * h:256 * h + 256].rearrange("p (m n) -> p m n", m=MT),
                            C("chunk_t").unsqueeze(1).to_broadcast([P, MT, P]), ALU.add))
            dve.nop().then_inc(sem("arg_ready"), 1)
            prepare("g1")
            dve.wait_ge(sem("if_ready"), 2)
            collect_piece(8, bc[:, 0, :])
            prepare("c9")
            for m in range(MT):
                dve.wait_ge(sem("kc_turned"), m + 1)
                wk = st[:, 64 + 16 * m + 4:64 + 16 * m + 8]
                TT(kw[:, m, :, :], bank[4 + m][:, :].rearrange("p (h n) -> p h n", h=HM), bcast(wk, 128), ALU.mult)\
                    .then_inc(sem("kw_ready"), 1)
            dve.wait_ge(sem("wT_ready"), 8)
            for h2 in range(2):
                dve.wait_ge(sem("ms_done"), h2 + 1)
                TT(sw[:, 2 * h2:2 * h2 + 2, :, :],
                   bank[6 + h2][:, :].rearrange("p (h m n) -> p h m n", h=2, m=MT),
                   wT[:, 2 * h2:2 * h2 + 2, :, :], ALU.mult).then_inc(sem("sw_ready"), 1)
            prepare("g2")
            collect_piece(9, bc[:, 0, :])
            for c in range(NCH - 1):
                for h2 in range(2):
                    dve.wait_ge(sem("kv_done"), 2 * c + h2 + 1)
                    for h in range(2 * h2, 2 * h2 + 2):
                        src = bank[4 + 2 * (c % 2) + h2][:, 129 * (h % 2):129 * (h % 2) + 129]
                        if c == 0:
                            ins = dve.tensor_copy(cstate[:, 1, h, :], src)
                        else:
                            ins = STT(cstate[:, c + 1, h, :], cstate[:, c, h, :],
                                      st[:, 96 + 4 * h + c:97 + 4 * h + c], src, ALU.mult, ALU.add)
                        step(ins)
                    dve.nop().then_inc(sem("state_ready"), 1)

            prepare("g3")
            sink = bsm[:, 8:16]
            for m, sm in ((0, sm0), (1, sm1)):
                n = 128 if m == 0 else 256
                mask = C("attn")[:, 256 - n:256]
                hb = 4 if m == 0 else 2
                for b in range(HQ // hb):
                    dve.wait_ge(sem("s_done"), (0 if m == 0 else 2) + b + 1)
                    bk = bank[(4, 5)[b] if m == 0 else (6, 7, 4, 5)[b]]
                    TT(sm[:, hb * b:hb * b + hb, :], bk[:, :].rearrange("p (h n) -> p h n", h=hb),
                       mask.unsqueeze(1).to_broadcast([P, hb, n]), ALU.add).then_inc(sem("s_masked"), 1)
                dve.wait_ge(sem("s_masked"), 2 if m == 0 else 6)
                mx = st[:, 16 + 8 * m:24 + 8 * m]
                step(dve.tensor_reduce(mx, sm, AX, ALU.max))
                step(TT(mx, mx, sink, ALU.max))
                step(TT(st[:, 48 + 8 * m:56 + 8 * m], sink, mx, ALU.subtract))
                step(TS(mx, mx, -1.0, None, ALU.mult))
                dve.nop().then_inc(sem("smax_ready"), 1)
            prepare("ba0")
            prepare("ba1")
            for m in range(MT):
                dve.wait_ge(sem("exp_ready"), 9 * m + 9)
                step(TT(st[:, 32 + 8 * m:40 + 8 * m], st[:, 32 + 8 * m:40 + 8 * m], st[:, 48 + 8 * m:56 + 8 * m],
                        ALU.add))
                step(dve.reciprocal(st[:, 32 + 8 * m:40 + 8 * m], st[:, 32 + 8 * m:40 + 8 * m]))
            for m in range(MT):
                dve.wait_ge(sem("o_done"), m + 1)
                TT(ya[:, m, :].rearrange("p (h c) -> p h c", h=HQ), bank[6 + m][:, :].rearrange("p (h c) -> p h c", h=HQ),
                   bcast(st[:, 32 + 8 * m:40 + 8 * m], 64), ALU.mult)\
                    .then_inc(sem("ya_ready"), 1)
            for m in range(MT):
                for h2 in range(2):
                    dve.wait_ge(sem("inter_done"), 2 * m + h2 + 1)
                    dve.wait_ge(sem("intra_ready"), 2 * m + h2 + 1)
                    for h in range(2 * h2, 2 * h2 + 2):
                        ins = STT(intra[:, m, h, :], bank[6 + h2][:, 129 * (h % 2):129 * (h % 2) + 129],
                                  st[:, 64 + 16 * m + 8 + h:64 + 16 * m + 9 + h], intra[:, m, h, :],
                                  ALU.mult, ALU.add)
                        if h % 2:
                            ins.then_inc(sem("inter_used"), 1)
                        else:
                            step(ins)
                dve.wait_ge(sem("inter_used"), 2 * m + 2)
                den = st[:, 136 + 4 * m:140 + 4 * m]
                step(TS(den, intra[:, m, :, 128], -1.0, None, ALU.mult))
                step(TT(den, den, intra[:, m, :, 128], ALU.max))
                step(TT(den, den, st[:, 64 + 16 * m + 12:64 + 16 * m + 16], ALU.max))
                step(dve.reciprocal(den, den))
                step(TT(intra[:, m, :, 0:128], intra[:, m, :, 0:128], bcast(den, 128), ALU.mult))
                for h in range(HM):
                    step(dve.bn_stats(st[:, 144 + 6 * h:150 + 6 * h], intra[:, m, h, 0:128]))
                    step(dve.bn_aggr(st[:, 176 + 8 * m + 2 * h:178 + 8 * m + 2 * h], st[:, 144 + 6 * h:150 + 6 * h]))
            mv = st[:, 176:192].rearrange("p (q w) -> p q w", w=2)
            step(TS(st[:, 112:120], mv[:, :, 1], EPS, None, ALU.add))
            step(dve.reciprocal(st[:, 112:120], st[:, 112:120]))
            dve.nop().then_inc(sem("hvar_ready"), 1)
            dve.wait_ge(sem("hstd_ready"), 1)
            for m in range(MT):
                for h in range(HM):
                    step(TS(intra[:, m, h, 0:128], intra[:, m, h, 0:128], mv[:, 4 * m + h, 0:1],
                            st[:, 112 + 4 * m + h:113 + 4 * m + h], ALU.subtract, ALU.mult))
                TT(ym[:, m, :].rearrange("p (h n) -> p h n", h=HM), intra[:, m, :, 0:128],
                   osig[:, m, :].rearrange("p (h n) -> p h n", h=HM), ALU.mult).then_inc(sem("ym_ready"), 1)
            for m in range(MT):
                t = slice(m * P, (m + 1) * P)
                dve.wait_ge(sem("yah_ready"), m + 1)
                TT(yal[:, :, t], bank[4 + m][:, :].rearrange("p (i n) -> p i n", i=4), yah[:, :, t].bitcast(fp),
                   ALU.subtract).then_inc(sem("ya_split"), 1)
            for m in range(MT):
                t = slice(m * P, (m + 1) * P)
                dve.wait_ge(sem("ymh_ready"), m + 1)
                TT(yml[:, :, t], bank[6 + m][:, :].rearrange("p (i n) -> p i n", i=4), ymh[:, :, t].bitcast(fp),
                   ALU.subtract).then_inc(sem("ym_split"), 1)
            dve.wait_ge(sem("gT_ready"), 4)
            for n in range(4):
                dve.wait_ge(sem(f"pair{place[f'g{n}'][0] % 2}_free"), place[f"g{n}"][0] // 2 + 1)
            prepare("bm0")
            for n in range(2):
                if n:
                    prepare("bm1")
                for h, b in enumerate(item(f"ba{n}")):
                    t = 4 * n + 2 * h
                    step(TT(gT[:, t:t + 2, :], b[:, :].rearrange("p (t n) -> p t n", t=2), gT[:, t:t + 2, :],
                            ALU.mult))
                dve.nop().then_inc(sem(f"pair{place[f'ba{n}'][0] % 2}_free"), 1)
            for n in range(2):
                for h, b in enumerate(item(f"bm{n}")):
                    t = 4 * n + 2 * h
                    step(TT(gT[:, 8 + t:10 + t, :], b[:, :].rearrange("p (t n) -> p t n", t=2),
                            gT[:, 8 + t:10 + t, :], ALU.mult))
                dve.nop().then_inc(sem(f"pair{place[f'bm{n}'][0] % 2}_free"), 1)
                t = slice(4 * n, 4 * n + 4)
                step(TT(gT[:, t, :], gT[:, t, :], gT[:, 8 + 4 * n:12 + 4 * n, :], ALU.add))
                dve.nop().then_inc(sem("sum_ready"), 1)
                dve.wait_ge(sem("mgh_ready"), n + 1)
                TT(merged[1][:, t, :], gT[:, t, :], merged[0][:, t, :].bitcast(fp), ALU.subtract)\
                    .then_inc(sem("merged_ready"), 1)

            def post_rms(n, banks, free, squares):
                dve.wait_ge(sem("post_squares"), n + 1)
                sq = st[:, 120:124].rearrange("p (m h) -> p m h", m=MT)
                step(TT(st[:, 124:126], sq[:, :, 0], sq[:, :, 1], ALU.add))
                step(TS(st[:, 124:126], st[:, 124:126], 1.0 / D, EPS, ALU.mult, ALU.add))
                step(dve.reciprocal(st[:, 124:126], st[:, 124:126]))
                dve.nop().then_inc(sem("var_ready"), 1)
                dve.wait_ge(sem("std_ready"), squares)
                for m in range(MT):
                    for h in range(2):
                        step(STT(xn[:, 1024 + 512 * h:1536 + 512 * h], banks[m][h][:, :], st[:, 124 + m:125 + m],
                                 gg[:, 512 * h:512 * h + 512], ALU.mult, ALU.mult))
                    step(TT(xt[:, m, :], xt[:, m, :], xn[:, 1024:2048], ALU.add))
                    dve.nop().then_inc(sem("x_added"), 1)
                for name in free:
                    dve.nop().then_inc(sem(f"pair{place[name][0] % 2}_free"), 1)

            prepare("wo0")
            prepare("wo1")
            w0, w1 = item("wo0"), item("wo1")
            post_rms(0, [(w0[0], w1[0]), (w0[1], w1[1])], ("wo0", "wo1"), 2)
            prepare("ff0")
            rms_rows(1)
            dve.wait_ge(sem("std_ready"), 3)
            for m in range(MT):
                TS(xn[:, m * D:(m + 1) * D], xt[:, m, :], st[:, 4 + m:5 + m], None, ALU.mult)\
                    .then_inc(sem("xn_ready"), 1)
            scale_h(1)

            def feed_forward(letter, down, n, pieces, gpost):
                names = [x for x, _ in ITEMS]
                for j in range(FT // 2):
                    name = f"{letter}{j}"
                    at = names.index(name) + 1
                    while names[at][0] == "c":
                        prepare(names[at])
                        at += 1
                    prepare(names[at]) if names[at][0] != "d" else None
                    q = n * (FT // 2) + j
                    _, up = item(name)
                    dve.wait_ge(sem("sil_ready"), q + 1)
                    if j >= 2:
                        dve.wait_ge(sem("ffh_ready"), q - 1)
                    step(TT(ffp[:, j % 2, :], up[:, :], sil[:, j % 2, :], ALU.mult))
                    dve.nop().then_inc(sem("ffp_ready"), 1)
                    dve.nop().then_inc(sem(f"pair{place[name][0] % 2}_free"), 1)
                    dve.wait_ge(sem("ffh_ready"), q + 1)
                    t = slice(2 * j, 2 * j + 2)
                    TT(ffl[:, t, :], ffp[:, j % 2, :].rearrange("p (t n) -> p t n", t=2), ffh[:, t, :].bitcast(fp),
                       ALU.subtract).then_inc(sem("ff_ready"), 1)
                    at = names.index(name) + 1
                    while names[at][0] == "c":
                        a = int(names[at][1:])
                        collect_piece(a, gpost if a in GATES else None)
                        if a == 15:
                            gains(2, None)
                        if a == 19:
                            gains(3, None)
                        at += 1
                prepare(down)

            feed_forward("ff", "dn1", 0, 10, bc[:, 1, :])
            dve.wait_ge(sem("blocks_done"), place["dn1"][2])
            post_rms(1, [(bank[4], bank[5]), (bank[6], bank[7])], (), 4)

            def layer_norm(n, g, b):
                for m in range(MT):
                    for h in range(2):
                        step(dve.bn_stats(st[:, 192 + 6 * h:198 + 6 * h], xt[:, m, 512 * h:512 * h + 512]))
                    step(dve.bn_aggr(st[:, 204 + 2 * m:206 + 2 * m], st[:, 192:204]))
                mv = st[:, 204:208].rearrange("p (m w) -> p m w", w=2)
                step(TS(st[:, 126:128], mv[:, :, 1], LN_EPS, None, ALU.add))
                step(dve.reciprocal(st[:, 126:128], st[:, 126:128]))
                dve.nop().then_inc(sem("var_ready"), 1)
                dve.wait_ge(sem("std_ready"), n)
                for m in range(MT):
                    step(TS(xt[:, m, :], xt[:, m, :], mv[:, m, 0:1], st[:, 126 + m:127 + m], ALU.subtract, ALU.mult))
                    step(TT(xt[:, m, :], xt[:, m, :], g, ALU.mult))
                    step(TT(xt[:, m, :], xt[:, m, :], b, ALU.add))
                    yield m

            dve.wait_ge(sem("spread2"), 32)
            for m in layer_norm(5, bc[:, 2, :], bc[:, 3, :]):
                dve.nop().then_inc(sem("emb_done"), 1)
            prepare("pu")
            scale_h(2)
            prepare("pv")

            dve.wait_ge(sem("ws_turned"), 1)
            step(TT(wsT, bank[4][:, :].rearrange("p (g n) -> p g n", g=4),
                    C("ws").unsqueeze(1).to_broadcast([P, 4, P]), ALU.mult))
            dve.nop().then_inc(sem("wsT_ready"), 1)
            prepare("r")
            item("pv")
            pair_wait("pv")
            dve.wait_ge(sem("gelu_done"), 2)
            for m in range(MT):
                step(dve.bn_stats(st[:, 192:198], gv[:, m, :]))
                step(dve.bn_aggr(st[:, 208 + 2 * m:210 + 2 * m], st[:, 192:198]))
            mv = st[:, 208:212].rearrange("p (m w) -> p m w", w=2)
            step(TS(st[:, 132:134], mv[:, :, 1], LN_EPS, None, ALU.add))
            step(dve.reciprocal(st[:, 132:134], st[:, 132:134]))
            dve.nop().then_inc(sem("gvar_ready"), 1)
            dve.wait_ge(sem("gstd_ready"), 1)
            for m in range(MT):
                step(TS(gv[:, m, :], gv[:, m, :], mv[:, m, 0:1], st[:, 132 + m:133 + m], ALU.subtract, ALU.mult))
                step(TT(gv[:, m, :], gv[:, m, :], bcs[:, 1, :], ALU.mult))
                step(TT(gv[:, m, :], gv[:, m, :], bcs[:, 2, :], ALU.add))
                dve.nop().then_inc(sem("gv_ready"), 1)
            prepare("k")
            prepare("v")
            pair_wait("pu")
            prepare("lora")
            for m in range(MT):
                dve.wait_ge(sem("sg_done"), m + 1)
                for g in range(4):
                    c0 = v2["b_s_2"][0] + g
                    step(STT(gu[:, m, 128 * g:128 * g + 128], bank[4 + m][:, 128 * g:128 * g + 128],
                             v2T[:, c0:c0 + 1], gu[:, m, 128 * g:128 * g + 128], ALU.add, ALU.mult))
                dve.nop().then_inc(sem("ga_ready"), 1)
            for m in range(MT):
                t = slice(m * P, (m + 1) * P)
                dve.wait_ge(sem("gah_ready"), m + 1)
                step(TT(hl[:, 0:4, t], bank[6 + m][:, :].rearrange("p (i n) -> p i n", i=4),
                        hh[:, 0:4, t].bitcast(fp), ALU.subtract))
            dve.nop().then_inc(sem("cat_a_ready"), 1)
            def shift(t0, t1, rows_):
                for t in range(t0, t1):
                    now = praw[0:rows_, t, 1:257]
                    d = dtmp[0:rows_, t % 4, :]
                    mu = v2T[0:rows_, v2["mu_shift_2"][0] + t:v2["mu_shift_2"][0] + t + 1]
                    step(TT(d, praw[0:rows_, t, 0:256], now, ALU.subtract))
                    step(STT(pm[0:rows_, t, :], d, mu, now, ALU.mult, ALU.add))

            def raw_in(name):
                pair_wait(name)

            dve.wait_ge(sem("praw_ready"), 4)
            for name in ("r", "k", "v", "lora"):
                raw_in(name)
            shift(12, 15, P)
            dve.nop().then_inc(sem("lora_mixed"), 1)
            shift(0, 12, P)
            prepare("c20")

            def col(name, j):
                c0 = v2[name][0] + j
                return v2T[:, c0:c0 + 1]

            rT, kT2, vT = pm[:, 0:4, :], pm[:, 4:8, :], pm[:, 8:12, :]
            for j in range(4):
                step(TS(kk[:, j, :], kT2[:, j, :], col("k_k_2", j), None, ALU.mult))
            step(TT(dtmp, kk, kk, ALU.mult))
            dve.nop().then_inc(sem("kk_squared"), 1)
            dve.wait_ge(sem("lwa_ready"), 8)
            step(TS(lw, lw, -math.exp(-0.5), None, ALU.mult))
            dve.wait_ge(sem("pads2"), 4)
            f = lambda t: t.rearrange("p j n -> p (j n)")
            step(dve.tensor_tensor_scan(f(cum), reset, f(lw), 0.0, ALU.mult, ALU.add))
            dve.nop().then_inc(sem("cum_ready"), 1)
            step(TT(lw, cum, lw, ALU.subtract))
            dve.nop().then_inc(sem("cum_ready"), 1)
            dve.wait_ge(sem("kk_len"), 1)
            step(TS(nrm[0:8, :], nrm[0:8, :], 1e-12, None, ALU.max))
            step(dve.reciprocal(nrm[0:8, :], nrm[0:8, :]))
            dve.nop().then_inc(sem("kk_inv"), 1)
            for j in range(4):
                step(TS(dtmp[:, j, :], av[:, j, :], 1.0, col("k_a_2", j), ALU.subtract, ALU.mult))
                step(STT(kT2[:, j, :], dtmp[:, j, :], 1.0, kT2[:, j, :], ALU.add, ALU.mult))
            for h in range(2):
                dve.wait_ge(sem("kk_spread"), h + 1)
                step(TT(kk[:, 2 * h:2 * h + 2, :], kk[:, 2 * h:2 * h + 2, :],
                        bank[4 + h][:, :].rearrange("p (t n) -> p t n", t=2), ALU.mult))
            dve.wait_ge(sem("dec_ready"), 3)
            ch = lambda t: t.rearrange("p j (c n) -> p j c n", c=NCH)
            for j in range(4):
                step(TT(aT_rT[:, j, :, 1, :], ch(rT)[:, j], ch(dec1)[:, j], ALU.mult))
                step(STT(aT_rT[:, j, :, 0, :], ch(kk)[:, j], -1.0, ch(dec2)[:, j], ALU.mult, ALU.mult))
            step(TT(bT, kk, av, ALU.mult))
            step(TT(bT, bT, lw, ALU.mult))
            step(TT(kTt, kT2, lw, ALU.mult))
            step(dve.tensor_copy(st[:, 212:228].rearrange("p (j c) -> p j c", j=4), ch(dec1)[:, :, :, L - 1]))
            for j in range(4):
                step(STT(dtmp[:, j, :], rT[:, j, :], col("r_k_2", j), kT2[:, j, :], ALU.mult, ALU.mult))
            dve.nop().then_inc(sem("tilde_ready"), 1)
            for h in range(2):
                dve.wait_ge(sem("bonus_summed"), h + 1)
                step(TT(bonus[:, 2 * h:2 * h + 2, :], vT[:, 2 * h:2 * h + 2, :],
                        bank[6 + h][:, :].rearrange("p (t n) -> p t n", t=2), ALU.mult))
            dve.nop().then_inc(sem("bonus_ready"), 1)
            dve.wait_ge(sem("tok_ready"), 6)

            def quad(b, w):
                return b[:, :].rearrange("p (q w n) -> p q w n", w=w, n=L) if w > 1 else \
                    b[:, :].rearrange("p (q n) -> p q n", n=L)

            ar = C("ar").rearrange("p (w n) -> p w n", w=2)

            def masked(dst, src, mask_name, n):
                return TT(dst, src, C(mask_name).unsqueeze(1).to_broadcast([P, n, L]), ALU.mult)

            for n, dst in enumerate((gB, gK)):
                for b in range(4):
                    dve.wait_ge(sem("gram_done"), 4 * n + b + 1)
                    for w in range(2):
                        step(TT(dst[:, 4 * b:4 * b + 4, w, :], quad(bank[4 + b], 2)[:, :, w, :],
                                ar[:, w, :].unsqueeze(1).to_broadcast([P, 4, L]), ALU.mult))
                    dve.nop().then_inc(sem("gram_ready"), 1)
            for h in range(2):
                dve.wait_ge(sem("gram_done"), 9 + h)
                step(masked(inv[5][:, 8 * h:8 * h + 8, :], quad(bank[4 + h], 1), "b8low", 8))
            eye = C("eye2").unsqueeze(1).to_broadcast([P, 16, L])
            S1, S1t, P2, P2t, P4, T2, T2t = inv
            step(masked(T2t, gB[:, :, 0, :], "b8", 16))
            step(TT(S1, T2, eye, ALU.add))
            step(TT(S1t, T2t, eye, ALU.add))
            dve.nop().then_inc(sem("inv_ready"), 2)

            def collect(n, dst, add):
                for h in range(2):
                    dve.wait_ge(sem("inv_done"), 2 * n + h + 1)
                    src = quad(bank[4 + 2 * (n % 2) + h], 1)
                    s = slice(8 * h, 8 * h + 8)
                    step(TT(dst[:, s, :], src, add[:, s, :], ALU.add) if add is not None
                         else dve.tensor_copy(dst[:, s, :], src))
                    dve.nop().then_inc(sem("inv_ready"), 1)

            collect(0, P2, None)
            collect(1, P2t, None)
            collect(2, T2, S1)
            collect(3, T2t, S1t)
            collect(4, P4, None)
            dve.wait_ge(sem("inv_done"), 10)
            step(masked(P2t, gB[:, :, 0, :], "o8", 16))
            collect(5, S1, T2)
            collect(6, S1t, T2t)
            n = 7
            cur, curt, nxt, nxtt = S1, S1t, T2, T2t
            for lvl, name in enumerate(("o16", "o32", None)):
                dve.nop().then_inc(sem("off_ready"), 1)
                collect(n, P2, None)
                if name:
                    step(masked(P2t, gB[:, :, 0, :], name, 16))
                collect(n + 1, nxtt, curt)
                n += 2
                if lvl < 2:
                    collect(n, nxt, cur)
                    n += 1
                cur, curt, nxt, nxtt = nxt, nxtt, cur, curt
            prepare("c21")

            dl = st[:, 212:228].rearrange("p (j c) -> p j c", j=4)
            for c in range(NCH - 1):
                dve.wait_ge(sem("m_done"), c + 1)
                dve.wait_ge(sem("yc_done"), c + 1)
                step(TT(ms, bank[6][:, 0:256].rearrange("p (j n) -> p j n", j=4), ms, ALU.add))
                step(TT(ms, ms, bcast(dl[:, :, c], L), ALU.mult))
                dve.nop().then_inc(sem("m_ready"), 1)
            dve.wait_ge(sem("yc_ready"), NCH)
            for h in range(2):
                dve.wait_ge(sem("ymean_done"), h + 1)
                step(STT(f(yT)[:, 512 * h:512 * h + 512], bank[4 + h][:, :], -1.0 / L, f(yT)[:, 512 * h:512 * h + 512],
                         ALU.mult, ALU.add))
            step(TT(dtmp, yT, yT, ALU.mult))
            dve.nop().then_inc(sem("ysq_ready"), 1)
            dve.wait_ge(sem("yvar_done"), 1)
            step(TS(nrm[0:8, :], bank[6][0:8, 0:256], 1.0 / L, GN_EPS, ALU.mult, ALU.add))
            step(dve.reciprocal(nrm[0:8, :], nrm[0:8, :]))
            dve.nop().then_inc(sem("yvar_ready"), 1)
            for h in range(2):
                dve.wait_ge(sem("ystd_spread"), h + 1)
                step(TT(yT[:, 2 * h:2 * h + 2, :], yT[:, 2 * h:2 * h + 2, :],
                        bank[4 + h][:, :].rearrange("p (t n) -> p t n", t=2), ALU.mult))
            for j in range(4):
                step(TS(yT[:, j, :], yT[:, j, :], col("lnx_g_2", j), col("lnx_b_2", j), ALU.mult, ALU.add))
            step(TT(yT, yT, bonus, ALU.add))
            dve.wait_ge(sem("gm_ready"), 2)
            step(TT(yT, yT, gmT, ALU.mult))
            dve.nop().then_inc(sem("yb_ready"), 1)
            dve.wait_ge(sem("ybh_ready"), 1)
            TT(hl[:, 4:8, :], yT, hh[:, 4:8, :].bitcast(fp), ALU.subtract).then_inc(sem("yb_split"), 1)

            def post_ln(banks):
                for m in range(MT):
                    for h in range(2):
                        step(TT(xn[:, 1024 + 512 * h:1536 + 512 * h], banks[m][h][:, :],
                                gg[:, 512 * h:512 * h + 512], ALU.mult))
                    step(STT(xt[:, m, :], xt[:, m, :], ALPHA, xn[:, 1024:2048], ALU.mult, ALU.add))

            collect_piece(20)
            collect_piece(21)
            prepare("wo2")
            prepare("wo3")
            w0, w1 = item("wo2"), item("wo3")
            post_ln([(w0[0], w1[0]), (w0[1], w1[1])])
            for name in ("wo2", "wo3"):
                dve.nop().then_inc(sem(f"pair{place[name][0] % 2}_free"), 1)
            prepare("gf0")
            dve.wait_ge(sem("spread3"), 64)
            for m in layer_norm(6, bc[:, 0, :], bc[:, 1, :]):
                dve.nop().then_inc(sem("ln1_done"), 1)
            scale_h(3)
            feed_forward("gf", "dn2", 1, 22, None)
            dve.wait_ge(sem("blocks_done"), place["dn2"][2])
            post_ln([(bank[4], bank[5]), (bank[6], bank[7])])
            for m in layer_norm(7, bc[:, 2, :], bc[:, 3, :]):
                dve.nop().then_inc(sem("y_out"), 1)

        @block.tensor
        def _(pe):
            mm = nc.tensor.matmul
            tr = nc.tensor.transpose

            def start_item(name):
                pair, _, _ = place[name]
                if pair >= 2:
                    pe.wait_ge(sem(f"pair{pair % 2}_free"), pair // 2)
                return bank[2 * (pair % 2)], bank[2 * (pair % 2) + 1]

            def weights(g):
                b = [o[6] for o in order].index(g)
                _, i, nk, width, _, _, _ = order[b]
                pe.wait_ge(sem("block_ready"), b + 1)
                return i, nk, cut(whi, g % HL, nk, width), cut(wlo, g % HL, nk, width)

            def piece(a):
                b0, _ = start_item(f"c{a}")
                pe.wait_ge(sem("acc_ready"), a + 1)
                if a in GATES:
                    last = mm(b0[:, :], C("ones"), acc[:, a % 2, :], start=True, stop=True)
                else:
                    for t in range(4):
                        last = mm(b0[:, t:t + 1], acc[:, a % 2, t * P:(t + 1) * P], C("ones")[:, 0:1],
                                  start=True, stop=True)
                last.then_inc(sem("piece_done"), 1)

            def tokens_out(name, n, src, extra=None):
                banks = start_item(name)
                xh, xl = src
                _, g0, g1 = place[name]
                for g in range(g0, g1):
                    i, nk, wh, wl = weights(g)
                    for dsts, c0, cn in ([([bank[4][:, 0:8], bank[5][:, 0:8]], extra, 8)] if extra else []) + \
                            [([banks[0][:, 0:n], banks[1][:, 0:n]], 0, n)]:
                        for m in range(MT):
                            t = slice(m * P, (m + 1) * P)
                            for k in range(nk):
                                kk_ = nk * i + k
                                first, end = g == g0 and k == 0, g == g1 - 1 and k == nk - 1
                                c = slice(c0, c0 + cn)
                                mm(dsts[m], xh[:, kk_, t], wh[:, k, c], start=first, stop=False)
                                mm(dsts[m], xh[:, kk_, t], wl[:, k, c], start=False, stop=False)
                                last = mm(dsts[m], xl[:, kk_, t], wh[:, k, c], start=False, stop=end)
                    last.then_inc(sem("blocks_done"), 1)

            def features_out(name, cols, src):
                banks = start_item(name)
                xh, xl = src
                _, g0, g1 = place[name]
                for g in range(g0, g1):
                    i, nk, wh, wl = weights(g)
                    for t, c0 in enumerate(cols):
                        o = banks[t // 2][:, 256 * (t % 2):256 * (t % 2) + 256]
                        in_bank = [x for x in range(len(cols)) if x // 2 == t // 2]
                        for k in range(nk):
                            kk_ = nk * i + k
                            first = g == g0 and k == 0 and t == in_bank[0]
                            end = g == g1 - 1 and k == nk - 1 and t == in_bank[-1]
                            c = slice(c0, c0 + P)
                            mm(o, wh[:, k, c], xh[:, kk_, :], start=first, stop=False)
                            mm(o, wh[:, k, c], xl[:, kk_, :], start=False, stop=False)
                            last = mm(o, wl[:, k, c], xh[:, kk_, :], start=False, stop=end)
                    last.then_inc(sem("blocks_done"), 1)

            def turn_h(src):
                for k in range(8):
                    for m in range(MT):
                        last = tr(bank[4 + k // 2][:, 256 * (k % 2) + P * m:256 * (k % 2) + P * m + P],
                                  src(m)[:, k * P:(k + 1) * P], ident)
                    if k % 2:
                        last.then_inc(sem("hx_turned"), 1)

            four = [0, P, 2 * P, 3 * P]
            modulated = (hh, hl)
            pe.wait_ge(sem("const_in"), 16)
            pe.wait_ge(sem("vec0_in"), 16 * len(ROWS1))
            tr(bank[4][:, 0:n1], vraw[0:n1, 0, :], ident[0:n1, 0:n1]).then_inc(sem("vec_turned"), 1)
            pe.wait_ge(sem("vec1_in"), 16 * (len(ROWS2) + 1))
            tr(bank[5][:, 0:n2], vraw[0:n2, 1, :], ident[0:n2, 0:n2]).then_inc(sem("vec_turned"), 1)
            pe.wait_ge(sem("xn_ready"), 2)
            turn_h(lambda m: xn[:, m * D:(m + 1) * D])
            for a in range(4):
                piece(a)
            pe.wait_ge(sem("h_ready"), 2)
            tokens_out("o_if", 512, modulated, extra=512)
            features_out("qm", four, modulated)
            features_out("km", four, modulated)
            pe.wait_ge(sem("if_ready"), 2)
            for w in range(2):
                for m in range(MT):
                    last = tr(bank[7][0:4, 256 * w + P * m:256 * w + P * m + P],
                              st[:, 240 + 8 * m + 4 * w:244 + 8 * m + 4 * w], ident)
            last.then_inc(sem("if_turned"), 1)
            piece(4)
            tokens_out("vm", 512, modulated)
            piece(5)
            tokens_out("qa", 512, modulated)
            piece(6)
            tokens_out("kva", 256, modulated)
            piece(7)
            pe.wait_ge(sem("rows_exp"), 4)
            for m in range(MT):
                for q, r in enumerate((0, 4, 5, 6)):
                    tr(bank[7][:, 16 * m + 4 * q:16 * m + 4 * q + 4], rows[0:4, r, m * P:(m + 1) * P], ident[0:4, 0:4])
            for h in range(HM):
                last = mm(bank[7][:, 32 + 4 * h:36 + 4 * h], ident[0:4, h:h + 1].to_broadcast([4, P]), rows[0:4, 2, 16:20],
                          start=True, stop=True)
            last.then_inc(sem("cols_turned"), 1)
            for h2 in range(2):
                for h in range(2):
                    last = mm(bank[4 + h2][:, 256 * h:256 * h + 256], ident[0:4, 2 * h2 + h:2 * h2 + h + 1].to_broadcast([4, P]),
                              rows[0:4, 7, :], start=True, stop=True)
                last.then_inc(sem("bm_spread"), 1)
            features_out("g0", four, modulated)
            piece(8)
            pe.wait_ge(sem("k_scaled"), 1)
            pe.wait_ge(sem("arg_ready"), 1)
            for m in range(MT):
                for h in range(HM):
                    last = tr(bank[4 + m][:, h * P:(h + 1) * P], qk[:, 4 + h, m * P:(m + 1) * P], ident)
                last.then_inc(sem("kc_turned"), 1)
            for h2 in range(2):
                for h in range(2):
                    for m in range(MT):
                        t = slice(m * P, (m + 1) * P)
                        last = mm(bank[6 + h2][:, 256 * h + P * m:256 * h + P * m + P], qk[:, 4 + 2 * h2 + h, t],
                                  qk[:, 2 * h2 + h, t], start=True, stop=True)
                last.then_inc(sem("ms_done"), 1)
            features_out("g1", four, modulated)
            piece(9)
            pe.wait_ge(sem("kw_ready"), 2)
            pe.wait_ge(sem(f"pair{place['vm'][0] % 2}_free"), place["vm"][0] // 2 + 1)
            pe.wait_ge(sem("v_ready"), 1)
            pe.wait_ge(sem("pads"), 3)
            pe.wait_ge(sem("sw_ready"), 2)
            for c in range(NCH - 1):
                rows_ = slice(L * (c % 2), L * (c % 2) + L)
                for h2 in range(2):
                    if c == 2:
                        pe.wait_ge(sem("state_ready"), h2 + 1)
                    for h in range(2 * h2, 2 * h2 + 2):
                        last = mm(bank[4 + 2 * (c % 2) + h2][:, 129 * (h % 2):129 * (h % 2) + 129],
                                  kw[rows_, c // 2, h, :], vaug[rows_, c // 2, h, :], start=True, stop=True)
                    last.then_inc(sem("kv_done"), 1)
            features_out("g2", four, modulated)
            pe.wait_ge(sem("state_ready"), 6)
            for m in range(MT):
                pe.wait_ge(sem("qr_ready"), m + 1)
                for i in range(4):
                    last = tr(bank[4 + m][:, i * P:(i + 1) * P], qr[:, m, i * P:(i + 1) * P], ident)
                last.then_inc(sem("qr_turned"), 1)
            pe.wait_ge(sem("qr_ready"), 4)
            for m in range(MT):
                last = tr(bank[6][:, m * P:(m + 1) * P], kr[:, m, :], ident)
            last.then_inc(sem("qr_turned"), 1)
            pe.wait_ge(sem("qT_ready"), 3)

            def scores(m, h, b, at, n):
                g, i = h // 4, h % 4
                half = slice(64 * g, 64 * g + 64)
                return mm(b[:, at:at + n], qT[half, i, m * P:(m + 1) * P], kT[half, S - n if m else 0:S if m else n],
                          start=True, stop=True)

            for b in range(2):
                for h in range(4):
                    last = scores(0, 4 * b + h, bank[4 + b], 128 * h, 128)
                last.then_inc(sem("s_done"), 1)
            for b in range(4):
                if b >= 2:
                    pe.wait_ge(sem("s_masked"), b - 1)
                for h in range(2):
                    last = scores(1, 2 * b + h, bank[(6, 7, 4, 5)[b]], 256 * h, 256)
                last.then_inc(sem("s_done"), 1)
            features_out("g3", four, modulated)
            for n in range(6):
                m = 0 if n < 2 else 1
                pe.wait_ge(sem("s_masked"), 6)
                pe.wait_ge(sem("exp_ready"), 9 * m + 9)
                if n >= 4:
                    pe.wait_ge(sem("pT_ready"), n - 3)
                for q in range(4):
                    if m == 0:
                        src = sm0[:, 4 * n + q, :]
                    else:
                        idx = 4 * (n - 2) + q
                        src = sm1[:, idx // 2, P * (idx % 2):P * (idx % 2) + P]
                    last = tr(bank[4 + n % 4][:, q * P:(q + 1) * P], src, ident)
                last.then_inc(sem("p_turned"), 1)
            pe.wait_ge(sem("pT_ready"), 6)
            pe.wait_ge(sem("va_ready"), 2)
            for h in range(HQ):
                g = h // 4
                last = mm(bank[6][:, 64 * h:64 * h + 64], pT[:, h, :], va[:, 0, 64 * g:64 * g + 64],
                          start=True, stop=True)
            last.then_inc(sem("o_done"), 1)
            for h in range(HQ):
                g = h // 4
                for kb in range(2):
                    last = mm(bank[7][:, 64 * h:64 * h + 64], pT[:, 8 + 2 * h + kb, :], va[:, kb, 64 * g:64 * g + 64],
                              start=(kb == 0), stop=(kb == 1))
            last.then_inc(sem("o_done"), 1)
            for m in range(MT):
                for h2 in range(2):
                    if m:
                        pe.wait_ge(sem("intra_ready"), h2 + 1)
                    for h in range(2 * h2, 2 * h2 + 2):
                        last = mm(bank[4 + h2][:, 129 * (h % 2):129 * (h % 2) + 129], sw[:, h, m, :],
                                  vaug[:, m, h, :], start=True, stop=True)
                    last.then_inc(sem("intra_done"), 1)
                if m == 0:
                    pe.wait_ge(sem("ya_ready"), 2)
                for h2 in range(2):
                    if m:
                        pe.wait_ge(sem("inter_used"), h2 + 1)
                    for h in range(2 * h2, 2 * h2 + 2):
                        for half in range(2):
                            c = 2 * m + half
                            last = mm(bank[6 + h2][L * half:L * half + L, 129 * (h % 2):129 * (h % 2) + 129],
                                      qk[:, h, c * L:(c + 1) * L], cstate[:, c, h, :], start=True, stop=True)
                    last.then_inc(sem("inter_done"), 1)
            pe.wait_ge(sem("intra_ready"), 4)
            for m in range(MT):
                for i in range(4):
                    last = tr(bank[4 + m][:, i * P:(i + 1) * P], ya[:, m, i * P:(i + 1) * P], ident)
                last.then_inc(sem("ya_turned"), 1)
            pe.wait_ge(sem("inter_used"), 4)
            for m in range(MT):
                pe.wait_ge(sem("ym_ready"), m + 1)
                for i in range(4):
                    last = tr(bank[6 + m][:, i * P:(i + 1) * P], ym[:, m, i * P:(i + 1) * P], ident)
                last.then_inc(sem("ym_turned"), 1)
            pe.wait_ge(sem("ya_split"), 2)
            features_out("ba0", four, (yah, yal))
            features_out("ba1", four, (yah, yal))
            pe.wait_ge(sem("ym_split"), 2)
            features_out("bm0", four, (ymh, yml))
            features_out("bm1", four, (ymh, yml))

            pe.wait_ge(sem("merged_ready"), 2)
            tokens_out("wo0", 512, merged)
            tokens_out("wo1", 512, merged)
            pe.wait_ge(sem("xn_ready"), 4)
            turn_h(lambda m: xn[:, m * D:(m + 1) * D])

            def feed_forward(letter, down, n):
                names = [x for x, _ in ITEMS]
                pe.wait_ge(sem("h_ready"), 4 + 4 * n)
                for j in range(FT // 2):
                    name = f"{letter}{j}"
                    features_out(name, four, modulated)
                    if names[names.index(name) + 1][0] == "c":
                        piece(int(names[names.index(name) + 1][1:]))
                for g in range(*place[down][1:]):
                    i, nk, wh, wl = weights(g)
                    for k in range(nk):
                        t = nk * i + k
                        pe.wait_ge(sem("ff_ready"), n * (FT // 2) + t // 2 + 1)
                        for m in range(MT):
                            x = slice(m * P, (m + 1) * P)
                            for c in range(2):
                                o, cs = bank[4 + 2 * m + c][:, :], slice(512 * c, 512 * c + 512)
                                mm(o, ffh[:, t, x], wh[:, k, cs], start=(t == 0), stop=False)
                                mm(o, ffh[:, t, x], wl[:, k, cs], start=False, stop=False)
                                last = mm(o, ffl[:, t, x], wh[:, k, cs], start=False, stop=(t == FT - 1))
                    last.then_inc(sem("blocks_done"), 1)

            feed_forward("ff", "dn1", 0)
            pe.wait_ge(sem("emb_done"), 2)
            turn_h(lambda m: xt[:, m, :])
            pe.wait_ge(sem("h_ready"), 6)
            tokens_out("pu", 512, modulated)
            tokens_out("pv", 512, modulated)
            pe.wait_ge(sem("ws_in"), 16)
            for g in range(4):
                last = tr(bank[4][:, g * P:(g + 1) * P], wsr[:, g, :], ident)
            last.then_inc(sem("ws_turned"), 1)
            features_out("r", four, modulated)
            features_out("k", four, modulated)
            features_out("v", four, modulated)
            features_out("lora", [0, P, 288 - P], modulated)
            pe.wait_ge(sem("wsT_ready"), 1)
            for m in range(MT):
                pe.wait_ge(sem("gv_ready"), m + 1)
                for g in range(4):
                    last = mm(bank[4 + m][:, g * P:(g + 1) * P], wsT[:, g, :], gv[:, m, g * P:(g + 1) * P],
                              start=True, stop=True)
                last.then_inc(sem("sg_done"), 1)
            for m in range(MT):
                pe.wait_ge(sem("ga_ready"), m + 1)
                for i in range(4):
                    last = tr(bank[6 + m][:, i * P:(i + 1) * P], gu[:, m, i * P:(i + 1) * P], ident)
                last.then_inc(sem("ga_turned"), 1)
            pe.wait_ge(sem("cat_a_ready"), 1)
            pe.wait_ge(sem("lora_in"), 64)
            pe.wait_ge(sem("lora_act"), 3)
            for n, half in enumerate((slice(0, 64), slice(64, 128))):
                for j in range(4):
                    last = mm(bank[4 + 2 * n + j // 2][:, 256 * (j % 2):256 * (j % 2) + 256],
                              lup[half, j * P:(j + 1) * P], pm[half, 12, :], start=True, stop=True)
                    if j % 2:
                        last.then_inc(sem("lora_done"), 1)
            for j in range(4):
                if j % 2 == 0:
                    pe.wait_ge(sem("lwa_ready"), j + 2)
                o = bank[4 + j // 2][:, 256 * (j % 2):256 * (j % 2) + 256]
                mm(o, gu0[:, j * P:(j + 1) * P], pm[:, 13, :], start=True, stop=False)
                last = mm(o, gu1[96:128, j * P:(j + 1) * P], pm[96:128, 14, :], start=False, stop=True)
                if j % 2:
                    last.then_inc(sem("lora_done"), 1)
            heads = C("heads").rearrange("p (j n) -> p j n", j=4)

            def head_sums(src, dst, s):
                for j in range(4):
                    last = mm(dst, heads[:, j, :], src[:, j, :], start=(j == 0), stop=(j == 3))
                last.then_inc(s, 1)

            def head_spread(s):
                for j in range(4):
                    for g in range(2):
                        last = mm(bank[4 + j // 2][L * g:L * g + L, 256 * (j % 2):256 * (j % 2) + 256],
                                  ident[0:8, 2 * j + g:2 * j + g + 1].to_broadcast([8, L]), nrm[0:8, :],
                                  start=True, stop=True)
                    if j % 2:
                        last.then_inc(s, 1)

            pe.wait_ge(sem("kk_squared"), 1)
            pe.wait_ge(sem("lwa_ready"), 8)
            head_sums(dtmp, bank[6][0:8, 0:256], sem("kk_summed"))
            pe.wait_ge(sem("kk_inv"), 1)
            pe.wait_ge(sem("gm_ready"), 2)
            head_spread(sem("kk_spread"))
            pe.wait_ge(sem("tilde_ready"), 1)
            for j in range(4):
                last = mm(bank[6 + j // 2][:, 256 * (j % 2):256 * (j % 2) + 256], C("pairs"), dtmp[:, j, :],
                          start=True, stop=True)
                if j % 2:
                    last.then_inc(sem("bonus_summed"), 1)
            eye2 = C("eye2")
            half = (slice(0, 64), slice(64, 128))

            def each(q0, q1):
                for q in range(q0, q1):
                    for g in range(2):
                        yield q, q // 4, q % 4, half[g]

            pe.wait_ge(sem("bonus_ready"), 1)
            for n, src in enumerate((bT, kTt, pm[:, 8:12, :])):
                for h in range(2):
                    i = 2 * n + h
                    if i >= 4:
                        pe.wait_ge(sem("tok_ready"), i - 3)
                    for q, c, j, r in each(8 * h, 8 * h + 8):
                        last = mm(bank[4 + i % 4][r, L * (q % 8):L * (q % 8) + L], src[r, j, c * L:(c + 1) * L],
                                  eye2[r, :], start=True, stop=True)
                    last.then_inc(sem("tok_turned"), 1)
            pe.wait_ge(sem("tok_ready"), 6)
            for n, src in enumerate((bT, kTt)):
                for b in range(4):
                    if n:
                        pe.wait_ge(sem("gram_ready"), b + 1)
                    for q, c, j, r in each(4 * b, 4 * b + 4):
                        last = mm(bank[4 + b][r, 2 * L * (q % 4):2 * L * (q % 4) + 2 * L],
                                  src[r, j, c * L:(c + 1) * L],
                                  aT_rT[r, j, c, :, :].rearrange("p w n -> p (w n)"), start=True, stop=True)
                    last.then_inc(sem("gram_done"), 1)
            for h in range(2):
                pe.wait_ge(sem("gram_ready"), 5 + h)
                for q, c, j, r in each(8 * h, 8 * h + 8):
                    last = mm(bank[4 + h][r, L * (q % 8):L * (q % 8) + L], aT_rT[r, j, c, 0, :],
                              bT[r, j, c * L:(c + 1) * L], start=True, stop=True)
                last.then_inc(sem("gram_done"), 1)
            S1, S1t, P2, P2t, P4, T2, T2t = inv

            def product(n, lhsT, rhs, ready):
                for h in range(2):
                    pe.wait_ge(sem("inv_ready"), ready + h)
                    for q, c, j, r in each(8 * h, 8 * h + 8):
                        last = mm(bank[4 + 2 * (n % 2) + h][r, L * (q % 8):L * (q % 8) + L], lhsT[r, q, :],
                                  rhs[r, q, :], start=True, stop=True)
                    last.then_inc(sem("inv_done"), 1)

            done = lambda n: 2 + 2 * n + 1
            pe.wait_ge(sem("gram_ready"), 8)
            product(0, T2t, T2, 1)
            product(1, T2, T2t, 1)
            product(2, S1t, P2, done(0))
            product(3, P2, S1t, done(1))
            product(4, P2t, P2, done(2))
            product(5, T2t, P4, done(4))
            product(6, P4, T2t, done(4))
            n = 7
            cur, curt, nxt, nxtt = S1, S1t, T2, T2t
            for lvl in range(3):
                pe.wait_ge(sem("off_ready"), lvl + 1)
                product(n, P2t, cur, done(n - 1))
                product(n + 1, P2, curt, done(n))
                n += 2
                if lvl < 2:
                    product(n, curt, P2, done(n - 1))
                    n += 1
                cur, curt, nxt, nxtt = nxt, nxtt, cur, curt
            solve = curt
            pe.wait_ge(sem("inv_ready"), done(n - 1) + 1)
            pe.wait_ge(sem("pads2"), 4)
            for c in range(NCH):
                if c:
                    pe.wait_ge(sem("m_ready"), c)
                for q, _, j, r in each(4 * c, 4 * c + 4):
                    mm(bank[4][r, L * j:L * j + L], aT_rT[r, j, c, 0, :], ms[r, j, :], start=True, stop=False)
                    last = mm(bank[4][r, L * j:L * j + L], gK[r, q, 0, :], vtok[r, q, :], start=False, stop=True)
                last.then_inc(sem("x_done"), 1)
                pe.wait_ge(sem("x_ready"), c + 1)
                for q, _, j, r in each(4 * c, 4 * c + 4):
                    last = mm(bank[5][r, L * j:L * j + L], solve[r, q, :], xs[r, j, :], start=True, stop=True)
                last.then_inc(sem("u_done"), 1)
                pe.wait_ge(sem("u_ready"), c + 1)
                if c < NCH - 1:
                    for q, _, j, r in each(4 * c, 4 * c + 4):
                        mm(bank[6][r, L * j:L * j + L], btok[r, q, :], us[r, j, :], start=True, stop=False)
                        last = mm(bank[6][r, L * j:L * j + L], ktok[r, q, :], vtok[r, q, :], start=False, stop=True)
                    last.then_inc(sem("m_done"), 1)
                if c:
                    pe.wait_ge(sem("yc_ready"), c)
                for q, _, j, r in each(4 * c, 4 * c + 4):
                    o = bank[7][r, L * j:L * j + L]
                    mm(o, ms[r, j, :], aT_rT[r, j, c, 1, :], start=True, stop=False)
                    mm(o, us[r, j, :], gB[r, q, 1, :], start=False, stop=False)
                    last = mm(o, vtok[r, q, :], gK[r, q, 1, :], start=False, stop=True)
                last.then_inc(sem("yc_done"), 1)
            pe.wait_ge(sem("yc_ready"), NCH)
            for j in range(4):
                last = mm(bank[4 + j // 2][:, 256 * (j % 2):256 * (j % 2) + 256], C("pairs"), yT[:, j, :],
                          start=True, stop=True)
                if j % 2:
                    last.then_inc(sem("ymean_done"), 1)
            pe.wait_ge(sem("ysq_ready"), 1)
            head_sums(dtmp, bank[6][0:8, 0:256], sem("yvar_done"))
            pe.wait_ge(sem("ystd_ready"), 1)
            head_spread(sem("ystd_spread"))
            piece(20)
            piece(21)
            pe.wait_ge(sem("yb_split"), 1)
            tokens_out("wo2", 512, cat)
            tokens_out("wo3", 512, cat)
            pe.wait_ge(sem("ln1_done"), 2)
            turn_h(lambda m: xt[:, m, :])
            feed_forward("gf", "dn2", 1)


_INS = ["x", "c", "positions", "w_ada", "b_ada", "g_pre_mix", "g_post_mix", "w_in", "b_if", "conv_w", "conv_b",
        "attn_sinks", "mlstm_norm_w", "w_branch_attn", "w_branch_mlstm", "w_out", "g_pre_ffn", "g_post_ffn",
        "w_ffn_gate", "w_ffn_up", "w_ffn_down", "c_2", "emb_ln_g_2", "emb_ln_b_2", "w_ada_2", "b_ada_2", "w_in_2",
        "mu_shift_2", "sg_ln_g_2", "sg_ln_b_2", "w_s_2", "b_s_2", "w0_2", "w_up_2", "a0_2", "a_up_2", "g_up_2",
        "k_k_2", "k_a_2", "r_k_2", "lnx_g_2", "lnx_b_2", "w_out_2", "ln1_g_2", "ln1_b_2", "w_ffn_in_2",
        "w_ffn_out_2", "ln2_g_2", "ln2_b_2"]


def kernel(**inputs):
    import numpy as _np
    import concourse.bacc as _bacc
    from concourse import mybir as _mybir
    from concourse.bass_utils import run_bass_kernel_spmd as _run

    nc = _bacc.Bacc("TRN2", target_bir_lowering=False, num_devices=1)
    arrays, args = {}, {}
    const = constants()
    for name in _INS + ["const"]:
        a = const if name == "const" else _np.ascontiguousarray(inputs[name])
        arrays[f"in_{name}"] = a
        args[name] = nc.dram_tensor(f"in_{name}", a.shape, _mybir.dt.from_np(a.dtype), kind="ExternalInput").ap()
    out = nc.dram_tensor("out_dram", (1, S, D), _mybir.dt.float32, kind="ExternalOutput").ap()
    build(nc, args, out)
    r = _run(nc, [arrays], core_ids=[0])
    return r.results[0]["out_dram"]
```

```python
import math
import numpy as np
import concourse.bass as bass
from concourse import mybir
from contextlib import ExitStack

S = 256
D = 1024
P = 128
MT = S // P
KT = D // P
FF = 2816
FT = FF // P
HQ, HG, DH = 8, 2, 64
HM, DM = 4, 128
L = 64
NCH = S // L
SLOT = 2 * 520
RAW = 6
HL = 4
NEG = -1e30
EPS = 1e-6
LN_EPS = 1e-5
GN_EPS = 64e-5
ALPHA = 2 ** 0.25
TWO_PI_1 = 6.28125
TWO_PI_2 = float(np.float32(np.frombuffer(np.uint32(
    np.float32(2 * math.pi - TWO_PI_1).view(np.uint32) & 0xFFFFF000).tobytes(), np.float32)[0]))
TWO_PI_3 = float(np.float32(2 * math.pi - TWO_PI_1 - TWO_PI_2))
ROUND = 12582912.0
SIN_MAX = 3.1415925

CONST = {}
_at = 0
for _name, _n in (("ident", 128), ("attn", 256), ("chunk_t", 128), ("ws", 128), ("ar", 128), ("low", 64),
                  ("b4", 64), ("o4", 64), ("o8", 64), ("o16", 64), ("o32", 64), ("eye2", 64), ("pairs", 128),
                  ("heads", 32), ("ones", 128), ("freq", 32), ("b4low", 64)):
    CONST[_name] = (_at, _at + _n)
    _at += _n
CONST_N = _at


def constants():
    p = np.arange(P)[:, None]
    f = np.arange(P)[None, :]
    c = np.zeros((P, CONST_N), np.float32)

    def put(name, v):
        a, b = CONST[name]
        c[:, a:b] = v

    q, k = np.arange(P)[:, None], np.arange(2 * P)[None, :]
    rel = k - P
    h = p % L
    g = np.arange(L)[None, :]
    same = lambda n: (h // n == g // n)
    put("ident", np.eye(P))
    put("attn", np.where((rel <= q) & (q - rel < P), 0.0, NEG))
    put("chunk_t", np.where((p // L == f // L) & (p <= f), 0.0, NEG))
    put("ws", p <= f)
    put("ar", np.concatenate([h < g, h <= g], axis=1))
    put("low", g < h)
    put("b4", same(4))
    put("b4low", same(4) & (g < h))
    put("o4", same(8) & ~same(4))
    put("o8", same(16) & ~same(8))
    put("o16", same(32) & ~same(16))
    put("o32", ~same(32))
    put("eye2", h == g)
    put("pairs", p // L == f // L)
    heads = np.zeros((P, 4, 8))
    for j in range(4):
        heads[:L, j, 2 * j] = 1
        heads[L:, j, 2 * j + 1] = 1
    put("heads", heads.reshape(P, 32))
    put("ones", 1.0)
    put("freq", np.float32(10000.0) ** (np.float32(-2.0) * np.arange(32, dtype=np.float32) / np.float32(64)))
    return c


ROWS1 = (("g_pre_mix", 8), ("g_pre_ffn", 8), ("conv_w", 32), ("conv_b", 8))
ROWS2 = (("mu_shift_2", 15), ("w0_2", 4), ("a0_2", 4), ("k_k_2", 4), ("k_a_2", 4),
         ("r_k_2", 4), ("lnx_g_2", 4), ("lnx_b_2", 4), ("b_s_2", 4))


def first_rows(rows):
    at, out = 0, {}
    for name, n in rows:
        out[name] = (at, at + n)
        at += n
    return out, at


def stream():
    head = ["c0", "c1", "c2", "c3", "o_if", "qm", "km", "vm", "qa", "c4", "kva", "c5", "g0", "c6", "g1",
            "c7", "g2", "c8", "g3", "c9", "ba0", "ba1", "bm0", "bm1", "wo0", "wo1"]
    first = [x for j in range(FT // 2) for x in ([f"ff{j}"] + ([f"c{10 + j // 2}"] if j % 2 else []))]
    first += [x for i in range(FT // 2) for x in ([f"dA{i}"] + ([f"c{15 + i // 3}"] if i in (1, 4, 7) else []))]
    middle = ["r", "c18", "k", "c19", "v", "lora", "pu", "pv", "c20", "c21", "wo2", "wo3"]
    second = [x for j in range(FT // 2) for x in ([f"gf{j}"] + ([f"c{18 + j}"] if j in (4, 5) else []))]
    second += [f"dB{i}" for i in range(FT // 2)]
    return head + first + middle + second


PIECES = [(0, 512 * i) for i in (0, 1, 2, 3, 6, 7, 8, 9, 4, 5, 10, 11)] + \
         [(1, 512 * i) for i in (0, 1, 2, 3, 6, 7, 8, 9, 4, 5, 10, 11)]
GATES = (8, 9, 10, 11, 20, 21, 22, 23)


ITEMS = stream()


def build(nc, A, out):
    fp = mybir.dt.float32
    ALU = mybir.AluOpType
    ACT = mybir.ActivationFunctionType
    AX = mybir.AxisListType.X
    ctx = ExitStack()
    with ctx:
        sems = {}

        def sem(name):
            if name not in sems:
                sems[name] = ctx.enter_context(nc.semaphore(name))
            return sems[name]

        def sb(name, shape):
            return ctx.enter_context(nc.sbuf_tensor(name, shape, fp))

        fr = mybir.dt.float32r

        ARENA = 20496
        arena_at = -(-nc.sbuf_base // 32) * 32
        arena = sb("arena", [P, ARENA])
        hreg = sb("hreg", [P, 4096])

        def rounded(name, at, shape):
            return nc.alloc_sbuf_tensor_at(name, [P] + shape, fr, offset=arena_at + 4 * at)

        hh = rounded("hh", ARENA, [KT, S])
        hl = rounded("hl", ARENA + 2048, [KT, S])
        raw = sb("raw", [P, RAW, SLOT])
        whi = ctx.enter_context(nc.sbuf_tensor("whi", [P, HL, SLOT], fr))
        wlo = ctx.enter_context(nc.sbuf_tensor("wlo", [P, HL, SLOT], fr))
        acc = sb("acc", [P, 2, 512])
        xt = sb("xt", [P, MT, D])
        xn = sb("xn", [P, MT * D])
        bc = sb("bc", [P, 4, D])
        bcs = sb("bcs", [P, 3, 512])
        bsm = sb("bsm", [P, 16])
        gg = sb("gg", [P, D])
        cst = sb("cst", [P, CONST_N])
        vraw = hreg[:, 0:256].rearrange("p (i n) -> p i n", i=2)
        v1, n1 = first_rows(ROWS1)
        v2, n2 = first_rows(ROWS2)
        v1T = sb("v1T", [P, n1])
        v2T = sb("v2T", [P, n2])
        modT = sb("modT", [P, 2, 48])
        gain = sb("gain", [P, 4, 8])
        cc = sb("cc", [P, 2, 8])
        st = sb("st", [P, 256])
        posi = ctx.enter_context(nc.sbuf_tensor("posi", [P, MT], mybir.dt.int32))

        def C(name):
            a, b = CONST[name]
            return cst[:, a:b]

        ident = C("ident")

        def region(at, n):
            assert at + n <= ARENA, (at, n)
            return arena[:, at:at + n]

        pos = [0]

        def take(n):
            pos[0] += n
            return region(pos[0] - n, n)

        conv_in = take(8 * 259).rearrange("p (t n) -> p t n", t=8)
        rope_a = take(640)
        rope_b = take(640)
        pT = region(0, 24 * 128).rearrange("p (t n) -> p t n", t=24)
        qk = take(8 * S).rearrange("p (t n) -> p t n", t=8)
        qr = take(MT * 512).rearrange("p (m n) -> p m n", m=MT)
        ya = qr
        kr = take(MT * 128).rearrange("p (m n) -> p m n", m=MT)
        va = take(MT * 128).rearrange("p (m n) -> p m n", m=MT)
        qT = take(4 * S).rearrange("p (i n) -> p i n", i=4)
        yah, yal = rounded("yah", ARENA, [4, S]), rounded("yal", ARENA + 1024, [4, S])
        ymh, yml = rounded("ymh", ARENA + 2048, [4, S]), rounded("yml", ARENA + 3072, [4, S])
        kT = take(S)
        sm0 = take(8 * 128).rearrange("p (h n) -> p h n", h=8)
        sm1 = xn[:, :].rearrange("p (h n) -> p h n", h=8)
        vaug = take(MT * HM * 129).rearrange("p (m h n) -> p m h n", m=MT, h=HM)
        osig = take(MT * 512).rearrange("p (m n) -> p m n", m=MT)
        ym = osig
        resets = gg[:, 0:512].rearrange("p (r n) -> p r n", r=2)
        rows = xn[:, :].rearrange("p (r n) -> p r n", r=8)
        wT = bc[:, 2, :].rearrange("p (h m n) -> p h m n", h=HM, m=MT)
        sw = bc[:, 3, :].rearrange("p (h m n) -> p h m n", h=HM, m=MT)
        kw = take(MT * 512).rearrange("p (m h n) -> p m h n", m=MT, h=HM)
        cstate = take(NCH * HM * 129).rearrange("p (c h n) -> p c h n", c=NCH, h=HM)
        merged = (rounded("mgh", 0, [KT, S]), rounded("mgl", 2048, [KT, S]))
        intra = take(MT * HM * 129).rearrange("p (m h n) -> p m h n", m=MT, h=HM)
        gT = take(16 * S).rearrange("p (t n) -> p t n", t=16)
        rsc = gg[:, 512:768].rearrange("p (w m f c) -> p w m f c", w=2, m=MT, f=2)
        cossin = gg[:, 768:896].rearrange("p (m f c) -> p m f c", m=MT, f=2)
        ffh, ffl = rounded("ffh", 0, [FT, S]), rounded("ffl", FT * S, [FT, S])
        sil = region(2 * FT * S, 2 * 512).rearrange("p (b n) -> p b n", b=2)
        ffp = region(2 * FT * S + 1024, 2 * 512).rearrange("p (b n) -> p b n", b=2)
        hx = region(ARENA - 2048, 2048).rearrange("p (t n) -> p t n", t=KT)
        pos[0] = 0
        praw = take(15 * 257).rearrange("p (t n) -> p t n", t=15)
        aT_rT = region(0, 2048).rearrange("p (j c w n) -> p j c w n", j=4, c=NCH, w=2)
        bT = region(2048, 1024).rearrange("p (j n) -> p j n", j=4)
        pm = take(15 * S).rearrange("p (t n) -> p t n", t=15)
        t_at = pos[0]
        tmp = [take(1024).rearrange("p (j n) -> p j n", j=4) for _ in range(7)]
        kk, av, lw, cum, dec1, dec2, dtmp = tmp
        inv = [t.rearrange("p j n -> p (j n)").rearrange("p (q n) -> p q n", q=16) for t in tmp]
        kTt = take(1024).rearrange("p (j n) -> p j n", j=4)
        vtok = take(1024).rearrange("p (q n) -> p q n", q=16)
        gB = take(2048).rearrange("p (q w n) -> p q w n", q=16, w=2)
        gK = xn[:, :].rearrange("p (q w n) -> p q w n", q=16, w=2)
        xs = bc[:, 2, 512:768].rearrange("p (j n) -> p j n", j=4)
        us = bc[:, 2, 768:1024].rearrange("p (j n) -> p j n", j=4)
        ms = take(256).rearrange("p (j n) -> p j n", j=4)
        cat = (hh, hl)
        yT = take(1024).rearrange("p (j n) -> p j n", j=4)
        reset = gg[:, :]
        nrm = take(256)
        btok = hreg[:, 1024:2048].rearrange("p (q n) -> p q n", q=16)
        ktok = hreg[:, 3072:4096].rearrange("p (q n) -> p q n", q=16)
        bonus = pm[:, 4:8, :]
        lup = bc[:, 0, 0:512]
        gu0 = bc[:, 0, 512:1024]
        gu1 = bc[:, 1, 0:512]
        wsr = bc[:, 1, 512:1024].rearrange("p (g n) -> p g n", g=4)
        wsT = bc[:, 2, 0:512].rearrange("p (g n) -> p g n", g=4)
        gmT = bc[:, 3, :].rearrange("p (j n) -> p j n", j=4)
        gv = xn[:, 0:1024].rearrange("p (m n) -> p m n", m=MT)
        gu = xn[:, 1024:2048].rearrange("p (m n) -> p m n", m=MT)

        bank = [ctx.enter_context(nc.psum_tensor(f"bank{i}", [P, 512], fp)) for i in range(8)]

        def wsrc(w, r0, nk, c0, n):
            return w[0, r0:r0 + nk * P, c0:c0 + n].rearrange("(k p) n -> p k n", p=P)

        def cut(buf, i, nk, n):
            return buf[:, i, 0:nk * n].rearrange("p (k n) -> p k n", k=nk)

        IN1 = {"o_if": (2304, 520), "qm": (768, 512), "km": (1280, 512), "vm": (1792, 512), "qa": (0, 512),
               "kva": (512, 256), "g0": (2824, 512), "g1": (3336, 512), "g2": (3848, 512), "g3": (4360, 512)}
        IN2 = {"pu": (0, 512), "pv": (512, 512), "r": (1024, 512), "k": (1536, 512), "v": (2048, 512),
               "lora": (2560, 288)}

        def sources(name):
            if name in IN1 or name in IN2:
                w, (c0, n) = (A["w_in"], IN1[name]) if name in IN1 else (A["w_in_2"], IN2[name])
                nk = 4 if name == "kva" else 2
                return [(nk, n, [(wsrc(w, P * k, nk, c0, n), 0, n)]) for k in range(0, 8, nk)]
            if name[0] == "c":
                i, c0 = PIECES[int(name[1:])]
                w = (A["w_ada"], A["w_ada_2"])[i][0, :, c0:c0 + 512].rearrange("(p k) n -> p k n", k=8)
                return [(2, 512, [(w[:, k:k + 2, :], 0, 512)]) for k in range(0, 8, 2)]
            if name[0] == "b":
                w = A["w_branch_attn"] if name[1] == "a" else A["w_branch_mlstm"]
                return [(2, 512, [(wsrc(w, P * k, 2, 512 * int(name[2]), 512), 0, 512)]) for k in (0, 2)]
            if name[:2] == "wo":
                n = int(name[2])
                w = (A["w_out"], A["w_out_2"])[n // 2]
                return [(2, 512, [(wsrc(w, P * k, 2, 512 * (n % 2), 512), 0, 512)]) for k in range(0, 8, 2)]
            if name[:2] == "ff":
                c0 = 256 * int(name[2:])
                return [(2, 512, [(wsrc(A["w_ffn_gate"], P * k, 2, c0, 256), 0, 256),
                                  (wsrc(A["w_ffn_up"], P * k, 2, c0, 256), 256, 512)]) for k in range(0, 8, 2)]
            if name[:2] == "gf":
                c0 = 256 * int(name[2:])
                return [(2, 512, [(wsrc(A["w_ffn_in_2"], P * k, 2, c0, 256), 0, 256),
                                  (wsrc(A["w_ffn_in_2"], P * k, 2, FF + c0, 256), 256, 512)]) for k in range(0, 8, 2)]
            w = A["w_ffn_down"] if name[1] == "A" else A["w_ffn_out_2"]
            return [(1, 1024, [(wsrc(w, P * (2 * int(name[2:]) + k), 1, 0, 1024), 0, 1024)]) for k in (0, 1)]

        place, order, split_n, pairs = {}, [], 0, 0
        total = [0] * RAW

        def with_piece(name):
            at = ITEMS.index(name) + 1
            alone = name[0] == "c" or name == "pv" or at == len(ITEMS)
            return None if alone or ITEMS[at][0] != "c" else ITEMS[at]

        mixed = [with_piece(name) for name in ITEMS]
        for name in ITEMS:
            if name in mixed:
                continue
            own = [(name, i, x) for i, x in enumerate(sources(name))]
            if name[0] not in "cd":
                place[name] = (pairs, split_n, split_n + len(own))
                pairs += 1
            elif name[0] == "d":
                place[name] = (None, split_n, split_n + len(own))
            blocks = own
            if with_piece(name):
                other = [(with_piece(name), i, x) for i, x in enumerate(sources(with_piece(name)))]
                n = min(len(own), len(other))
                blocks = [b for two in zip(own, other) for b in two] + own[n:] + other[n:]
            for what, i, (nk, width, parts) in blocks:
                b = len(order)
                total[b % RAW] += 16 * len(parts)
                split = None
                if what[0] != "c":
                    split = split_n
                    split_n += 1
                order.append((what, i, nk, width, parts, total[b % RAW], split))
        at_block = {}
        for b, o in enumerate(order):
            at_block.setdefault(o[0], []).append(b)

        POOL_ITEMS = ["r", "ff0", "gf0"]
        counts = {"dve": 0, "pool": 0}
        ready = []
        for name, *_ in order:
            who = "pool" if name in POOL_ITEMS else "dve"
            counts[who] += 1
            ready.append((who, counts[who]))
        of_split = {o[6]: b for b, o in enumerate(order) if o[6] is not None}

        def piece_place(a):
            if a < 4:
                return bank[a], 0
            if a < 10:
                return bank[6], a if a > 4 else 0
            if a in (20, 21):
                return bank[27 - a], 0
            if a in (15, 16, 17):
                return bank[2 * (a % 2)], a - 1 if a == 17 else 0
            if a in (18, 19):
                return bank[a - 12], 0
            return bank[4 + a % 2], a - 1 if 12 <= a < 15 else 0

        block = ctx.enter_context(nc.Block())

        def prepare_on(eng, me, name):
            for b in sorted(at_block[name] + at_block.get(with_piece(name), [])):
                what, i, nk, width, _, landed, g = order[b]
                who, count = ready[b]
                if who != me:
                    continue
                if g is not None:
                    eng.wait_ge(sem("hi_ready"), g + 1)
                    eng.tensor_tensor(wlo[:, g % HL, 0:nk * width], raw[:, b % RAW, 0:nk * width],
                                      whi[:, g % HL, 0:nk * width].bitcast(fp), ALU.subtract)\
                       .then_inc(sem(f"{me}_blocks"), 1)
                    continue
                a = int(what[1:])
                which = PIECES[a][0]
                eng.wait_ge(sem(f"raw{b % RAW}_in"), landed)
                if i == 0:
                    eng.wait_ge(sem(f"acc{a % 2}_started"), 16 * (a // 2 + 1))
                    eng.wait_ge(sem("small_in"), 48)
                    if a >= 12:
                        eng.wait_ge(sem("cs_ready"), 1)
                w = cut(raw, b % RAW, nk, width)
                for k in range(nk):
                    n = 8 * a + nk * i + k
                    if n:
                        eng.wait_ge(sem("sums"), n)
                    eng.scalar_tensor_tensor(acc[:, a % 2, :], w[:, k, :], cc[:, which, n % 8:n % 8 + 1],
                                             acc[:, a % 2, :], ALU.mult, ALU.add).then_inc(sem("sums"), 1)
                eng.wait_ge(sem("sums"), n + 1)
                eng.nop().then_inc(sem(f"{me}_blocks"), 1)

        @block.sync
        def _(sp):
            sp.dma_start(xt[:, :, :], A["x"][0].rearrange("(m p) n -> p m n", p=P)).then_inc(sem("x_in"), 16)
            for b, (_, _, nk, width, parts, _, _) in enumerate(order):
                if b >= RAW:
                    who, count = ready[b - RAW]
                    sp.wait_ge(sem(f"{who}_blocks"), count)
                for src, a, z in parts:
                    sp.dma_start(cut(raw, b % RAW, nk, width)[:, :, a:z], src).then_inc(sem(f"raw{b % RAW}_in"), 16)
            for m in range(MT):
                sp.wait_ge(sem("y_out"), m + 1)
                sp.dma_start(out[0, m * P:(m + 1) * P, :], xt[:, m, :]).then_inc(sem("out_stored"), 16)
            sp.wait_ge(sem("out_stored"), 16 * MT)

        @block.gpsimd
        def _(pool):
            pool.memset(conv_in[:, :, 0:3], 0.0).then_inc(sem("pads"), 1)
            pool.memset(vaug[:, :, :, 128:129], 1.0).then_inc(sem("pads"), 1)
            pool.memset(cstate[:, 0, :, :], 0.0).then_inc(sem("pads"), 1)
            pool.memset(resets[0:4, 0, :], 1.0).then_inc(sem("pads"), 1)
            pool.memset(resets[0:4, 1, :], 0.0).then_inc(sem("pads"), 1)
            pool.wait_ge(sem("pads"), 5)
            pool.memset(resets[0:4, 0, :].rearrange("p (c n) -> p c n", c=NCH)[:, :, 0:1], 0.0).then_inc(sem("pads"), 1)
            pool.memset(resets[0:4, 1, :].rearrange("p (c n) -> p c n", c=NCH)[:, :, 0:1], NEG).then_inc(sem("pads"), 1)

            def start_piece(a):
                i, c0 = PIECES[a]
                if a >= 2:
                    pool.wait_ge(sem("piece_done"), a - 1)
                pool.memset(acc[:, a % 2, :], 0.0).then_inc(sem("acc_zero"), 1)
                pool.wait_ge(sem("acc_zero"), a + 1)
                pool.dma_start(acc[0:1, a % 2, :], (A["b_ada"], A["b_ada_2"])[i][0:1, c0:c0 + 512])\
                    .then_inc(sem(f"acc{a % 2}_started"), 16)

            def spread(dst, src, s):
                pool.dma_start(dst, src.partition_broadcast(P)).then_inc(s, 16)

            def prepare(name):
                if name[0] == "c" and int(name[1:]) >= 1:
                    a = int(name[1:])
                    for x in ([] if a == 21 else [22, 23] if a == 22 else [a + 1] if a < 23 else []):
                        start_piece(x)
                if name in POOL_ITEMS:
                    prepare_on(pool, "pool", name)

            for a in range(2):
                start_piece(a)
            spread(bsm[:, 0:8], A["b_if"][0], sem("spreads"))
            spread(bsm[:, 8:16], A["attn_sinks"][0], sem("spreads"))
            spread(bcs[:, 0, :], A["mlstm_norm_w"][0], sem("spreads"))
            spread(bcs[:, 1, :], A["sg_ln_g_2"][0], sem("spreads"))
            spread(bcs[:, 2, :], A["sg_ln_b_2"][0], sem("spreads"))
            spread(bc[:, 0, :], A["g_post_mix"][0], sem("spreads"))
            spread(bc[:, 1, :], A["g_post_ffn"][0], sem("spreads"))
            names = ITEMS
            for name in names[:names.index("ff1")]:
                prepare(name)
            pool.wait_ge(sem("h_ready"), 4)
            spread(bc[:, 2, :], A["emb_ln_g_2"], sem("spreads"))
            spread(bc[:, 3, :], A["emb_ln_b_2"], sem("spreads"))
            for name in names[names.index("ff1"):names.index("c18")]:
                prepare(name)
            pool.wait_ge(sem("emb_done"), 2)
            pool.dma_start(lup[0:64, :], A["w_up_2"][0]).then_inc(sem("lora_in"), 16)
            pool.dma_start(lup[64:128, :], A["a_up_2"][0]).then_inc(sem("lora_in"), 16)
            pool.dma_start(gu0, A["g_up_2"][0, 0:128, :]).then_inc(sem("lora_in"), 16)
            pool.dma_start(gu1[96:128, :], A["g_up_2"][0, 128:160, :]).then_inc(sem("lora_in"), 16)
            pool.dma_start(wsr, A["w_s_2"][0].rearrange("g t s -> t g s")).then_inc(sem("ws_in"), 16)
            pool.memset(praw[:, :, 0:1], 0.0).then_inc(sem("pads2"), 1)
            pool.wait_ge(sem("h_ready"), 6)
            pool.memset(ms, 0.0).then_inc(sem("pads2"), 1)
            pool.memset(reset, 1.0).then_inc(sem("pads2"), 1)
            pool.wait_ge(sem("pads2"), 3)
            pool.memset(reset.rearrange("p (q n) -> p q n", q=16)[:, :, 0:1], 0.0).then_inc(sem("pads2"), 1)
            for name in names[names.index("c18"):names.index("wo2")]:
                prepare(name)
            pool.wait_ge(sem("yb_ready"), 1)
            spread(bc[:, 0, :], A["ln1_g_2"][0], sem("spreads"))
            spread(bc[:, 1, :], A["ln1_b_2"][0], sem("spreads"))
            spread(bc[:, 2, :], A["ln2_g_2"][0], sem("spreads"))
            spread(bc[:, 3, :], A["ln2_b_2"][0], sem("spreads"))
            for name in names[names.index("wo2"):]:
                prepare(name)

        def flat(name):
            a = A[name]
            if name == "conv_w":
                return a[0].rearrange("j (t p) -> (j t) p", p=P)
            if name == "b_s_2":
                return a[0]
            if name == "r_k_2":
                return a[0].rearrange("(t h) n -> t (h n)", h=2)
            return a[0].rearrange("(t p) -> t p", p=P)

        @block.scalar
        def _(act):
            chain = [0]

            def step(ins):
                chain[0] += 1
                ins.then_inc(sem("act_chain"), 1)
                act.wait_ge(sem("act_chain"), chain[0])

            def item(name):
                pair, _, z = place[name]
                act.wait_ge(sem("blocks_done"), z)
                return bank[2 * (pair % 2)], bank[2 * (pair % 2) + 1]

            def freed(name, ins):
                ins.then_inc(sem(f"pair{place[name][0] % 2}_free"), 1)

            act.dma_start(cst[:, :], A["const"]).then_inc(sem("const_in"), 16)
            act.dma_start(cc[:, 0, :], A["c"][0].rearrange("(p k) -> p k", k=8)).then_inc(sem("small_in"), 16)
            act.dma_start(cc[:, 1, :], A["c_2"][0].rearrange("(p k) -> p k", k=8)).then_inc(sem("small_in"), 16)
            act.dma_start(posi[:, :], A["positions"][0].rearrange("(m p) -> p m", p=P),
                          allow_slow_non_contiguous=True).then_inc(sem("small_in"), 16)
            for i, (tab, where) in enumerate(((ROWS1, v1), (ROWS2, v2))):
                for name, n in tab:
                    a, b = where[name]
                    if name == "mu_shift_2":
                        act.dma_start(vraw[a:b - 1, i, :], A[name][0, 0:14 * P].rearrange("(t p) -> t p", p=P))\
                           .then_inc(sem("vectors_in"), 16)
                        act.dma_start(vraw[b - 1:b, i, :], A[name][:, 1824 - P:1824]).then_inc(sem("vectors_in"), 16)
                    else:
                        act.dma_start(vraw[a:b, i, :], flat(name)).then_inc(sem("vectors_in"), 16)

            def split(name, part=slice(None)):
                for b in at_block[name][part]:
                    _, _, nk, width, _, count, g = order[b]
                    act.wait_ge(sem(f"raw{b % RAW}_in"), count)
                    if g >= HL:
                        act.wait_ge(sem("blocks_done"), g - HL + 1)
                    act.activation(whi[:, g % HL, 0:nk * width], raw[:, b % RAW, 0:nk * width], ACT.Copy)\
                       .then_inc(sem("hi_ready"), 1)

            def scale_h(u):
                g = gain[:, u, :]
                sh = modT[:, u // 2, (24 if u % 2 else 0):(32 if u % 2 else 8)]
                act.wait_ge(sem("gain_ready"), u + 1)
                for k in range(4):
                    act.wait_ge(sem("hx_turned"), 4 * u + k // 2 + 1)
                    act.activation(hx[:, k, :], bank[4 + k // 2][:, 256 * (k % 2):256 * (k % 2) + 256], ACT.Identity,
                                   bias=sh[:, k:k + 1], scale=g[:, k:k + 1]).then_inc(sem("hx_scaled"), 1)
                for n in range(2):
                    act.wait_ge(sem("hx_scaled" if n == 0 else "hx_high_half"), 4 * u + 4)
                    act.activation(hh[:, 4 * n:4 * n + 4, :], hx[:, 4 * n:4 * n + 4, :], ACT.Copy)\
                       .then_inc(sem("hh_ready"), 1)

            def branch_gates(n):
                for h, b in enumerate(item(f"g{n}")):
                    ins = act.activation(gT[:, 4 * n + 2 * h:4 * n + 2 * h + 2, :],
                                         b[:, :].rearrange("p (t n) -> p t n", t=2), ACT.Sigmoid)
                    ins.then_inc(sem("gT_ready"), 1) if h == 0 else freed(f"g{n}", ins)

            act.wait_ge(sem("x_in"), 16)
            for m in range(MT):
                act.activation(xn[:, m * D:(m + 1) * D], xt[:, m, :], ACT.Square,
                               accum_out=st[:, m:m + 1]).then_inc(sem("squares"), 1)
            act.wait_ge(sem("var_ready"), 1)
            act.activation(st[:, 4:6], st[:, 2:4], ACT.Sqrt).then_inc(sem("std_ready"), 1)
            act.wait_ge(sem("small_in"), 48)
            act.activation(cc[:, 1, :], cc[:, 1, :], ACT.Silu).then_inc(sem("cs_ready"), 1)
            scale_h(0)
            split("o_if")
            split("qm")
            b0, b1 = item("o_if")
            act.activation(osig[:, 0, :], b0[:, :], ACT.Sigmoid).then_inc(sem("osig_ready"), 1)
            freed("o_if", act.activation(osig[:, 1, :], b1[:, :], ACT.Sigmoid))
            split("km")
            act.wait_ge(sem("angles"), 1)
            act.activation(cossin, rsc[:, 1], ACT.Sin).then_inc(sem("cossin_ready"), 1)
            for t0, name, nxt in ((0, "qm", "vm"), (4, "km", None)):
                for h, b in enumerate(item(name)):
                    act.wait_ge(sem("pads"), 1)
                    ins = act.activation(conv_in[:, t0 + 2 * h:t0 + 2 * h + 2, 3:259],
                                         b[:, :].rearrange("p (t n) -> p t n", t=2), ACT.Copy)
                    if h == 0:
                        ins.then_inc(sem("conv_raw"), 1)
                    else:
                        freed(name, ins)
                if nxt:
                    split(nxt)
            act.wait_ge(sem("if_turned"), 1)
            r_i, r_f, r_l = rows[0:4, 0, :], rows[0:4, 1, :], rows[0:4, 2, :]
            act.activation(r_i, bank[7][0:4, 0:256], ACT.Copy).then_inc(sem("act_chain"), 1)
            chain[0] += 1
            step(act.activation(r_f, bank[7][0:4, 256:512], ACT.Copy))
            step(act.activation(r_l, r_f, ACT.Abs))
            step(act.activation(r_l, r_l, ACT.Exp, scale=-1.0))
            act.activation(r_l, r_l, ACT.Ln, bias=1.0).then_inc(sem("log_ready"), 1)
            for m, b in enumerate(item("vm")):
                ins = act.activation(vaug[:, m, :, 0:128], b[:, :].rearrange("p (h n) -> p h n", h=HM), ACT.Copy)
                ins.then_inc(sem("v_ready"), 1) if m == 0 else freed("vm", ins)
            split("qa")
            split("kva")
            act.wait_ge(sem("rows_ready"), 1)
            act.activation(rows[0:4, 4, :], rows[0:4, 4, :], ACT.Exp).then_inc(sem("rows_exp"), 1)
            act.activation(rows[0:4, 5, :], rows[0:4, 5, :], ACT.Exp).then_inc(sem("rows_exp"), 1)
            act.activation(rows[0:4, 6, :], rows[0:4, 6, :], ACT.Exp, scale=-1.0).then_inc(sem("rows_exp"), 1)
            act.activation(rows[0:4, 2, 16:20], rows[0:4, 2, 16:20], ACT.Exp).then_inc(sem("rows_exp"), 1)
            act.wait_ge(sem("conv_done"), 1)
            for t in range(2):
                act.activation(qk[:, 4 * t:4 * t + 4, :], qk[:, 4 * t:4 * t + 4, :], ACT.Silu)\
                   .then_inc(sem("silu_done"), 1)
            split("g0")
            act.wait_ge(sem("arg_ready"), 1)
            for h in range(HM):
                for m in range(MT):
                    act.activation(wT[:, h, m, :], wT[:, h, m, :], ACT.Exp,
                                   bias=st[:, 64 + 16 * m + h:64 + 16 * m + h + 1]).then_inc(sem("wT_ready"), 1)
            split("g1")
            branch_gates(0)
            split("g2")
            branch_gates(1)
            split("g3")
            branch_gates(2)
            for m in range(MT):
                act.wait_ge(sem("qr_turned"), m + 1)
                act.activation(qT[:, :, m * P:(m + 1) * P], bank[4 + m][:, :].rearrange("p (i n) -> p i n", i=4),
                               ACT.Copy, scale=DH ** -0.5).then_inc(sem("qT_ready"), 1)
            act.wait_ge(sem("qr_turned"), 3)
            act.activation(kT, bank[6][:, 0:256], ACT.Copy).then_inc(sem("qT_ready"), 1)
            for m, sm in ((0, sm0), (1, sm1)):
                act.wait_ge(sem("smax_ready"), m + 1)
                for h in range(HQ):
                    act.activation(sm[:, h, :], sm[:, h, :], ACT.Exp, bias=st[:, 16 + 8 * m + h:17 + 8 * m + h],
                                   accum_out=st[:, 32 + 8 * m + h:33 + 8 * m + h]).then_inc(sem("exp_ready"), 1)
                act.activation(st[:, 48 + 8 * m:56 + 8 * m], st[:, 48 + 8 * m:56 + 8 * m], ACT.Exp)\
                   .then_inc(sem("exp_ready"), 1)
            branch_gates(3)
            split("ba0")
            split("ba1")
            for n in range(6):
                act.wait_ge(sem("p_turned"), n + 1)
                act.activation(pT[:, 4 * n:4 * n + 4, :], bank[4 + n % 4][:, :].rearrange("p (h n) -> p h n", h=4),
                               ACT.Copy).then_inc(sem("pT_ready"), 1)
            for m in range(MT):
                for h2 in range(2):
                    act.wait_ge(sem("intra_done"), 2 * m + h2 + 1)
                    act.activation(intra[:, m, 2 * h2:2 * h2 + 2, :],
                                   bank[4 + 2 * 0 + h2][:, 0:258].rearrange("p (h n) -> p h n", h=2),
                                   ACT.Copy).then_inc(sem("intra_ready"), 1)
            for m in range(MT):
                act.wait_ge(sem("ya_turned"), m + 1)
                act.activation(yah[:, :, m * P:(m + 1) * P], bank[4 + m][:, :].rearrange("p (i n) -> p i n", i=4),
                               ACT.Copy).then_inc(sem("yah_ready"), 1)
            act.wait_ge(sem("hvar_ready"), 1)
            act.activation(st[:, 112:120], st[:, 112:120], ACT.Sqrt).then_inc(sem("hstd_ready"), 1)
            for m in range(MT):
                act.wait_ge(sem("ym_turned"), m + 1)
                act.activation(ymh[:, :, m * P:(m + 1) * P], bank[6 + m][:, :].rearrange("p (i n) -> p i n", i=4),
                               ACT.Copy).then_inc(sem("ymh_ready"), 1)
            split("bm0")
            split("bm1")
            for n in range(2):
                act.wait_ge(sem("sum_ready"), n + 1)
                act.activation(merged[0][:, 4 * n:4 * n + 4, :], gT[:, 4 * n:4 * n + 4, :], ACT.Copy)\
                   .then_inc(sem("mgh_ready"), 1)
            split("wo0")
            split("wo1")

            def std(n, a, z):
                act.wait_ge(sem("var_ready"), n)
                act.activation(st[:, a:z], st[:, a:z], ACT.Sqrt).then_inc(sem("std_ready"), 1)

            squared = hreg[:, 0:512]
            square_n = [0]

            def square(b, m, half):
                if square_n[0]:
                    act.wait_ge(sem("post_squares"), square_n[0])
                square_n[0] += 1
                act.activation(squared, b[:, :], ACT.Square, accum_out=st[:, 120 + 2 * m + half:121 + 2 * m + half])\
                   .then_inc(sem("post_squares"), 1)

            wo = [item("wo0"), item("wo1")]
            for m in range(MT):
                for half in range(2):
                    square(wo[half][m], m, half)
            std(2, 124, 126)
            split("ff0", slice(0, 2))
            for m in range(MT):
                act.wait_ge(sem("x_added"), m + 1)
                act.activation(xn[:, m * D:(m + 1) * D], xt[:, m, :], ACT.Square,
                               accum_out=st[:, m:m + 1]).then_inc(sem("squares"), 1)
            act.wait_ge(sem("var_ready"), 3)
            act.activation(st[:, 4:6], st[:, 2:4], ACT.Sqrt).then_inc(sem("std_ready"), 1)
            split("ff0", slice(2, 4))
            scale_h(1)

            def feed_forward(letter, down, n):
                for j in range(FT // 2):
                    for name in [f"{letter}{j + 1}"] if j + 1 < FT // 2 else [f"{down}0", f"{down}1"]:
                        split(name)
                    g, _ = item(f"{letter}{j}")
                    q = n * (FT // 2) + j
                    if j >= 2:
                        act.wait_ge(sem("ffp_ready"), q - 1)
                    act.activation(sil[:, j % 2, :], g[:, :], ACT.Silu).then_inc(sem("sil_ready"), 1)
                    act.wait_ge(sem("ffp_ready"), q + 1)
                    act.activation(ffh[:, 2 * j:2 * j + 2, :], ffp[:, j % 2, :].rearrange("p (t n) -> p t n", t=2),
                                   ACT.Copy).then_inc(sem("ffh_ready"), 1)
                for i in range(2, FT // 2):
                    split(f"{down}{i}")

            feed_forward("ff", "dA", 0)
            act.activation(st[:, 252:253], st[:, 4:5], ACT.Sqrt).then_inc(sem("warm"), 1)
            act.wait_ge(sem("blocks_done"), place["dA10"][2])
            for m in range(MT):
                for half in range(2):
                    square(bank[4 + 2 * m + half], m, half)
            std(4, 124, 126)
            split("r")
            std(5, 126, 128)
            scale_h(2)

            act.wait_ge(sem("pads2"), 1)
            for t0, name, nxt in ((0, "r", "k"), (4, "k", "v"), (8, "v", "lora")):
                split(nxt)
                for h, b in enumerate(item(name)):
                    ins = act.activation(praw[:, t0 + 2 * h:t0 + 2 * h + 2, 1:257],
                                         b[:, :].rearrange("p (t n) -> p t n", t=2), ACT.Copy)
                    ins.then_inc(sem("praw_ready"), 1) if h == 0 else freed(name, ins)
            split("pu")
            b0, b1 = item("lora")
            act.activation(praw[:, 12:14, 1:257], b0[:, :].rearrange("p (t n) -> p t n", t=2), ACT.Copy)\
               .then_inc(sem("praw_ready"), 1)
            freed("lora", act.activation(praw[:, 14, 1:257], b1[:, 0:256], ACT.Copy))
            act.wait_ge(sem("lora_mixed"), 1)
            act.activation(pm[0:64, 12, :], pm[0:64, 12, :], ACT.Tanh).then_inc(sem("lora_act"), 1)
            act.activation(pm[:, 13, :], pm[:, 13, :], ACT.Sigmoid).then_inc(sem("lora_act"), 1)
            act.activation(pm[96:128, 14, :], pm[96:128, 14, :], ACT.Sigmoid).then_inc(sem("lora_act"), 1)
            split("pv")

            def gelu(name, dst):
                for m, b in enumerate(item(name)):
                    ins = act.activation(dst[:, m, :], b[:, :], ACT.Gelu_apprx_tanh)
                    ins.then_inc(sem("gelu_done"), 1) if m == 0 else freed(name, ins)

            gelu("pu", gu)
            for n, (dst, off) in enumerate(((lw, "w0_2"), (av, "a0_2"))):
                for j in range(4):
                    act.wait_ge(sem("lora_done"), 2 * n + j // 2 + 1)
                    act.activation(dst[:, j, :], bank[4 + 2 * n + j // 2][:, 256 * (j % 2):256 * (j % 2) + 256],
                                   ACT.Sigmoid, bias=v2T[:, v2[off][0] + j:v2[off][0] + j + 1])\
                       .then_inc(sem("lwa_ready"), 1)
            gelu("pv", gv)
            for j in range(2):
                act.wait_ge(sem("lora_done"), 5 + j)
                act.activation(gmT[:, 2 * j:2 * j + 2, :], bank[4 + j][:, :].rearrange("p (t n) -> p t n", t=2),
                               ACT.Copy).then_inc(sem("gm_ready"), 1)
            act.wait_ge(sem("kk_summed"), 1)
            act.activation(nrm[0:8, :], bank[6][0:8, 0:256], ACT.Sqrt).then_inc(sem("kk_len"), 1)
            act.wait_ge(sem("cum_ready"), 1)
            act.activation(dec1, cum, ACT.Exp).then_inc(sem("dec_ready"), 1)
            act.wait_ge(sem("cum_ready"), 2)
            act.activation(dec2, lw, ACT.Exp).then_inc(sem("dec_ready"), 1)
            act.wait_ge(sem("dec_ready"), 2)
            act.activation(lw, cum, ACT.Exp, scale=-1.0).then_inc(sem("dec_ready"), 1)
            act.wait_ge(sem("gvar_ready"), 1)
            act.activation(st[:, 132:134], st[:, 132:134], ACT.Sqrt).then_inc(sem("gstd_ready"), 1)
            for n, dst in enumerate((btok, ktok, vtok)):
                for h in range(2):
                    act.wait_ge(sem("tok_turned"), 2 * n + h + 1)
                    act.activation(dst[:, 8 * h:8 * h + 8, :],
                                   bank[(2 * n + h) % 4 + 4][:, :].rearrange("p (q n) -> p q n", q=8), ACT.Copy)\
                       .then_inc(sem("tok_ready"), 1)
            for m in range(MT):
                act.wait_ge(sem("ga_turned"), m + 1)
                act.activation(hh[:, 0:4, m * P:(m + 1) * P], bank[2 + m][:, :].rearrange("p (i n) -> p i n", i=4),
                               ACT.Copy).then_inc(sem("gah_ready"), 1)
            for c in range(NCH):
                act.wait_ge(sem("x_done"), c + 1)
                act.activation(xs, bank[4][:, 0:256].rearrange("p (j n) -> p j n", j=4), ACT.Copy)\
                   .then_inc(sem("x_ready"), 1)
                act.wait_ge(sem("u_done"), c + 1)
                act.activation(us, bank[5][:, 0:256].rearrange("p (j n) -> p j n", j=4), ACT.Copy)\
                   .then_inc(sem("u_ready"), 1)
                act.wait_ge(sem("yc_done"), c + 1)
                act.activation(yT[:, :, c * L:(c + 1) * L], bank[7][:, 0:256].rearrange("p (j n) -> p j n", j=4),
                               ACT.Copy).then_inc(sem("yc_ready"), 1)
            split("wo2")
            act.wait_ge(sem("yvar_ready"), 1)
            act.activation(nrm[0:8, :], nrm[0:8, :], ACT.Sqrt).then_inc(sem("ystd_ready"), 1)
            act.wait_ge(sem("yb_ready"), 1)
            act.activation(hh[:, 4:8, :], yT, ACT.Copy).then_inc(sem("ybh_ready"), 1)
            split("wo3")
            split("gf0")
            std(6, 126, 128)
            scale_h(3)
            feed_forward("gf", "dB", 1)
            std(7, 126, 128)

        @block.vector
        def _(dve):
            chain = [0]

            def step(ins):
                chain[0] += 1
                ins.then_inc(sem("dve_chain"), 1)
                dve.wait_ge(sem("dve_chain"), chain[0])

            def item(name):
                pair, _, z = place[name]
                dve.wait_ge(sem("blocks_done"), z)
                return bank[2 * (pair % 2)], bank[2 * (pair % 2) + 1]

            def freed(name, ins):
                ins.then_inc(sem(f"pair{place[name][0] % 2}_free"), 1)

            def bcast(ap, n):
                return ap.unsqueeze(len(ap.shape)).to_broadcast(list(ap.shape) + [n])

            def prepare(name):
                prepare_on(dve, "dve", name)

            TT = dve.tensor_tensor
            TS = dve.tensor_scalar
            STT = dve.scalar_tensor_tensor
            def rms_rows(n):
                dve.wait_ge(sem("squares"), 2 * n + 2)
                step(TS(st[:, 2:4], st[:, 0:2], 1.0 / D, EPS, ALU.mult, ALU.add))
                step(dve.reciprocal(st[:, 2:4], st[:, 2:4]))
                dve.nop().then_inc(sem("var_ready"), 1)

            def pair_wait(name):
                dve.wait_ge(sem(f"pair{place[name][0] % 2}_free"), place[name][0] // 2 + 1)

            def collect_piece(a, gpost=None):
                i, c0 = PIECES[a]
                dve.wait_ge(sem("piece_done"), a + 1)
                b0, _ = piece_place(a)
                if a in GATES:
                    dst = gg[:, c0 % 1024:c0 % 1024 + 512]
                    ins = dve.tensor_copy(dst, b0[:, :]) if gpost is None else \
                        TT(dst, b0[:, :], gpost[:, c0 % 1024:c0 % 1024 + 512], ALU.mult)
                else:
                    ins = dve.tensor_copy(modT[:, i, c0 // P:c0 // P + 4], b0[:, 0:4])
                ins.then_inc(sem("piece_used"), 1)
                dve.wait_ge(sem("piece_used"), a + 1)

            def gains(u, g):
                i, c0 = u // 2, (32 if u % 2 else 8)
                sc = modT[:, i, c0:c0 + 8]
                step(TS(gain[:, u, :], sc, 1.0, None, ALU.add))
                if g is not None:
                    step(TT(gain[:, u, :], gain[:, u, :], g, ALU.mult))
                dve.nop().then_inc(sem("gain_ready"), 1)

            def scale_h(u):
                sh = modT[:, u // 2, (24 if u % 2 else 0):(32 if u % 2 else 8)]
                for k in range(4, 8):
                    dve.wait_ge(sem("hx_turned"), 4 * u + k // 2 + 1)
                    TS(hx[:, k, :], bank[4 + k // 2][:, 256 * (k % 2):256 * (k % 2) + 256], gain[:, u, k:k + 1],
                       sh[:, k:k + 1], ALU.mult, ALU.add).then_inc(sem("hx_high_half"), 1)
                dve.wait_ge(sem("hx_high_half"), 4 * u + 4)
                for n in range(2):
                    t = slice(4 * n, 4 * n + 4)
                    dve.wait_ge(sem("hh_ready"), 2 * u + n + 1)
                    TT(hl[:, t, :], hx[:, t, :], hh[:, t, :].bitcast(fp), ALU.subtract).then_inc(sem("h_ready"), 1)

            prepare("c0")
            for i, (dst, n) in enumerate(((v1T, n1), (v2T, n2))):
                dve.wait_ge(sem("vec_turned"), i + 1)
                step(dve.tensor_copy(dst[:, :], bank[4 + i][:, 0:n]))
            rms_rows(0)
            dve.wait_ge(sem("std_ready"), 1)
            for m in range(MT):
                TS(xn[:, m * D:(m + 1) * D], xt[:, m, :], st[:, 4 + m:5 + m], None, ALU.mult)\
                    .then_inc(sem("xn_ready"), 1)
            for a in range(1, 4):
                prepare(f"c{a}")
                collect_piece(a - 1)
            collect_piece(3)
            gains(0, v1T[:, v1["g_pre_mix"][0]:v1["g_pre_mix"][1]])
            scale_h(0)
            prepare("o_if")
            prepare("qm")
            dve.wait_ge(sem("small_in"), 48)
            dve.wait_ge(sem("const_in"), 16)
            step(dve.tensor_copy(st[:, 10:12], posi[:, :]))
            ang, red = rsc[:, 0], rsc[:, 1]
            for m in range(MT):
                for f in range(2):
                    TS(ang[:, m, f, :], C("freq"), st[:, 10 + m:11 + m], None, ALU.mult).then_inc(sem("dve_chain"), 1)
                    chain[0] += 1
            dve.wait_ge(sem("dve_chain"), chain[0])
            step(TS(red[:, :, 0, :], ang[:, :, 0, :], 1 / (2 * math.pi), 0.0, ALU.mult, ALU.add))
            step(TS(red[:, :, 1, :], ang[:, :, 1, :], 1 / (2 * math.pi), 0.25, ALU.mult, ALU.add))
            step(TS(red, red, ROUND, None, ALU.add))
            step(TS(red, red, ROUND, None, ALU.subtract))
            for piece in (TWO_PI_1, TWO_PI_2, TWO_PI_3):
                a2, r2 = (v.rearrange("p m f c -> p (m f c)") for v in (ang, red))
                step(STT(a2, r2, -piece, a2, ALU.mult, ALU.add))
            step(TS(ang[:, :, 1, :], ang[:, :, 1, :], math.pi / 2, None, ALU.add))
            TS(red, ang, SIN_MAX, -SIN_MAX, ALU.min, ALU.max).then_inc(sem("angles"), 1)
            item("o_if")
            dve.wait_ge(sem("spreads"), 7 * 16)
            for m in range(MT):
                TT(st[:, 240 + 8 * m:248 + 8 * m], bank[4 + m][:, 0:8], bsm[:, 0:8], ALU.add)\
                    .then_inc(sem("if_ready"), 1)
            dve.wait_ge(sem("osig_ready"), 1)
            dve.wait_ge(sem(f"pair{place['o_if'][0] % 2}_free"), place["o_if"][0] // 2 + 1)
            for m in range(MT):
                step(TT(osig[:, m, :], osig[:, m, :], bcs[:, 0, :], ALU.mult))
            prepare("km")
            for t in range(8):
                if t == 4:
                    prepare("vm")
                name = "qm" if t < 4 else "km"
                if t % 4 < 2:
                    dve.wait_ge(sem("conv_raw"), t // 4 + 1)
                else:
                    dve.wait_ge(sem(f"pair{place[name][0] % 2}_free"), place[name][0] // 2 + 1)
                w = lambda j: v1T[:, v1["conv_w"][0] + 8 * j + t:v1["conv_w"][0] + 8 * j + t + 1]
                cb = v1T[:, v1["conv_b"][0] + t:v1["conv_b"][0] + t + 1]
                step(TS(qk[:, t, :], conv_in[:, t, 0:256], w(0), cb, ALU.mult, ALU.add))
                for j in range(1, 4):
                    step(STT(qk[:, t, :], conv_in[:, t, j:j + 256], w(j), qk[:, t, :], ALU.mult, ALU.add))
            dve.nop().then_inc(sem("conv_done"), 1)
            prepare("qa")

            def row(i):
                return rows[0:4, i, :]

            def chunked(i):
                return rows[0:4, i, :].rearrange("p (c n) -> p c n", c=NCH)

            dve.wait_ge(sem("log_ready"), 1)
            dve.wait_ge(sem("pads"), 7)
            step(STT(row(1), row(1), 0.0, row(2), ALU.min, ALU.subtract))
            step(dve.tensor_tensor_scan(row(3), resets[0:4, 0, :], row(1), 0.0, ALU.mult, ALU.add))
            step(TT(row(0), row(0), row(3), ALU.subtract))
            step(dve.tensor_tensor_scan(row(6), resets[0:4, 1, :], row(0), 0.0, ALU.add, ALU.max))
            bl = rows[0:4, 2, 0:4]
            amax, mnew, mprev, dcy = (rows[0:4, 2, 4 * i:4 * i + 4] for i in range(1, 5))
            step(dve.tensor_copy(bl, chunked(3)[:, :, L - 1]))
            step(TT(chunked(4), chunked(0), bcast(bl, L), ALU.add))
            step(dve.tensor_reduce(amax, chunked(4), AX, ALU.max))
            step(dve.tensor_tensor_scan(mnew, bl, amax, 0.0, ALU.add, ALU.max))
            step(dve.memset(mprev[:, 0:1], 0.0))
            step(dve.tensor_copy(mprev[:, 1:4], mnew[:, 0:3]))
            step(TT(dcy, bl, mprev, ALU.add))
            step(TT(dcy, dcy, mnew, ALU.subtract))
            step(TT(chunked(4), chunked(4), bcast(mnew, L), ALU.subtract))
            step(TT(chunked(5), chunked(3), bcast(mprev, L), ALU.add))
            step(TT(row(6), row(6), row(3), ALU.add))
            step(TT(row(6), row(6), row(5), ALU.max))
            step(TT(row(5), row(5), row(6), ALU.subtract))
            step(TT(row(7), row(3), row(6), ALU.subtract))
            dve.nop().then_inc(sem("rows_ready"), 1)
            prepare("kva")
            def rotate(src, nh, m, dst):
                w = nh * 64
                v = src.rearrange("p (h f c) -> p h f c", h=nh, f=2)
                fa = rope_a[:, 0:w].rearrange("p (h f c) -> p h f c", h=nh, f=2)
                fb = rope_b[:, 0:w].rearrange("p (h f c) -> p h f c", h=nh, f=2)
                cos = cossin[:, m, 1, :].unsqueeze(1).to_broadcast([P, nh, 32])
                sin = cossin[:, m, 0, :].unsqueeze(1).to_broadcast([P, nh, 32])
                for f in range(2):
                    step(TT(fa[:, :, f, :], v[:, :, f, :], cos, ALU.mult))
                    step(TT(fb[:, :, f, :], v[:, :, f, :], sin, ALU.mult))
                step(TT(dst(0), fa[:, :, 0, :], fb[:, :, 1, :], ALU.subtract))
                return TT(dst(1), fa[:, :, 1, :], fb[:, :, 0, :], ALU.add)

            dve.wait_ge(sem("cossin_ready"), 1)
            for m, b in enumerate(item("qa")):
                q4 = qr[:, m, :].rearrange("p (i g f c) -> p g i f c", i=4, g=HG, f=2)
                v = b[:, :].rearrange("p (g i f c) -> p g i f c", g=HG, i=4, f=2)
                fa = rope_a[:, 0:512].rearrange("p (g i f c) -> p g i f c", g=HG, i=4, f=2)
                fb = rope_b[:, 0:512].rearrange("p (g i f c) -> p g i f c", g=HG, i=4, f=2)
                cos = cossin[:, m, 1, :].unsqueeze(1).to_broadcast([P, 8, 32])
                sin = cossin[:, m, 0, :].unsqueeze(1).to_broadcast([P, 8, 32])
                v8 = b[:, :].rearrange("p (h f c) -> p h f c", h=8, f=2)
                fa8 = rope_a[:, 0:512].rearrange("p (h f c) -> p h f c", h=8, f=2)
                fb8 = rope_b[:, 0:512].rearrange("p (h f c) -> p h f c", h=8, f=2)
                for f in range(2):
                    step(TT(fa8[:, :, f, :], v8[:, :, f, :], cos, ALU.mult))
                    step(TT(fb8[:, :, f, :], v8[:, :, f, :], sin, ALU.mult))
                for g in range(HG):
                    step(TT(q4[:, g, :, 0, :], fa[:, g, :, 0, :], fb[:, g, :, 1, :], ALU.subtract))
                    step(TT(q4[:, g, :, 1, :], fa[:, g, :, 1, :], fb[:, g, :, 0, :], ALU.add))
                dve.nop().then_inc(sem("qr_ready"), 1)
            dve.nop().then_inc(sem(f"pair{place['qa'][0] % 2}_free"), 1)
            collect_piece(4)
            for m, b in enumerate(item("kva")):
                k4 = kr[:, m, :].rearrange("p (g f c) -> p g f c", g=HG, f=2)
                step(rotate(b[:, 0:128], HG, m, lambda f: k4[:, :, f, :]))
                dve.nop().then_inc(sem("qr_ready"), 1)
                step(dve.tensor_copy(va[:, m, :], b[:, 128:256]))
                dve.nop().then_inc(sem("va_ready"), 1)
            dve.nop().then_inc(sem(f"pair{place['kva'][0] % 2}_free"), 1)

            prepare("g0")
            collect_piece(5)
            dve.wait_ge(sem("silu_done"), 2)
            TS(qk[:, 4:8, :], qk[:, 4:8, :], DM ** -0.5, None, ALU.mult).then_inc(sem("k_scaled"), 1)
            dve.wait_ge(sem("cols_turned"), 1)
            step(dve.tensor_copy(st[:, 64:96], bank[7][:, 0:32]))
            step(dve.tensor_copy(st[:, 96:112], bank[7][:, 32:48]))
            for h2 in range(2):
                dve.wait_ge(sem("bm_spread"), h2 + 1)
                for h in range(2):
                    step(TT(wT[:, 2 * h2 + h, :, :],
                            bank[4 + h2][:, 256 * h:256 * h + 256].rearrange("p (m n) -> p m n", m=MT),
                            C("chunk_t").unsqueeze(1).to_broadcast([P, MT, P]), ALU.add))
            dve.nop().then_inc(sem("arg_ready"), 1)
            prepare("g1")
            collect_piece(6)
            for m in range(MT):
                dve.wait_ge(sem("kc_turned"), m + 1)
                wk = st[:, 64 + 16 * m + 4:64 + 16 * m + 8]
                TT(kw[:, m, :, :], bank[4 + m][:, :].rearrange("p (h n) -> p h n", h=HM), bcast(wk, 128), ALU.mult)\
                    .then_inc(sem("kw_ready"), 1)
            prepare("g2")
            dve.wait_ge(sem("wT_ready"), 8)
            for h2 in range(2):
                dve.wait_ge(sem("ms_done"), h2 + 1)
                TT(sw[:, 2 * h2:2 * h2 + 2, :, :],
                   bank[6 + h2][:, :].rearrange("p (h m n) -> p h m n", h=2, m=MT),
                   wT[:, 2 * h2:2 * h2 + 2, :, :], ALU.mult).then_inc(sem("sw_ready"), 1)
            collect_piece(7)
            gains(1, v1T[:, v1["g_pre_ffn"][0]:v1["g_pre_ffn"][1]])
            for c in range(NCH - 1):
                for h2 in range(2):
                    dve.wait_ge(sem("kv_done"), 2 * c + h2 + 1)
                    for h in range(2 * h2, 2 * h2 + 2):
                        src = bank[4 + 2 * (c % 2) + h2][:, 129 * (h % 2):129 * (h % 2) + 129]
                        if c == 0:
                            ins = dve.tensor_copy(cstate[:, 1, h, :], src)
                        else:
                            ins = STT(cstate[:, c + 1, h, :], cstate[:, c, h, :],
                                      st[:, 96 + 4 * h + c:97 + 4 * h + c], src, ALU.mult, ALU.add)
                        step(ins)
                    dve.nop().then_inc(sem("state_ready"), 1)

            prepare("g3")
            collect_piece(8, bc[:, 0, :])
            sink = bsm[:, 8:16]
            for m, sm in ((0, sm0), (1, sm1)):
                n = 128 if m == 0 else 256
                mask = C("attn")[:, 256 - n:256]
                hb = 4 if m == 0 else 2
                for b in range(HQ // hb):
                    dve.wait_ge(sem("s_done"), (0 if m == 0 else 2) + b + 1)
                    bk = bank[(4, 5)[b] if m == 0 else (6, 7, 4, 5)[b]]
                    TT(sm[:, hb * b:hb * b + hb, :], bk[:, :].rearrange("p (h n) -> p h n", h=hb),
                       mask.unsqueeze(1).to_broadcast([P, hb, n]), ALU.add).then_inc(sem("s_masked"), 1)
                dve.wait_ge(sem("s_masked"), 2 if m == 0 else 6)
                mx = st[:, 16 + 8 * m:24 + 8 * m]
                step(dve.tensor_reduce(mx, sm, AX, ALU.max))
                step(TT(mx, mx, sink, ALU.max))
                step(TT(st[:, 48 + 8 * m:56 + 8 * m], sink, mx, ALU.subtract))
                step(TS(mx, mx, -1.0, None, ALU.mult))
                dve.nop().then_inc(sem("smax_ready"), 1)
            collect_piece(9, bc[:, 0, :])
            prepare("ba0")
            prepare("ba1")
            for m in range(MT):
                dve.wait_ge(sem("exp_ready"), 9 * m + 9)
                step(TT(st[:, 32 + 8 * m:40 + 8 * m], st[:, 32 + 8 * m:40 + 8 * m], st[:, 48 + 8 * m:56 + 8 * m],
                        ALU.add))
                step(dve.reciprocal(st[:, 32 + 8 * m:40 + 8 * m], st[:, 32 + 8 * m:40 + 8 * m]))
            for m in range(MT):
                dve.wait_ge(sem("o_done"), m + 1)
                TT(ya[:, m, :].rearrange("p (h c) -> p h c", h=HQ), bank[6 + m][:, :].rearrange("p (h c) -> p h c", h=HQ),
                   bcast(st[:, 32 + 8 * m:40 + 8 * m], 64), ALU.mult)\
                    .then_inc(sem("ya_ready"), 1)
            for m in range(MT):
                for h2 in range(2):
                    dve.wait_ge(sem("inter_done"), 2 * m + h2 + 1)
                    dve.wait_ge(sem("intra_ready"), 2 * m + h2 + 1)
                    for h in range(2 * h2, 2 * h2 + 2):
                        ins = STT(intra[:, m, h, :], bank[6 + h2][:, 129 * (h % 2):129 * (h % 2) + 129],
                                  st[:, 64 + 16 * m + 8 + h:64 + 16 * m + 9 + h], intra[:, m, h, :],
                                  ALU.mult, ALU.add)
                        if h % 2:
                            ins.then_inc(sem("inter_used"), 1)
                        else:
                            step(ins)
                dve.wait_ge(sem("inter_used"), 2 * m + 2)
                if m == MT - 1:
                    for m_ in range(MT):
                        t = slice(m_ * P, (m_ + 1) * P)
                        dve.wait_ge(sem("yah_ready"), m_ + 1)
                        TT(yal[:, :, t], bank[4 + m_][:, :].rearrange("p (i n) -> p i n", i=4),
                           yah[:, :, t].bitcast(fp), ALU.subtract).then_inc(sem("ya_split"), 1)
                den = st[:, 136 + 4 * m:140 + 4 * m]
                step(TS(den, intra[:, m, :, 128], -1.0, None, ALU.mult))
                step(TT(den, den, intra[:, m, :, 128], ALU.max))
                step(TT(den, den, st[:, 64 + 16 * m + 12:64 + 16 * m + 16], ALU.max))
                step(dve.reciprocal(den, den))
                step(TT(intra[:, m, :, 0:128], intra[:, m, :, 0:128], bcast(den, 128), ALU.mult))
                for h in range(HM):
                    step(dve.bn_stats(st[:, 144 + 6 * h:150 + 6 * h], intra[:, m, h, 0:128]))
                    step(dve.bn_aggr(st[:, 176 + 8 * m + 2 * h:178 + 8 * m + 2 * h], st[:, 144 + 6 * h:150 + 6 * h]))
            mv = st[:, 176:192].rearrange("p (q w) -> p q w", w=2)
            step(TS(st[:, 112:120], mv[:, :, 1], EPS, None, ALU.add))
            step(dve.reciprocal(st[:, 112:120], st[:, 112:120]))
            dve.nop().then_inc(sem("hvar_ready"), 1)
            dve.wait_ge(sem("hstd_ready"), 1)
            for m in range(MT):
                for h in range(HM):
                    step(TS(intra[:, m, h, 0:128], intra[:, m, h, 0:128], mv[:, 4 * m + h, 0:1],
                            st[:, 112 + 4 * m + h:113 + 4 * m + h], ALU.subtract, ALU.mult))
                TT(ym[:, m, :].rearrange("p (h n) -> p h n", h=HM), intra[:, m, :, 0:128],
                   osig[:, m, :].rearrange("p (h n) -> p h n", h=HM), ALU.mult).then_inc(sem("ym_ready"), 1)
            for m in range(MT):
                t = slice(m * P, (m + 1) * P)
                dve.wait_ge(sem("ymh_ready"), m + 1)
                TT(yml[:, :, t], bank[6 + m][:, :].rearrange("p (i n) -> p i n", i=4), ymh[:, :, t].bitcast(fp),
                   ALU.subtract).then_inc(sem("ym_split"), 1)
            dve.wait_ge(sem("gT_ready"), 4)
            for n in range(4):
                dve.wait_ge(sem(f"pair{place[f'g{n}'][0] % 2}_free"), place[f"g{n}"][0] // 2 + 1)
            prepare("bm0")
            for n in range(2):
                if n:
                    prepare("bm1")
                for h, b in enumerate(item(f"ba{n}")):
                    t = 4 * n + 2 * h
                    step(TT(gT[:, t:t + 2, :], b[:, :].rearrange("p (t n) -> p t n", t=2), gT[:, t:t + 2, :],
                            ALU.mult))
                dve.nop().then_inc(sem(f"pair{place[f'ba{n}'][0] % 2}_free"), 1)
            for n in range(2):
                for h, b in enumerate(item(f"bm{n}")):
                    t = 4 * n + 2 * h
                    step(TT(gT[:, 8 + t:10 + t, :], b[:, :].rearrange("p (t n) -> p t n", t=2),
                            gT[:, 8 + t:10 + t, :], ALU.mult))
                dve.nop().then_inc(sem(f"pair{place[f'bm{n}'][0] % 2}_free"), 1)
                t = slice(4 * n, 4 * n + 4)
                step(TT(gT[:, t, :], gT[:, t, :], gT[:, 8 + 4 * n:12 + 4 * n, :], ALU.add))
                dve.nop().then_inc(sem("sum_ready"), 1)
                dve.wait_ge(sem("mgh_ready"), n + 1)
                TT(merged[1][:, t, :], gT[:, t, :], merged[0][:, t, :].bitcast(fp), ALU.subtract)\
                    .then_inc(sem("merged_ready"), 1)

            def post_rms(n, banks, free, squares):
                for m in range(MT):
                    for h in range(2):
                        dve.wait_ge(sem("post_squares"), 4 * n + 2 * m + h + 1)
                        step(TT(xn[:, D * m + 512 * h:D * m + 512 * h + 512], banks[m][h][:, :],
                                gg[:, 512 * h:512 * h + 512], ALU.mult))
                for name in free:
                    dve.nop().then_inc(sem(f"pair{place[name][0] % 2}_free"), 1)
                sq = st[:, 120:124].rearrange("p (m h) -> p m h", m=MT)
                step(TT(st[:, 124:126], sq[:, :, 0], sq[:, :, 1], ALU.add))
                step(TS(st[:, 124:126], st[:, 124:126], 1.0 / D, EPS, ALU.mult, ALU.add))
                step(dve.reciprocal(st[:, 124:126], st[:, 124:126]))
                dve.nop().then_inc(sem("var_ready"), 1)
                dve.wait_ge(sem("std_ready"), squares)
                for m in range(MT):
                    step(STT(xt[:, m, :], xn[:, D * m:D * m + D], st[:, 124 + m:125 + m], xt[:, m, :],
                             ALU.mult, ALU.add))
                    dve.nop().then_inc(sem("x_added"), 1)

            prepare("wo0")
            prepare("wo1")
            w0, w1 = item("wo0"), item("wo1")
            post_rms(0, [(w0[0], w1[0]), (w0[1], w1[1])], ("wo0", "wo1"), 2)
            prepare("ff0")
            rms_rows(1)
            dve.wait_ge(sem("std_ready"), 3)
            for m in range(MT):
                TS(xn[:, m * D:(m + 1) * D], xt[:, m, :], st[:, 4 + m:5 + m], None, ALU.mult)\
                    .then_inc(sem("xn_ready"), 1)
            scale_h(1)

            def feed_forward(letter, down, n, gpost):
                names = ITEMS
                for j in range(FT // 2):
                    name = f"{letter}{j}"
                    at = names.index(name) + 1
                    while names[at][0] == "c":
                        at += 1
                    for x in [names[at]] if names[at][0] != "d" else [f"{down}0", f"{down}1"]:
                        prepare(x)
                    q = n * (FT // 2) + j
                    _, up = item(name)
                    dve.wait_ge(sem("sil_ready"), q + 1)
                    if j >= 2:
                        dve.wait_ge(sem("ffh_ready"), q - 1)
                    step(TT(ffp[:, j % 2, :], up[:, :], sil[:, j % 2, :], ALU.mult))
                    dve.nop().then_inc(sem("ffp_ready"), 1)
                    dve.nop().then_inc(sem(f"pair{place[name][0] % 2}_free"), 1)
                    dve.wait_ge(sem("ffh_ready"), q + 1)
                    t = slice(2 * j, 2 * j + 2)
                    TT(ffl[:, t, :], ffp[:, j % 2, :].rearrange("p (t n) -> p t n", t=2), ffh[:, t, :].bitcast(fp),
                       ALU.subtract).then_inc(sem("ff_ready"), 1)
                    at = names.index(name) + 1
                    while names[at][0] == "c":
                        a = int(names[at][1:])
                        collect_piece(a, gpost if a in GATES else None)
                        at += 1
                for i in range(FT // 2):
                    if i > 1:
                        prepare(f"{down}{i}")
                    if n == 0 and i in (1, 4, 7):
                        a = 15 + i // 3
                        collect_piece(a)
                        if a == 15:
                            gains(2, None)

            feed_forward("ff", "dA", 0, bc[:, 1, :])
            dve.wait_ge(sem("blocks_done"), place["dA10"][2])
            post_rms(1, [(bank[4], bank[5]), (bank[6], bank[7])], (), 4)

            def layer_norm(n, g, b):
                for m in range(MT):
                    for h in range(2):
                        step(dve.bn_stats(st[:, 192 + 6 * h:198 + 6 * h], xt[:, m, 512 * h:512 * h + 512]))
                    step(dve.bn_aggr(st[:, 204 + 2 * m:206 + 2 * m], st[:, 192:204]))
                mv = st[:, 204:208].rearrange("p (m w) -> p m w", w=2)
                step(TS(st[:, 126:128], mv[:, :, 1], LN_EPS, None, ALU.add))
                step(dve.reciprocal(st[:, 126:128], st[:, 126:128]))
                dve.nop().then_inc(sem("var_ready"), 1)
                for m in range(MT):
                    step(STT(xt[:, m, :], xt[:, m, :], mv[:, m, 0:1], g, ALU.subtract, ALU.mult))
                dve.wait_ge(sem("std_ready"), n)
                for m in range(MT):
                    step(STT(xt[:, m, :], xt[:, m, :], st[:, 126 + m:127 + m], b, ALU.mult, ALU.add))
                    yield m

            dve.wait_ge(sem("spreads"), 9 * 16)
            for m in layer_norm(5, bc[:, 2, :], bc[:, 3, :]):
                dve.nop().then_inc(sem("emb_done"), 1)
            scale_h(2)
            prepare("r")
            prepare("k")
            collect_piece(18)
            prepare("v")
            collect_piece(19)
            gains(3, None)
            prepare("lora")

            dve.wait_ge(sem("ws_turned"), 1)
            step(TT(wsT, bank[4][:, :].rearrange("p (g n) -> p g n", g=4),
                    C("ws").unsqueeze(1).to_broadcast([P, 4, P]), ALU.mult))
            dve.nop().then_inc(sem("wsT_ready"), 1)
            def shift(t0, t1, rows_):
                for t in range(t0, t1):
                    now = praw[0:rows_, t, 1:257]
                    d = dtmp[0:rows_, t % 4, :]
                    mu = v2T[0:rows_, v2["mu_shift_2"][0] + t:v2["mu_shift_2"][0] + t + 1]
                    step(TT(d, praw[0:rows_, t, 0:256], now, ALU.subtract))
                    step(STT(pm[0:rows_, t, :], d, mu, now, ALU.mult, ALU.add))

            def shift_item(t0, t1, name, n):
                dve.wait_ge(sem("praw_ready"), n)
                pair_wait(name)
                shift(t0, t1, P)

            shift_item(0, 4, "r", 1)
            prepare("pu")
            shift_item(4, 8, "k", 2)
            shift_item(12, 15, "lora", 4)
            dve.nop().then_inc(sem("lora_mixed"), 1)
            prepare("pv")
            shift_item(8, 12, "v", 3)

            def col(name, j):
                c0 = v2[name][0] + j
                return v2T[:, c0:c0 + 1]

            rT, kT2, vT = pm[:, 0:4, :], pm[:, 4:8, :], pm[:, 8:12, :]
            for j in range(4):
                step(TS(kk[:, j, :], kT2[:, j, :], col("k_k_2", j), None, ALU.mult))
            step(TT(dtmp, kk, kk, ALU.mult))
            dve.nop().then_inc(sem("kk_squared"), 1)
            dve.wait_ge(sem("lwa_ready"), 8)
            step(TS(lw, lw, -math.exp(-0.5), None, ALU.mult))
            dve.wait_ge(sem("pads2"), 4)
            f = lambda t: t.rearrange("p j n -> p (j n)")
            step(dve.tensor_tensor_scan(f(cum), reset, f(lw), 0.0, ALU.mult, ALU.add))
            dve.nop().then_inc(sem("cum_ready"), 1)
            step(TT(lw, cum, lw, ALU.subtract))
            dve.nop().then_inc(sem("cum_ready"), 1)
            dve.wait_ge(sem("kk_len"), 1)
            step(TS(nrm[0:8, :], nrm[0:8, :], 1e-12, None, ALU.max))
            step(dve.reciprocal(nrm[0:8, :], nrm[0:8, :]))
            dve.nop().then_inc(sem("kk_inv"), 1)
            for j in range(4):
                step(TS(dtmp[:, j, :], av[:, j, :], 1.0, col("k_a_2", j), ALU.subtract, ALU.mult))
                step(STT(kT2[:, j, :], dtmp[:, j, :], 1.0, kT2[:, j, :], ALU.add, ALU.mult))
            for h in range(2):
                dve.wait_ge(sem("kk_spread"), h + 1)
                step(TT(kk[:, 2 * h:2 * h + 2, :], kk[:, 2 * h:2 * h + 2, :],
                        bank[4 + h][:, :].rearrange("p (t n) -> p t n", t=2), ALU.mult))
            dve.wait_ge(sem("dec_ready"), 3)
            ch = lambda t: t.rearrange("p j (c n) -> p j c n", c=NCH)
            for j in range(4):
                step(TT(aT_rT[:, j, :, 1, :], ch(rT)[:, j], ch(dec1)[:, j], ALU.mult))
                step(STT(aT_rT[:, j, :, 0, :], ch(kk)[:, j], -1.0, ch(dec2)[:, j], ALU.mult, ALU.mult))
            step(TT(bT, kk, av, ALU.mult))
            step(TT(bT, bT, lw, ALU.mult))
            step(TT(kTt, kT2, lw, ALU.mult))
            step(dve.tensor_copy(st[:, 212:228].rearrange("p (j c) -> p j c", j=4), ch(dec1)[:, :, :, L - 1]))
            for j in range(4):
                step(STT(dtmp[:, j, :], rT[:, j, :], col("r_k_2", j), kT2[:, j, :], ALU.mult, ALU.mult))
            dve.nop().then_inc(sem("tilde_ready"), 1)
            dve.wait_ge(sem("gelu_done"), 2)
            pair_wait("pu")
            pair_wait("pv")
            for m in range(MT):
                step(dve.bn_stats(st[:, 192:198], gv[:, m, :]))
                step(dve.bn_aggr(st[:, 208 + 2 * m:210 + 2 * m], st[:, 192:198]))
            mv = st[:, 208:212].rearrange("p (m w) -> p m w", w=2)
            step(TS(st[:, 132:134], mv[:, :, 1], LN_EPS, None, ALU.add))
            step(dve.reciprocal(st[:, 132:134], st[:, 132:134]))
            dve.nop().then_inc(sem("gvar_ready"), 1)
            for h in range(2):
                dve.wait_ge(sem("bonus_summed"), h + 1)
                step(TT(bonus[:, 2 * h:2 * h + 2, :], vT[:, 2 * h:2 * h + 2, :],
                        bank[6 + h][:, :].rearrange("p (t n) -> p t n", t=2), ALU.mult))
            dve.nop().then_inc(sem("bonus_ready"), 1)
            dve.wait_ge(sem("gstd_ready"), 1)
            for m in range(MT):
                step(TS(gv[:, m, :], gv[:, m, :], mv[:, m, 0:1], st[:, 132 + m:133 + m], ALU.subtract, ALU.mult))
                step(TT(gv[:, m, :], gv[:, m, :], bcs[:, 1, :], ALU.mult))
                step(TT(gv[:, m, :], gv[:, m, :], bcs[:, 2, :], ALU.add))
                dve.nop().then_inc(sem("gv_ready"), 1)
            for m in range(MT):
                dve.wait_ge(sem("sg_done"), m + 1)
                for g in range(4):
                    c0 = v2["b_s_2"][0] + g
                    step(STT(gu[:, m, 128 * g:128 * g + 128], bank[m][:, 128 * g:128 * g + 128],
                             v2T[:, c0:c0 + 1], gu[:, m, 128 * g:128 * g + 128], ALU.add, ALU.mult))
                dve.nop().then_inc(sem("ga_ready"), 1)

            def quad(b, w):
                return b[:, :].rearrange("p (q w n) -> p q w n", w=w, n=L) if w > 1 else \
                    b[:, :].rearrange("p (q n) -> p q n", n=L)

            ar = C("ar").rearrange("p (w n) -> p w n", w=2)

            def masked(dst, src, mask_name, n):
                return TT(dst, src, C(mask_name).unsqueeze(1).to_broadcast([P, n, L]), ALU.mult)

            for n, dst in enumerate((gB, gK)):
                if n:
                    for m in range(MT):
                        t = slice(m * P, (m + 1) * P)
                        dve.wait_ge(sem("gah_ready"), m + 1)
                        step(TT(hl[:, 0:4, t], bank[2 + m][:, :].rearrange("p (i n) -> p i n", i=4),
                                hh[:, 0:4, t].bitcast(fp), ALU.subtract))
                for b in range(4):
                    dve.wait_ge(sem("gram_done"), 4 * n + b + 1)
                    for w in range(2):
                        step(TT(dst[:, 4 * b:4 * b + 4, w, :], quad(bank[4 + b], 2)[:, :, w, :],
                                ar[:, w, :].unsqueeze(1).to_broadcast([P, 4, L]), ALU.mult))
                    dve.nop().then_inc(sem("gram_ready"), 1)
            for h in range(2):
                dve.wait_ge(sem("gram_done"), 9 + h)
                step(masked(inv[5][:, 8 * h:8 * h + 8, :], quad(bank[4 + h], 1), "b4low", 8))
            eye = C("eye2").unsqueeze(1).to_broadcast([P, 16, L])
            S1, S1t, P2, P2t, _, T2, T2t = inv
            step(masked(T2t, gB[:, :, 0, :], "b4", 16))
            step(TT(S1, T2, eye, ALU.add))
            step(TT(S1t, T2t, eye, ALU.add))
            dve.nop().then_inc(sem("inv_ready"), 2)

            def collect(n, dst, add):
                for h in range(2):
                    dve.wait_ge(sem("inv_done"), 2 * n + h + 1)
                    src = quad(bank[4 + 2 * (n % 2) + h], 1)
                    s = slice(8 * h, 8 * h + 8)
                    step(TT(dst[:, s, :], src, add[:, s, :], ALU.add) if add is not None
                         else dve.tensor_copy(dst[:, s, :], src))
                    dve.nop().then_inc(sem("inv_ready"), 1)

            step(masked(P2t, gB[:, :, 0, :], "o4", 16))
            collect(0, P2, None)
            collect(1, T2, S1)
            collect(2, T2t, S1t)
            n = 3
            cur, curt, nxt, nxtt = T2, T2t, S1, S1t
            for lvl, name in enumerate(("o8", "o16", "o32", None)):
                dve.nop().then_inc(sem("off_ready"), 1)
                collect(n, P2, None)
                if name:
                    step(masked(P2t, gB[:, :, 0, :], name, 16))
                collect(n + 1, nxtt, curt)
                n += 2
                if lvl < 3:
                    collect(n, nxt, cur)
                    n += 1
                cur, curt, nxt, nxtt = nxt, nxtt, cur, curt
            prepare("c20")

            dl = st[:, 212:228].rearrange("p (j c) -> p j c", j=4)
            for c in range(NCH - 1):
                dve.wait_ge(sem("m_done"), c + 1)
                dve.wait_ge(sem("yc_done"), c + 1)
                step(TT(ms, bank[6][:, 0:256].rearrange("p (j n) -> p j n", j=4), ms, ALU.add))
                step(TT(ms, ms, bcast(dl[:, :, c], L), ALU.mult))
                dve.nop().then_inc(sem("m_ready"), 1)
                if c == 0:
                    prepare("c21")
            dve.wait_ge(sem("yc_ready"), NCH)
            for h in range(2):
                dve.wait_ge(sem("ymean_done"), h + 1)
                step(STT(f(yT)[:, 512 * h:512 * h + 512], bank[4 + h][:, :], -1.0 / L, f(yT)[:, 512 * h:512 * h + 512],
                         ALU.mult, ALU.add))
            step(TT(dtmp, yT, yT, ALU.mult))
            dve.nop().then_inc(sem("ysq_ready"), 1)
            dve.wait_ge(sem("yvar_done"), 1)
            step(TS(nrm[0:8, :], bank[6][0:8, 0:256], 1.0 / L, GN_EPS, ALU.mult, ALU.add))
            step(dve.reciprocal(nrm[0:8, :], nrm[0:8, :]))
            dve.nop().then_inc(sem("yvar_ready"), 1)
            for h in range(2):
                dve.wait_ge(sem("ystd_spread"), h + 1)
                step(TT(yT[:, 2 * h:2 * h + 2, :], yT[:, 2 * h:2 * h + 2, :],
                        bank[4 + h][:, :].rearrange("p (t n) -> p t n", t=2), ALU.mult))
            for j in range(4):
                step(TS(yT[:, j, :], yT[:, j, :], col("lnx_g_2", j), col("lnx_b_2", j), ALU.mult, ALU.add))
            step(TT(yT, yT, bonus, ALU.add))
            dve.wait_ge(sem("gm_ready"), 2)
            step(TT(yT, yT, gmT, ALU.mult))
            dve.nop().then_inc(sem("yb_ready"), 1)
            dve.wait_ge(sem("ybh_ready"), 1)
            TT(hl[:, 4:8, :], yT, hh[:, 4:8, :].bitcast(fp), ALU.subtract).then_inc(sem("yb_split"), 1)

            def post_ln(banks):
                for m in range(MT):
                    for h in range(2):
                        step(TT(xn[:, 1024 + 512 * h:1536 + 512 * h], banks[m][h][:, :],
                                gg[:, 512 * h:512 * h + 512], ALU.mult))
                    step(STT(xt[:, m, :], xt[:, m, :], ALPHA, xn[:, 1024:2048], ALU.mult, ALU.add))

            collect_piece(20)
            collect_piece(21)
            prepare("wo2")
            prepare("wo3")
            w0, w1 = item("wo2"), item("wo3")
            post_ln([(w0[0], w1[0]), (w0[1], w1[1])])
            for name in ("wo2", "wo3"):
                dve.nop().then_inc(sem(f"pair{place[name][0] % 2}_free"), 1)
            prepare("gf0")
            dve.wait_ge(sem("spreads"), 13 * 16)
            for m in layer_norm(6, bc[:, 0, :], bc[:, 1, :]):
                dve.nop().then_inc(sem("ln1_done"), 1)
            scale_h(3)
            feed_forward("gf", "dB", 1, None)
            dve.wait_ge(sem("blocks_done"), place["dB10"][2])
            post_ln([(bank[4], bank[5]), (bank[6], bank[7])])
            for m in layer_norm(7, bc[:, 2, :], bc[:, 3, :]):
                dve.nop().then_inc(sem("y_out"), 1)

        @block.tensor
        def _(pe):
            mm = nc.tensor.matmul
            tr = nc.tensor.transpose

            def start_item(name):
                pair, _, _ = place[name]
                if pair >= 2:
                    pe.wait_ge(sem(f"pair{pair % 2}_free"), pair // 2)
                return bank[2 * (pair % 2)], bank[2 * (pair % 2) + 1]

            def weights(g):
                b = of_split[g]
                _, i, nk, width, _, _, _ = order[b]
                who, count = ready[b]
                pe.wait_ge(sem(f"{who}_blocks"), count)
                return i, nk, cut(whi, g % HL, nk, width), cut(wlo, g % HL, nk, width)

            def piece(a):
                b0, used = piece_place(a)
                if used:
                    pe.wait_ge(sem("piece_used"), used)
                who, count = ready[at_block[f"c{a}"][-1]]
                pe.wait_ge(sem(f"{who}_blocks"), count)
                if a in GATES:
                    last = mm(b0[:, :], C("ones"), acc[:, a % 2, :], start=True, stop=True)
                else:
                    for t in range(4):
                        last = mm(b0[:, t:t + 1], acc[:, a % 2, t * P:(t + 1) * P], C("ones")[:, 0:1],
                                  start=True, stop=True)
                last.then_inc(sem("piece_done"), 1)

            def tokens_out(name, n, src, extra=None, half_ready=None):
                banks = start_item(name)
                xh, xl = src
                _, g0, g1 = place[name]
                for g in range(g0, g1):
                    i, nk, wh, wl = weights(g)
                    if half_ready is not None:
                        pe.wait_ge(sem("h_ready"), half_ready + nk * i // 4 + 1)
                    for dsts, c0, cn in ([([bank[4][:, 0:8], bank[5][:, 0:8]], extra, 8)] if extra else []) + \
                            [([banks[0][:, 0:n], banks[1][:, 0:n]], 0, n)]:
                        for m in range(MT):
                            t = slice(m * P, (m + 1) * P)
                            for k in range(nk):
                                kk_ = nk * i + k
                                first, end = g == g0 and k == 0, g == g1 - 1 and k == nk - 1
                                c = slice(c0, c0 + cn)
                                mm(dsts[m], xh[:, kk_, t], wh[:, k, c], start=first, stop=False)
                                mm(dsts[m], xh[:, kk_, t], wl[:, k, c], start=False, stop=False)
                                last = mm(dsts[m], xl[:, kk_, t], wh[:, k, c], start=False, stop=end)
                    last.then_inc(sem("blocks_done"), 1)

            def features_out(name, cols, src, half_ready=None):
                banks = start_item(name)
                xh, xl = src
                _, g0, g1 = place[name]
                for g in range(g0, g1):
                    i, nk, wh, wl = weights(g)
                    if half_ready is not None:
                        pe.wait_ge(sem("h_ready"), half_ready + nk * i // 4 + 1)
                    for t, c0 in enumerate(cols):
                        o = banks[t // 2][:, 256 * (t % 2):256 * (t % 2) + 256]
                        in_bank = [x for x in range(len(cols)) if x // 2 == t // 2]
                        for k in range(nk):
                            kk_ = nk * i + k
                            first = g == g0 and k == 0 and t == in_bank[0]
                            end = g == g1 - 1 and k == nk - 1 and t == in_bank[-1]
                            c = slice(c0, c0 + P)
                            mm(o, wh[:, k, c], xh[:, kk_, :], start=first, stop=False)
                            mm(o, wh[:, k, c], xl[:, kk_, :], start=False, stop=False)
                            last = mm(o, wl[:, k, c], xh[:, kk_, :], start=False, stop=end)
                    last.then_inc(sem("blocks_done"), 1)

            def turn_h(src, name, before):
                for m in range(MT):
                    pe.wait_ge(sem(name), before + m + 1)
                    for k in range(8):
                        last = tr(bank[4 + k // 2][:, 256 * (k % 2) + P * m:256 * (k % 2) + P * m + P],
                                  src(m)[:, k * P:(k + 1) * P], ident)
                        if k % 2 and m == MT - 1:
                            last.then_inc(sem("hx_turned"), 1)

            four = [0, P, 2 * P, 3 * P]
            modulated = (hh, hl)
            pe.wait_ge(sem("const_in"), 16)
            pe.wait_ge(sem("vectors_in"), 16 * (len(ROWS1) + len(ROWS2) + 1))
            tr(bank[4][:, 0:n1], vraw[0:n1, 0, :], ident[0:n1, 0:n1]).then_inc(sem("vec_turned"), 1)
            tr(bank[5][:, 0:n2], vraw[0:n2, 1, :], ident[0:n2, 0:n2]).then_inc(sem("vec_turned"), 1)
            turn_h(lambda m: xn[:, m * D:(m + 1) * D], "xn_ready", 0)
            for a in range(4):
                piece(a)
            tokens_out("o_if", 512, modulated, extra=512, half_ready=0)
            features_out("qm", four, modulated)
            features_out("km", four, modulated)
            pe.wait_ge(sem("if_ready"), 2)
            for w in range(2):
                for m in range(MT):
                    last = tr(bank[7][0:4, 256 * w + P * m:256 * w + P * m + P],
                              st[:, 240 + 8 * m + 4 * w:244 + 8 * m + 4 * w], ident)
            last.then_inc(sem("if_turned"), 1)
            tokens_out("vm", 512, modulated)
            tokens_out("qa", 512, modulated)
            piece(4)
            tokens_out("kva", 256, modulated)
            piece(5)
            pe.wait_ge(sem("rows_exp"), 4)
            for m in range(MT):
                for q, r in enumerate((0, 4, 5, 6)):
                    tr(bank[7][:, 16 * m + 4 * q:16 * m + 4 * q + 4], rows[0:4, r, m * P:(m + 1) * P], ident[0:4, 0:4])
            for h in range(HM):
                last = mm(bank[7][:, 32 + 4 * h:36 + 4 * h], ident[0:4, h:h + 1].to_broadcast([4, P]), rows[0:4, 2, 16:20],
                          start=True, stop=True)
            last.then_inc(sem("cols_turned"), 1)
            for h2 in range(2):
                for h in range(2):
                    last = mm(bank[4 + h2][:, 256 * h:256 * h + 256], ident[0:4, 2 * h2 + h:2 * h2 + h + 1].to_broadcast([4, P]),
                              rows[0:4, 7, :], start=True, stop=True)
                last.then_inc(sem("bm_spread"), 1)
            features_out("g0", four, modulated)
            piece(6)
            pe.wait_ge(sem("k_scaled"), 1)
            pe.wait_ge(sem("arg_ready"), 1)
            for m in range(MT):
                for h in range(HM):
                    last = tr(bank[4 + m][:, h * P:(h + 1) * P], qk[:, 4 + h, m * P:(m + 1) * P], ident)
                last.then_inc(sem("kc_turned"), 1)
            features_out("g1", four, modulated)
            pe.wait_ge(sem("piece_used"), 7)
            for h2 in range(2):
                for h in range(2):
                    for m in range(MT):
                        t = slice(m * P, (m + 1) * P)
                        last = mm(bank[6 + h2][:, 256 * h + P * m:256 * h + P * m + P], qk[:, 4 + 2 * h2 + h, t],
                                  qk[:, 2 * h2 + h, t], start=True, stop=True)
                last.then_inc(sem("ms_done"), 1)
            features_out("g2", four, modulated)
            pe.wait_ge(sem("kw_ready"), 2)
            pe.wait_ge(sem(f"pair{place['vm'][0] % 2}_free"), place["vm"][0] // 2 + 1)
            pe.wait_ge(sem("v_ready"), 1)
            pe.wait_ge(sem("pads"), 3)
            pe.wait_ge(sem("sw_ready"), 2)
            piece(7)
            for c in range(NCH - 1):
                if c == 1:
                    pe.wait_ge(sem("piece_used"), 8)
                rows_ = slice(L * (c % 2), L * (c % 2) + L)
                for h2 in range(2):
                    if c == 2:
                        pe.wait_ge(sem("state_ready"), h2 + 1)
                    for h in range(2 * h2, 2 * h2 + 2):
                        last = mm(bank[4 + 2 * (c % 2) + h2][:, 129 * (h % 2):129 * (h % 2) + 129],
                                  kw[rows_, c // 2, h, :], vaug[rows_, c // 2, h, :], start=True, stop=True)
                    last.then_inc(sem("kv_done"), 1)
            pe.wait_ge(sem("state_ready"), 6)
            piece(8)
            for m in range(MT):
                pe.wait_ge(sem("qr_ready"), m + 1)
                for i in range(4):
                    last = tr(bank[4 + m][:, i * P:(i + 1) * P], qr[:, m, i * P:(i + 1) * P], ident)
                last.then_inc(sem("qr_turned"), 1)
            pe.wait_ge(sem("qr_ready"), 4)
            pe.wait_ge(sem("piece_used"), 9)
            for m in range(MT):
                last = tr(bank[6][:, m * P:(m + 1) * P], kr[:, m, :], ident)
            last.then_inc(sem("qr_turned"), 1)
            pe.wait_ge(sem("qT_ready"), 3)

            def scores(m, h, b, at, n):
                g, i = h // 4, h % 4
                half = slice(64 * g, 64 * g + 64)
                return mm(b[:, at:at + n], qT[half, i, m * P:(m + 1) * P], kT[half, S - n if m else 0:S if m else n],
                          start=True, stop=True)

            for b in range(2):
                for h in range(4):
                    last = scores(0, 4 * b + h, bank[4 + b], 128 * h, 128)
                last.then_inc(sem("s_done"), 1)
            for b in range(4):
                if b >= 2:
                    pe.wait_ge(sem("s_masked"), b - 1)
                for h in range(2):
                    last = scores(1, 2 * b + h, bank[(6, 7, 4, 5)[b]], 256 * h, 256)
                last.then_inc(sem("s_done"), 1)
            features_out("g3", four, modulated)
            pe.wait_ge(sem("s_masked"), 6)
            piece(9)
            pe.wait_ge(sem("piece_used"), 10)
            for n in range(6):
                m = 0 if n < 2 else 1
                pe.wait_ge(sem("s_masked"), 6)
                pe.wait_ge(sem("exp_ready"), 9 * m + 9)
                if n >= 4:
                    pe.wait_ge(sem("pT_ready"), n - 3)
                for q in range(4):
                    if m == 0:
                        src = sm0[:, 4 * n + q, :]
                    else:
                        idx = 4 * (n - 2) + q
                        src = sm1[:, idx // 2, P * (idx % 2):P * (idx % 2) + P]
                    last = tr(bank[4 + n % 4][:, q * P:(q + 1) * P], src, ident)
                last.then_inc(sem("p_turned"), 1)
            pe.wait_ge(sem("pT_ready"), 6)
            pe.wait_ge(sem("va_ready"), 2)
            for h in range(HQ):
                g = h // 4
                last = mm(bank[6][:, 64 * h:64 * h + 64], pT[:, h, :], va[:, 0, 64 * g:64 * g + 64],
                          start=True, stop=True)
            last.then_inc(sem("o_done"), 1)
            for h in range(HQ):
                g = h // 4
                for kb in range(2):
                    last = mm(bank[7][:, 64 * h:64 * h + 64], pT[:, 8 + 2 * h + kb, :], va[:, kb, 64 * g:64 * g + 64],
                              start=(kb == 0), stop=(kb == 1))
            last.then_inc(sem("o_done"), 1)
            for m in range(MT):
                for h2 in range(2):
                    if m:
                        pe.wait_ge(sem("intra_ready"), h2 + 1)
                    for h in range(2 * h2, 2 * h2 + 2):
                        last = mm(bank[4 + h2][:, 129 * (h % 2):129 * (h % 2) + 129], sw[:, h, m, :],
                                  vaug[:, m, h, :], start=True, stop=True)
                    last.then_inc(sem("intra_done"), 1)
                if m == 0:
                    pe.wait_ge(sem("ya_ready"), 2)
                for h2 in range(2):
                    if m:
                        pe.wait_ge(sem("inter_used"), h2 + 1)
                    for h in range(2 * h2, 2 * h2 + 2):
                        for half in range(2):
                            c = 2 * m + half
                            last = mm(bank[6 + h2][L * half:L * half + L, 129 * (h % 2):129 * (h % 2) + 129],
                                      qk[:, h, c * L:(c + 1) * L], cstate[:, c, h, :], start=True, stop=True)
                    last.then_inc(sem("inter_done"), 1)
            pe.wait_ge(sem("intra_ready"), 4)
            for m in range(MT):
                for i in range(4):
                    last = tr(bank[4 + m][:, i * P:(i + 1) * P], ya[:, m, i * P:(i + 1) * P], ident)
                last.then_inc(sem("ya_turned"), 1)
            pe.wait_ge(sem("ya_split"), 2)
            features_out("ba0", four, (yah, yal))
            features_out("ba1", four, (yah, yal))
            pe.wait_ge(sem("inter_used"), 4)
            for m in range(MT):
                pe.wait_ge(sem("ym_ready"), m + 1)
                for i in range(4):
                    last = tr(bank[6 + m][:, i * P:(i + 1) * P], ym[:, m, i * P:(i + 1) * P], ident)
                last.then_inc(sem("ym_turned"), 1)
            pe.wait_ge(sem("ym_split"), 2)
            features_out("bm0", four, (ymh, yml))
            features_out("bm1", four, (ymh, yml))

            pe.wait_ge(sem("merged_ready"), 2)
            tokens_out("wo0", 512, merged)
            tokens_out("wo1", 512, merged)
            turn_h(lambda m: xn[:, m * D:(m + 1) * D], "xn_ready", 2)

            def feed_forward(letter, down, n):
                names = ITEMS
                for j in range(FT // 2):
                    name = f"{letter}{j}"
                    features_out(name, four, modulated, half_ready=2 + 4 * n if j == 0 else None)
                    if names[names.index(name) + 1][0] == "c":
                        piece(int(names[names.index(name) + 1][1:]))
                pe.wait_ge(sem("piece_used"), 24 if n else 15)
                for t in range(FT):
                    _, nk, wh, wl = weights(place[f"{down}0"][1] + t)
                    for k in range(nk):
                        pe.wait_ge(sem("ff_ready"), n * (FT // 2) + t // 2 + 1)
                        for m in range(MT):
                            x = slice(m * P, (m + 1) * P)
                            for c in range(2):
                                o, cs = bank[4 + 2 * m + c][:, :], slice(512 * c, 512 * c + 512)
                                mm(o, ffh[:, t, x], wh[:, k, cs], start=(t == 0), stop=False)
                                mm(o, ffh[:, t, x], wl[:, k, cs], start=False, stop=False)
                                last = mm(o, ffl[:, t, x], wh[:, k, cs], start=False, stop=(t == FT - 1))
                    last.then_inc(sem("blocks_done"), 1)
                    if n == 0 and t in (3, 9, 15):
                        piece(15 + t // 6)

            feed_forward("ff", "dA", 0)
            turn_h(lambda m: xt[:, m, :], "emb_done", 0)
            features_out("r", four, modulated, half_ready=4)
            piece(18)
            features_out("k", four, modulated)
            piece(19)
            pe.wait_ge(sem("ws_in"), 16)
            for g in range(4):
                last = tr(bank[4][:, g * P:(g + 1) * P], wsr[:, g, :], ident)
            last.then_inc(sem("ws_turned"), 1)
            features_out("v", four, modulated)
            features_out("lora", [0, P, 288 - P], modulated)
            tokens_out("pu", 512, modulated)
            pe.wait_ge(sem("wsT_ready"), 1)
            pe.wait_ge(sem("piece_used"), 20)
            pe.wait_ge(sem("lora_in"), 64)
            pe.wait_ge(sem("lora_act"), 3)
            for n, half in enumerate((slice(0, 64), slice(64, 128))):
                for j in range(4):
                    last = mm(bank[4 + 2 * n + j // 2][:, 256 * (j % 2):256 * (j % 2) + 256],
                              lup[half, j * P:(j + 1) * P], pm[half, 12, :], start=True, stop=True)
                    if j % 2:
                        last.then_inc(sem("lora_done"), 1)
            tokens_out("pv", 512, modulated)
            for j in range(4):
                if j % 2 == 0:
                    pe.wait_ge(sem("lwa_ready"), j + 2)
                o = bank[4 + j // 2][:, 256 * (j % 2):256 * (j % 2) + 256]
                mm(o, gu0[:, j * P:(j + 1) * P], pm[:, 13, :], start=True, stop=False)
                last = mm(o, gu1[96:128, j * P:(j + 1) * P], pm[96:128, 14, :], start=False, stop=True)
                if j % 2:
                    last.then_inc(sem("lora_done"), 1)
            heads = C("heads").rearrange("p (j n) -> p j n", j=4)

            def head_sums(src, dst, s):
                for j in range(4):
                    last = mm(dst, heads[:, j, :], src[:, j, :], start=(j == 0), stop=(j == 3))
                last.then_inc(s, 1)

            def head_spread(s):
                for j in range(4):
                    for g in range(2):
                        last = mm(bank[4 + j // 2][L * g:L * g + L, 256 * (j % 2):256 * (j % 2) + 256],
                                  ident[0:8, 2 * j + g:2 * j + g + 1].to_broadcast([8, L]), nrm[0:8, :],
                                  start=True, stop=True)
                    if j % 2:
                        last.then_inc(s, 1)

            pe.wait_ge(sem("kk_squared"), 1)
            pe.wait_ge(sem("lwa_ready"), 8)
            head_sums(dtmp, bank[6][0:8, 0:256], sem("kk_summed"))
            pe.wait_ge(sem("kk_inv"), 1)
            pe.wait_ge(sem("gm_ready"), 2)
            head_spread(sem("kk_spread"))
            pe.wait_ge(sem("tilde_ready"), 1)
            for j in range(4):
                last = mm(bank[6 + j // 2][:, 256 * (j % 2):256 * (j % 2) + 256], C("pairs"), dtmp[:, j, :],
                          start=True, stop=True)
                if j % 2:
                    last.then_inc(sem("bonus_summed"), 1)
            eye2 = C("eye2")
            half = (slice(0, 64), slice(64, 128))

            def each(q0, q1):
                for q in range(q0, q1):
                    for g in range(2):
                        yield q, q // 4, q % 4, half[g]

            pe.wait_ge(sem("bonus_ready"), 1)
            for n, src in enumerate((bT, kTt, pm[:, 8:12, :])):
                for h in range(2):
                    i = 2 * n + h
                    if i >= 4:
                        pe.wait_ge(sem("tok_ready"), i - 3)
                    for q, c, j, r in each(8 * h, 8 * h + 8):
                        last = mm(bank[4 + i % 4][r, L * (q % 8):L * (q % 8) + L], src[r, j, c * L:(c + 1) * L],
                                  eye2[r, :], start=True, stop=True)
                    last.then_inc(sem("tok_turned"), 1)
            for m in range(MT):
                pe.wait_ge(sem("gv_ready"), m + 1)
                for g in range(4):
                    last = mm(bank[m][:, g * P:(g + 1) * P], wsT[:, g, :], gv[:, m, g * P:(g + 1) * P],
                              start=True, stop=True)
                last.then_inc(sem("sg_done"), 1)
            pe.wait_ge(sem("tok_ready"), 6)
            for n, src in enumerate((bT, kTt)):
                if n:
                    for m in range(MT):
                        pe.wait_ge(sem("ga_ready"), m + 1)
                        for i in range(4):
                            last = tr(bank[2 + m][:, i * P:(i + 1) * P], gu[:, m, i * P:(i + 1) * P], ident)
                        last.then_inc(sem("ga_turned"), 1)
                    pe.wait_ge(sem("ga_ready"), 2)
                for b in range(4):
                    if n:
                        pe.wait_ge(sem("gram_ready"), b + 1)
                    for q, c, j, r in each(4 * b, 4 * b + 4):
                        last = mm(bank[4 + b][r, 2 * L * (q % 4):2 * L * (q % 4) + 2 * L],
                                  src[r, j, c * L:(c + 1) * L],
                                  aT_rT[r, j, c, :, :].rearrange("p w n -> p (w n)"), start=True, stop=True)
                    last.then_inc(sem("gram_done"), 1)
            for h in range(2):
                pe.wait_ge(sem("gram_ready"), 5 + h)
                for q, c, j, r in each(8 * h, 8 * h + 8):
                    last = mm(bank[4 + h][r, L * (q % 8):L * (q % 8) + L], aT_rT[r, j, c, 0, :],
                              bT[r, j, c * L:(c + 1) * L], start=True, stop=True)
                last.then_inc(sem("gram_done"), 1)
            S1, S1t, P2, P2t, _, T2, T2t = inv

            def product(n, lhsT, rhs, ready):
                for h in range(2):
                    pe.wait_ge(sem("inv_ready"), ready + h)
                    for q, c, j, r in each(8 * h, 8 * h + 8):
                        last = mm(bank[4 + 2 * (n % 2) + h][r, L * (q % 8):L * (q % 8) + L], lhsT[r, q, :],
                                  rhs[r, q, :], start=True, stop=True)
                    last.then_inc(sem("inv_done"), 1)

            done = lambda n: 2 + 2 * n + 1
            pe.wait_ge(sem("gram_ready"), 8)
            product(0, T2t, T2, 1)
            product(1, S1t, P2, done(0))
            product(2, P2, S1t, done(0))
            n = 3
            cur, curt, nxt, nxtt = T2, T2t, S1, S1t
            for lvl in range(4):
                pe.wait_ge(sem("off_ready"), lvl + 1)
                product(n, P2t, cur, done(n - 1 if lvl else n - 2))
                product(n + 1, P2, curt, done(n))
                n += 2
                if lvl < 3:
                    product(n, curt, P2, done(n - 1))
                    n += 1
                cur, curt, nxt, nxtt = nxt, nxtt, cur, curt
            solve = curt
            pe.wait_ge(sem("inv_ready"), done(n - 1) + 1)
            pe.wait_ge(sem("pads2"), 4)
            for c in range(NCH):
                if c:
                    pe.wait_ge(sem("m_ready"), c)
                for q, _, j, r in each(4 * c, 4 * c + 4):
                    mm(bank[4][r, L * j:L * j + L], aT_rT[r, j, c, 0, :], ms[r, j, :], start=True, stop=False)
                    last = mm(bank[4][r, L * j:L * j + L], gK[r, q, 0, :], vtok[r, q, :], start=False, stop=True)
                last.then_inc(sem("x_done"), 1)
                pe.wait_ge(sem("x_ready"), c + 1)
                for q, _, j, r in each(4 * c, 4 * c + 4):
                    last = mm(bank[5][r, L * j:L * j + L], solve[r, q, :], xs[r, j, :], start=True, stop=True)
                last.then_inc(sem("u_done"), 1)
                pe.wait_ge(sem("u_ready"), c + 1)
                if c < NCH - 1:
                    for q, _, j, r in each(4 * c, 4 * c + 4):
                        mm(bank[6][r, L * j:L * j + L], btok[r, q, :], us[r, j, :], start=True, stop=False)
                        last = mm(bank[6][r, L * j:L * j + L], ktok[r, q, :], vtok[r, q, :], start=False, stop=True)
                    last.then_inc(sem("m_done"), 1)
                if c:
                    pe.wait_ge(sem("yc_ready"), c)
                for q, _, j, r in each(4 * c, 4 * c + 4):
                    o = bank[7][r, L * j:L * j + L]
                    mm(o, ms[r, j, :], aT_rT[r, j, c, 1, :], start=True, stop=False)
                    mm(o, us[r, j, :], gB[r, q, 1, :], start=False, stop=False)
                    last = mm(o, vtok[r, q, :], gK[r, q, 1, :], start=False, stop=True)
                last.then_inc(sem("yc_done"), 1)
            pe.wait_ge(sem("yc_ready"), NCH)
            for j in range(4):
                last = mm(bank[4 + j // 2][:, 256 * (j % 2):256 * (j % 2) + 256], C("pairs"), yT[:, j, :],
                          start=True, stop=True)
                if j % 2:
                    last.then_inc(sem("ymean_done"), 1)
            pe.wait_ge(sem("ysq_ready"), 1)
            head_sums(dtmp, bank[6][0:8, 0:256], sem("yvar_done"))
            pe.wait_ge(sem("ystd_ready"), 1)
            head_spread(sem("ystd_spread"))
            piece(20)
            piece(21)
            pe.wait_ge(sem("yb_split"), 1)
            tokens_out("wo2", 512, cat)
            tokens_out("wo3", 512, cat)
            turn_h(lambda m: xt[:, m, :], "ln1_done", 0)
            feed_forward("gf", "dB", 1)


_INS = ["x", "c", "positions", "w_ada", "b_ada", "g_pre_mix", "g_post_mix", "w_in", "b_if", "conv_w", "conv_b",
        "attn_sinks", "mlstm_norm_w", "w_branch_attn", "w_branch_mlstm", "w_out", "g_pre_ffn", "g_post_ffn",
        "w_ffn_gate", "w_ffn_up", "w_ffn_down", "c_2", "emb_ln_g_2", "emb_ln_b_2", "w_ada_2", "b_ada_2", "w_in_2",
        "mu_shift_2", "sg_ln_g_2", "sg_ln_b_2", "w_s_2", "b_s_2", "w0_2", "w_up_2", "a0_2", "a_up_2", "g_up_2",
        "k_k_2", "k_a_2", "r_k_2", "lnx_g_2", "lnx_b_2", "w_out_2", "ln1_g_2", "ln1_b_2", "w_ffn_in_2",
        "w_ffn_out_2", "ln2_g_2", "ln2_b_2"]


def kernel(**inputs):
    import numpy as _np
    import concourse.bacc as _bacc
    from concourse import mybir as _mybir
    from concourse.bass_utils import run_bass_kernel_spmd as _run

    nc = _bacc.Bacc("TRN2", target_bir_lowering=False, num_devices=1)
    arrays, args = {}, {}
    const = constants()
    for name in _INS + ["const"]:
        a = const if name == "const" else _np.ascontiguousarray(inputs[name])
        arrays[f"in_{name}"] = a
        args[name] = nc.dram_tensor(f"in_{name}", a.shape, _mybir.dt.from_np(a.dtype), kind="ExternalInput").ap()
    out = nc.dram_tensor("out_dram", (1, S, D), _mybir.dt.float32, kind="ExternalOutput").ap()
    build(nc, args, out)
    r = _run(nc, [arrays], core_ids=[0])
    return r.results[0]["out_dram"]
```
